# Optimizing a Trainium2 kernel written in Bass

```python
import jax, jax.numpy as jnp
from jax import lax
import numpy as np
import math

D_MODEL = 1024
BATCH = 1
SEQ = 512
DEPTH = 2

PLE_DIM = 256
MLA_HEADS = 8
MLA_NOPE = 64
MLA_ROPE = 32
MLA_V = 64
MLA_QK = MLA_NOPE + MLA_ROPE
MLA_Q_LORA = 384
MLA_KV_LORA = 128
ROPE_THETA = 10000.0
Q_BLOCK = 128
FNET_GROUPS = 4
GQA_Q_HEADS = 8
GQA_KV_HEADS = 2
GQA_GROUP = GQA_Q_HEADS // GQA_KV_HEADS
GQA_HEAD_DIM = 64
WINDOW = 128
WIN_BLOCK = 128
FFN_DIM = -(-8 * D_MODEL // (3 * 256)) * 256
RMS_EPS = 1e-6

IN_SPLITS = (MLA_Q_LORA, MLA_KV_LORA, MLA_ROPE,
             GQA_Q_HEADS * GQA_HEAD_DIM, GQA_KV_HEADS * GQA_HEAD_DIM, GQA_KV_HEADS * GQA_HEAD_DIM,
             D_MODEL, D_MODEL, D_MODEL)
IN_COLS = sum(IN_SPLITS)


def rms_norm(x, gain):
    xf = x.astype(jnp.float32)
    y = xf * lax.rsqrt(jnp.mean(xf * xf, axis=-1, keepdims=True) + RMS_EPS)
    return (y * gain.astype(jnp.float32)).astype(x.dtype)

def apply_rope(t, positions):
    half = t.shape[-1] // 2
    inv_freq = ROPE_THETA ** (-jnp.arange(half, dtype=jnp.float32) / half)
    ang = positions.astype(jnp.float32)[..., None] * inv_freq
    ang = ang.reshape(ang.shape[:2] + (1,) * (t.ndim - 3) + (half,))
    cos, sin = jnp.cos(ang), jnp.sin(ang)
    tf = t.astype(jnp.float32)
    t1, t2 = tf[..., :half], tf[..., half:]
    return jnp.concatenate([t1 * cos - t2 * sin, t1 * sin + t2 * cos], axis=-1).astype(t.dtype)

def alibi_slopes(n_heads):
    return 2.0 ** (-8.0 * (np.arange(n_heads, dtype=np.float32) + 1.0) / n_heads)

def mla_attention(c_q, c_kv, k_rope, positions, q_norm, w_uq, kv_norm, w_ukv):
    B, S, _ = c_q.shape
    q = (rms_norm(c_q, q_norm) @ w_uq).reshape(B, S, MLA_HEADS, MLA_QK)
    q_nope = q[..., :MLA_NOPE]
    q_rope = apply_rope(q[..., MLA_NOPE:], positions)
    kv = (rms_norm(c_kv, kv_norm) @ w_ukv).reshape(B, S, MLA_HEADS, MLA_NOPE + MLA_V)
    k_nope, v = kv[..., :MLA_NOPE], kv[..., MLA_NOPE:]
    k_r = apply_rope(k_rope, positions)
    scale = MLA_QK ** -0.5
    nb = S // Q_BLOCK
    qn_b = q_nope.reshape(B, nb, Q_BLOCK, MLA_HEADS, MLA_NOPE).transpose(1, 0, 2, 3, 4)
    qr_b = q_rope.reshape(B, nb, Q_BLOCK, MLA_HEADS, MLA_ROPE).transpose(1, 0, 2, 3, 4)

    def attend(blk):
        qn, qr = blk
        s = (jnp.einsum('bqhd,bkhd->bhqk', qn, k_nope)
             + jnp.einsum('bqhr,bkr->bhqk', qr, k_r)).astype(jnp.float32) * scale
        probs = jax.nn.softmax(s, axis=-1).astype(v.dtype)
        return jnp.einsum('bhqk,bkhd->bqhd', probs, v)

    o = lax.map(attend, (qn_b, qr_b))
    return o.transpose(1, 0, 2, 3, 4).reshape(B, S, MLA_HEADS * MLA_V)

def fourier_mix(h):
    B, S, D = h.shape
    hg = h.astype(jnp.float32).reshape(B, S, FNET_GROUPS, D // FNET_GROUPS)
    f = jnp.fft.fftn(hg, axes=(1, 3), norm='ortho').real
    return f.reshape(B, S, D).astype(h.dtype)

def windowed_gqa(q, k, v, positions, sink):
    B, S, _ = q.shape
    nb = S // WIN_BLOCK
    q = q.reshape(B, nb, WIN_BLOCK, GQA_KV_HEADS, GQA_GROUP, GQA_HEAD_DIM)
    k = k.reshape(B, S, GQA_KV_HEADS, GQA_HEAD_DIM)
    v = v.reshape(B, S, GQA_KV_HEADS, GQA_HEAD_DIM)

    def windows(t):
        pad = ((0, 0), (WIN_BLOCK, WIN_BLOCK)) + ((0, 0),) * (t.ndim - 2)
        tb = jnp.pad(t, pad).reshape((B, nb + 2, WIN_BLOCK) + t.shape[2:])
        return jnp.concatenate([tb[:, :-2], tb[:, 1:-1], tb[:, 2:]], axis=2)

    kw, vw, pw = windows(k), windows(v), windows(positions)
    scale = GQA_HEAD_DIM ** -0.5
    s = jnp.einsum('bnqhgd,bnkhd->bnhgqk', q, kw).astype(jnp.float32) * scale
    pq = positions.reshape(B, nb, WIN_BLOCK)
    dist = jnp.abs(pq[..., :, None] - pw[..., None, :]).astype(jnp.float32)
    slopes = jnp.asarray(alibi_slopes(GQA_Q_HEADS)).reshape(GQA_KV_HEADS, GQA_GROUP)
    s = s - slopes[None, None, :, :, None, None] * dist[:, :, None, None]
    qi = jnp.arange(WIN_BLOCK)
    kj = jnp.arange(3 * WIN_BLOCK)
    band = jnp.abs(kj[None, :] - WIN_BLOCK - qi[:, None]) <= WINDOW
    key_idx = jnp.arange(nb)[:, None] * WIN_BLOCK - WIN_BLOCK + kj[None, :]
    valid = (key_idx >= 0) & (key_idx < S)
    mask = band[None] & valid[:, None, :]
    s = jnp.where(mask[None, :, None, None], s, -jnp.inf)
    sink_l = sink.astype(jnp.float32).reshape(GQA_KV_HEADS, GQA_GROUP)[None, None, :, :, None, None]
    m = jnp.maximum(jnp.max(s, axis=-1, keepdims=True), sink_l)
    e = jnp.exp(s - m)
    probs = (e / (jnp.sum(e, axis=-1, keepdims=True) + jnp.exp(sink_l - m))).astype(v.dtype)
    o = jnp.einsum('bnhgqk,bnkhd->bnqhgd', probs, vw)
    return o.reshape(B, S, GQA_Q_HEADS * GQA_HEAD_DIM)

def first_inputs(seed: int = 0) -> dict:
    key = jax.random.key(seed)
    ks = iter(jax.random.split(key, 32))

    def w(shape, fan_in):
        return jax.random.normal(next(ks), shape, jnp.float32) * (fan_in ** -0.5)

    def gain(n):
        return 1.0 + 0.1 * jax.random.normal(next(ks), (DEPTH, n), jnp.float32)

    x = jax.random.normal(next(ks), (BATCH, SEQ, D_MODEL), jnp.float32)
    p = jax.random.normal(next(ks), (DEPTH, BATCH, SEQ, PLE_DIM), jnp.float32)
    offset = jax.random.randint(next(ks), (BATCH, 1), 0, 4096, jnp.int32)
    positions = (offset + jnp.arange(SEQ, dtype=jnp.int32)[None, :]).astype(jnp.int32)
    return {
        'x': x,
        'p': p,
        'positions': positions,
        'norm_mix_pre': gain(D_MODEL),
        'w_in': w((DEPTH, D_MODEL, IN_COLS), D_MODEL),
        'mla_q_norm': gain(MLA_Q_LORA),
        'w_uq': w((DEPTH, MLA_Q_LORA, MLA_HEADS * MLA_QK), MLA_Q_LORA),
        'mla_kv_norm': gain(MLA_KV_LORA),
        'w_ukv': w((DEPTH, MLA_KV_LORA, MLA_HEADS * (MLA_NOPE + MLA_V)), MLA_KV_LORA),
        'gqa_sink': 0.5 * jax.random.normal(next(ks), (DEPTH, GQA_Q_HEADS), jnp.float32),
        'w_branch_a': w((DEPTH, MLA_HEADS * MLA_V, D_MODEL), MLA_HEADS * MLA_V),
        'w_branch_b': w((DEPTH, D_MODEL, D_MODEL), D_MODEL),
        'w_branch_c': w((DEPTH, GQA_Q_HEADS * GQA_HEAD_DIM, D_MODEL), GQA_Q_HEADS * GQA_HEAD_DIM),
        'w_out': w((DEPTH, D_MODEL, D_MODEL), D_MODEL),
        'norm_mix_post': gain(D_MODEL),
        'norm_ffn_pre': gain(D_MODEL),
        'w_ffn_gate': w((DEPTH, D_MODEL, FFN_DIM), D_MODEL),
        'w_ffn_up': w((DEPTH, D_MODEL, FFN_DIM), D_MODEL),
        'w_ffn_down': w((DEPTH, FFN_DIM, D_MODEL), FFN_DIM),
        'norm_ffn_post': gain(D_MODEL),
        'w_ple_proj': w((DEPTH, PLE_DIM, D_MODEL), PLE_DIM),
        'w_ple_gate': w((DEPTH, D_MODEL, D_MODEL), D_MODEL),
        'norm_ple': gain(D_MODEL),
    }

def first_block(x, p, positions, norm_mix_pre, w_in, mla_q_norm, w_uq, mla_kv_norm, w_ukv,
              gqa_sink, w_branch_a, w_branch_b, w_branch_c, w_out, norm_mix_post,
              norm_ffn_pre, w_ffn_gate, w_ffn_up, w_ffn_down, norm_ffn_post,
              w_ple_proj, w_ple_gate, norm_ple):
    split_points = list(np.cumsum(IN_SPLITS)[:-1])
    for i in range(DEPTH):
        h = rms_norm(x, norm_mix_pre[i])
        z = h @ w_in[i]
        c_q, c_kv, k_rope, q_c, k_c, v_c, g_a, g_b, g_c = jnp.split(z, split_points, axis=-1)
        o_a = mla_attention(c_q, c_kv, k_rope, positions, mla_q_norm[i], w_uq[i],
                            mla_kv_norm[i], w_ukv[i])
        o_b = fourier_mix(h)
        o_c = windowed_gqa(q_c, k_c, v_c, positions, gqa_sink[i])
        merged = (jax.nn.sigmoid(g_a) * (o_a @ w_branch_a[i])
                  + jax.nn.sigmoid(g_b) * (o_b @ w_branch_b[i])
                  + jax.nn.sigmoid(g_c) * (o_c @ w_branch_c[i]))
        x = x + rms_norm(merged @ w_out[i], norm_mix_post[i])
        h = rms_norm(x, norm_ffn_pre[i])
        ff = (jax.nn.silu(h @ w_ffn_gate[i]) * (h @ w_ffn_up[i])) @ w_ffn_down[i]
        x = x + rms_norm(ff, norm_ffn_post[i])
        e = (p[i] @ w_ple_proj[i]) * jax.nn.sigmoid(x @ w_ple_gate[i])
        x = x + rms_norm(e, norm_ple[i])
    return x


HEAD_DIM = 64
A_HEADS = 8
B_HEADS = 4
DILATED_CONFIGS = ((128, 1), (512, 4), (2048, 16))
MAX_WINDOW = 2048
A_WIDTH = A_HEADS * HEAD_DIM
B_QK_WIDTH = B_HEADS * 2 * HEAD_DIM
B_V_WIDTH = B_HEADS * 2 * HEAD_DIM
ATTN_IN = 3 * A_WIDTH + 2 * B_QK_WIDTH + B_V_WIDTH
ATTN_OUT = A_WIDTH + B_V_WIDTH
ATTN_SPLITS = (A_WIDTH, 2 * A_WIDTH, 3 * A_WIDTH, 3 * A_WIDTH + B_QK_WIDTH, 3 * A_WIDTH + 2 * B_QK_WIDTH)
LRU_WIDTH = D_MODEL
LRU_BLOCKS = 8
LRU_BLOCK_WIDTH = LRU_WIDTH // LRU_BLOCKS
LRU_C = 8.0
REC_CONV = 4
FFN_DIM_2 = 3 * D_MODEL
FFN_CONV = 3

N_EVEN = (DEPTH + 1) // 2
N_ODD = DEPTH // 2
NORM_EPS = 1e-6
NEG_INF = -1e30


def rms_norm_2(x, g):
    xf = x.astype(jnp.float32)
    y = xf * lax.rsqrt(jnp.mean(xf * xf, axis=-1, keepdims=True) + NORM_EPS)
    return (y * g.astype(jnp.float32)).astype(x.dtype)

def alibi_slopes_2(n):
    return jnp.exp2(-8.0 * jnp.arange(1, n + 1, dtype=jnp.float32) / n)

def causal_depthwise_conv(x, w, b):
    K, C = w.shape
    y = lax.conv_general_dilated(
        x, w.astype(x.dtype)[:, None, :], window_strides=(1,), padding=((K - 1, 0),),
        dimension_numbers=('NWC', 'WIO', 'NWC'), feature_group_count=C)
    return y + b.astype(x.dtype)

def dilated_branch(q, k, v, slopes, window, dilation):
    B, S, H, E = q.shape
    n = window // dilation
    L = S // dilation
    nb = L // n

    def to_blocks(t):
        t = t.reshape(B, L, dilation, H, E).transpose(0, 2, 3, 1, 4)
        return t.reshape(B, dilation, H, nb, n, E)

    def with_prev(t):
        prev = jnp.pad(t[:, :, :, :-1], ((0, 0), (0, 0), (0, 0), (1, 0), (0, 0), (0, 0)))
        return jnp.concatenate([prev, t], axis=4)

    qb = to_blocks(q)
    kb = with_prev(to_blocks(k))
    vb = with_prev(to_blocks(v))
    s = jnp.einsum('bdhnqe,bdhnke->bdhnqk', qb, kb) * (E ** -0.5)
    kj = jnp.arange(2 * n)[None, :]
    delta = jnp.arange(n)[:, None] + n - kj
    in_band = (delta >= 0) & (delta <= n)
    after_start = (jnp.arange(nb)[:, None, None] > 0) | (kj[None] >= n)
    valid = in_band[None] & after_start
    dist = (delta * dilation).astype(jnp.float32)
    s = jnp.where(valid, s - slopes[:, None, None, None] * dist, NEG_INF)
    m = jnp.max(s, axis=-1, keepdims=True)
    e = jnp.exp(s - m)
    den = jnp.sum(e, axis=-1)
    o = jnp.einsum('bdhnqk,bdhnke->bdhnqe', e, vb) / den[..., None]
    lse = m[..., 0] + jnp.log(den)
    o = o.reshape(B, dilation, H, L, E).transpose(0, 3, 1, 2, 4).reshape(B, S, H, E)
    lse = lse.reshape(B, dilation, H, L).transpose(0, 3, 1, 2).reshape(B, S, H)
    return o, lse

def dilated_mixture_attention(q, k, v, slopes):
    B, S, H, E = q.shape
    s_pad = -(-S // MAX_WINDOW) * MAX_WINDOW
    pad = ((0, 0), (0, s_pad - S), (0, 0), (0, 0))
    qf, kf, vf = [jnp.pad(t.astype(jnp.float32), pad) for t in (q, k, v)]
    outs, lses = zip(*[dilated_branch(qf, kf, vf, slopes, w, d) for w, d in DILATED_CONFIGS])
    weights = jax.nn.softmax(jnp.stack(lses), axis=0)
    o = jnp.sum(weights[..., None] * jnp.stack(outs), axis=0)
    return o[:, :S]

def differential_attention(q, k, v, slopes, lam):
    B, S, H, _, E = q.shape
    n_blocks = S // Q_BLOCK
    kf = k.astype(jnp.float32)
    vf = v.astype(jnp.float32)
    kpos = jnp.arange(S)
    sl = slopes[:, None, None, None]

    def one_block(i):
        qs = lax.dynamic_slice_in_dim(q, i * Q_BLOCK, Q_BLOCK, axis=1).astype(jnp.float32)
        s = jnp.einsum('bqhce,bkhce->bhcqk', qs, kf) * (E ** -0.5)
        dist = (i * Q_BLOCK + jnp.arange(Q_BLOCK))[:, None] - kpos[None, :]
        s = jnp.where(dist >= 0, s - sl * dist.astype(jnp.float32), NEG_INF)
        p = jax.nn.softmax(s, axis=-1)
        attn = p[:, :, 0] - lam * p[:, :, 1]
        return jnp.einsum('bhqk,bkhe->bqhe', attn, vf)

    o = lax.map(one_block, jnp.arange(n_blocks))
    return jnp.moveaxis(o, 0, 1).reshape(B, S, H, 2 * E)

def hybrid_attention_mixer(x, w_in, w_out, a_q_norm, a_k_norm, b_q_norm, b_k_norm, b_sub_norm,
                           lam_q1, lam_k1, lam_q2, lam_k2, lam_init):
    B, S, _ = x.shape
    proj = x @ w_in.astype(x.dtype)
    qa, ka, va, qb, kb, vb = jnp.split(proj, list(ATTN_SPLITS), axis=-1)
    qa = rms_norm_2(qa.reshape(B, S, A_HEADS, HEAD_DIM), a_q_norm)
    ka = rms_norm_2(ka.reshape(B, S, A_HEADS, HEAD_DIM), a_k_norm)
    va = va.reshape(B, S, A_HEADS, HEAD_DIM)
    qb = rms_norm_2(qb.reshape(B, S, B_HEADS, 2, HEAD_DIM), b_q_norm)
    kb = rms_norm_2(kb.reshape(B, S, B_HEADS, 2, HEAD_DIM), b_k_norm)
    vb = vb.reshape(B, S, B_HEADS, 2 * HEAD_DIM)
    slopes = alibi_slopes_2(A_HEADS + B_HEADS)
    oa = dilated_mixture_attention(qa, ka, va, slopes[:A_HEADS])
    f32 = jnp.float32
    lam = (jnp.exp(jnp.sum(lam_q1.astype(f32) * lam_k1.astype(f32)))
           - jnp.exp(jnp.sum(lam_q2.astype(f32) * lam_k2.astype(f32))) + lam_init)
    ob = differential_attention(qb, kb, vb, slopes[A_HEADS:], lam)
    ob = rms_norm_2(ob, b_sub_norm) * (1.0 - lam_init)
    y = jnp.concatenate([oa.reshape(B, S, A_WIDTH), ob.reshape(B, S, B_V_WIDTH)], axis=-1).astype(x.dtype)
    return y @ w_out.astype(x.dtype)

def linear_combine(left, right):
    a_l, b_l = left
    a_r, b_r = right
    return a_l * a_r, a_r * b_l + b_r

def rg_lru(x, gate_a_w, gate_a_b, gate_x_w, gate_x_b, a_param):
    B, S, C = x.shape
    xb = x.reshape(B, S, LRU_BLOCKS, LRU_BLOCK_WIDTH)

    def block_diag(w, b):
        y = jnp.einsum('bsnc,ncd->bsnd', xb, w.astype(x.dtype)).reshape(B, S, C) + b.astype(x.dtype)
        return y.astype(jnp.float32)

    r = jax.nn.sigmoid(block_diag(gate_a_w, gate_a_b))
    i = jax.nn.sigmoid(block_diag(gate_x_w, gate_x_b))
    log_a = -LRU_C * r * jax.nn.softplus(-a_param.astype(jnp.float32))
    a = jnp.exp(log_a)
    u = jnp.sqrt(-jnp.expm1(2.0 * log_a)) * (i * x.astype(jnp.float32))
    _, h = lax.associative_scan(linear_combine, (a, u), axis=1)
    return h.astype(x.dtype)

def recurrent_mixer(x, w_in, conv_w, conv_b, gate_a_w, gate_a_b, gate_x_w, gate_x_b, a_param, w_out):
    gate, xr = jnp.split(x @ w_in.astype(x.dtype), [LRU_WIDTH], axis=-1)
    xr = causal_depthwise_conv(xr, conv_w, conv_b)
    h = rg_lru(xr, gate_a_w, gate_a_b, gate_x_w, gate_x_b, a_param)
    return (h * jax.nn.gelu(gate)) @ w_out.astype(x.dtype)

def conv_ffn(x, w_up, conv_w, conv_b, w_down):
    u = causal_depthwise_conv(x @ w_up.astype(x.dtype), conv_w, conv_b)
    g, val = jnp.split(u, [FFN_DIM_2], axis=-1)
    return (jax.nn.gelu(g) * val) @ w_down.astype(x.dtype)

def second_inputs(seed: int = 0) -> dict:
    key = jax.random.key(seed)
    ks = iter(jax.random.split(key, 40))
    f32 = jnp.float32

    def normal(shape, scale):
        return scale * jax.random.normal(next(ks), shape, f32)

    def gain(shape):
        return 1.0 + 0.02 * jax.random.normal(next(ks), shape, f32)

    u = jax.random.uniform(next(ks), (N_ODD, LRU_WIDTH), f32, 0.9, 0.999)
    a0 = u ** (1.0 / LRU_C)
    a_param = jnp.log(a0) - jnp.log1p(-a0)
    return {
        'x': normal((BATCH, SEQ, D_MODEL), 1.0),
        'attn_norm': gain((N_EVEN, D_MODEL)),
        'attn_w_in': normal((N_EVEN, D_MODEL, ATTN_IN), D_MODEL ** -0.5),
        'attn_w_out': normal((N_EVEN, ATTN_OUT, D_MODEL), ATTN_OUT ** -0.5),
        'a_q_norm': gain((N_EVEN, HEAD_DIM)),
        'a_k_norm': gain((N_EVEN, HEAD_DIM)),
        'b_q_norm': gain((N_EVEN, HEAD_DIM)),
        'b_k_norm': gain((N_EVEN, HEAD_DIM)),
        'b_sub_norm': gain((N_EVEN, 2 * HEAD_DIM)),
        'b_lam_q1': normal((N_EVEN, HEAD_DIM), 0.1),
        'b_lam_k1': normal((N_EVEN, HEAD_DIM), 0.1),
        'b_lam_q2': normal((N_EVEN, HEAD_DIM), 0.1),
        'b_lam_k2': normal((N_EVEN, HEAD_DIM), 0.1),
        'rec_norm': gain((N_ODD, D_MODEL)),
        'rec_w_in': normal((N_ODD, D_MODEL, 2 * LRU_WIDTH), D_MODEL ** -0.5),
        'rec_conv_w': normal((N_ODD, REC_CONV, LRU_WIDTH), REC_CONV ** -0.5),
        'rec_conv_b': normal((N_ODD, LRU_WIDTH), 0.01),
        'rec_gate_a_w': normal((N_ODD, LRU_BLOCKS, LRU_BLOCK_WIDTH, LRU_BLOCK_WIDTH), LRU_BLOCK_WIDTH ** -0.5),
        'rec_gate_a_b': normal((N_ODD, LRU_WIDTH), 0.01),
        'rec_gate_x_w': normal((N_ODD, LRU_BLOCKS, LRU_BLOCK_WIDTH, LRU_BLOCK_WIDTH), LRU_BLOCK_WIDTH ** -0.5),
        'rec_gate_x_b': normal((N_ODD, LRU_WIDTH), 0.01),
        'rec_a_param': a_param,
        'rec_w_out': normal((N_ODD, LRU_WIDTH, D_MODEL), LRU_WIDTH ** -0.5),
        'ffn_norm': gain((DEPTH, D_MODEL)),
        'ffn_w_up': normal((DEPTH, D_MODEL, 2 * FFN_DIM_2), D_MODEL ** -0.5),
        'ffn_conv_w': normal((DEPTH, FFN_CONV, 2 * FFN_DIM_2), FFN_CONV ** -0.5),
        'ffn_conv_b': normal((DEPTH, 2 * FFN_DIM_2), 0.01),
        'ffn_w_down': normal((DEPTH, FFN_DIM_2, D_MODEL), FFN_DIM_2 ** -0.5),
    }

def second_block(x, attn_norm, attn_w_in, attn_w_out, a_q_norm, a_k_norm, b_q_norm, b_k_norm, b_sub_norm,
              b_lam_q1, b_lam_k1, b_lam_q2, b_lam_k2, rec_norm, rec_w_in, rec_conv_w, rec_conv_b,
              rec_gate_a_w, rec_gate_a_b, rec_gate_x_w, rec_gate_x_b, rec_a_param, rec_w_out,
              ffn_norm, ffn_w_up, ffn_conv_w, ffn_conv_b, ffn_w_down):
    h = x
    for layer in range(DEPTH):
        j = layer // 2
        if layer % 2 == 0:
            lam_init = 0.8 - 0.6 * math.exp(-0.3 * layer)
            h = h + hybrid_attention_mixer(
                rms_norm_2(h, attn_norm[j]), attn_w_in[j], attn_w_out[j], a_q_norm[j], a_k_norm[j],
                b_q_norm[j], b_k_norm[j], b_sub_norm[j], b_lam_q1[j], b_lam_k1[j], b_lam_q2[j], b_lam_k2[j],
                lam_init)
        else:
            h = h + recurrent_mixer(
                rms_norm_2(h, rec_norm[j]), rec_w_in[j], rec_conv_w[j], rec_conv_b[j], rec_gate_a_w[j],
                rec_gate_a_b[j], rec_gate_x_w[j], rec_gate_x_b[j], rec_a_param[j], rec_w_out[j])
        h = h + conv_ffn(rms_norm_2(h, ffn_norm[layer]), ffn_w_up[layer], ffn_conv_w[layer],
                         ffn_conv_b[layer], ffn_w_down[layer])
    return h


def setup_inputs(seed=0):
    out = dict(first_inputs(seed))
    for name, value in second_inputs(seed + 1).items():
        if name != "x":
            out[name + "_2"] = value
    return out


def reference(
    x, p, positions, norm_mix_pre, w_in, mla_q_norm, w_uq, mla_kv_norm, w_ukv, gqa_sink,
    w_branch_a, w_branch_b, w_branch_c, w_out, norm_mix_post, norm_ffn_pre, w_ffn_gate,
    w_ffn_up, w_ffn_down, norm_ffn_post, w_ple_proj, w_ple_gate, norm_ple, attn_norm_2,
    attn_w_in_2, attn_w_out_2, a_q_norm_2, a_k_norm_2, b_q_norm_2, b_k_norm_2, b_sub_norm_2,
    b_lam_q1_2, b_lam_k1_2, b_lam_q2_2, b_lam_k2_2, rec_norm_2, rec_w_in_2, rec_conv_w_2,
    rec_conv_b_2, rec_gate_a_w_2, rec_gate_a_b_2, rec_gate_x_w_2, rec_gate_x_b_2, rec_a_param_2,
    rec_w_out_2, ffn_norm_2, ffn_w_up_2, ffn_conv_w_2, ffn_conv_b_2, ffn_w_down_2,
):
    x = first_block(
        x, p, positions, norm_mix_pre, w_in, mla_q_norm, w_uq, mla_kv_norm, w_ukv, gqa_sink,
        w_branch_a, w_branch_b, w_branch_c, w_out, norm_mix_post, norm_ffn_pre, w_ffn_gate,
        w_ffn_up, w_ffn_down, norm_ffn_post, w_ple_proj, w_ple_gate, norm_ple,
    )
    return second_block(
        x, attn_norm_2, attn_w_in_2, attn_w_out_2, a_q_norm_2, a_k_norm_2, b_q_norm_2,
        b_k_norm_2, b_sub_norm_2, b_lam_q1_2, b_lam_k1_2, b_lam_q2_2, b_lam_k2_2, rec_norm_2,
        rec_w_in_2, rec_conv_w_2, rec_conv_b_2, rec_gate_a_w_2, rec_gate_a_b_2, rec_gate_x_w_2,
        rec_gate_x_b_2, rec_a_param_2, rec_w_out_2, ffn_norm_2, ffn_w_up_2, ffn_conv_w_2,
        ffn_conv_b_2, ffn_w_down_2,
    )


_drawn_inputs = setup_inputs


def setup_inputs(seed=0):
    import zlib

    import numpy as np

    out = dict(_drawn_inputs(seed))
    spreads = {}
    factors = {'mla_q_norm': 4.023,
     'gqa_sink': 5.316,
     'attn_norm_2': 6.695,
     'a_q_norm_2': 8.0,
     'a_k_norm_2': 8.0,
     'b_q_norm_2': 8.0,
     'b_k_norm_2': 8.0,
     'b_sub_norm_2': 8.0,
     'b_lam_q1_2': 7.848,
     'b_lam_k1_2': 8.0,
     'rec_norm_2': 8.0,
     'rec_conv_b_2': 5.307,
     'rec_gate_a_b_2': 58.297,
     'rec_gate_x_b_2': 56.971,
     'ffn_norm_2': 5.825,
     'ffn_conv_b_2': 8.0}
    for name, (base, spread) in spreads.items():
        noise = np.random.default_rng([zlib.crc32(name.encode()), seed]).standard_normal(out[name].shape)
        drawn = base * np.exp(spread * noise) if base else spread * noise
        out[name] = __import__('jax').numpy.asarray(drawn.astype(out[name].dtype))
    for name, factor in factors.items():
        out[name] = (out[name] * factor).astype(out[name].dtype)
    return out
```

```python
from contextlib import ExitStack

import numpy as np
import concourse.bass as bass
from concourse import mybir

P = 128
SEQ = 512
ST = SEQ // P
DM = 1024
DT = DM // P
LAYERS = 2
FFN1 = 2816
FT1 = FFN1 // P
FFN2 = 3 * DM
FT2 = FFN2 // P
MLA_H, MLA_QK, MLA_NOPE, MLA_ROPE, MLA_V = 8, 96, 64, 32, 64
Q_LORA, KV_LORA = 384, 128
QT = Q_LORA // P
HD = 64
GQA_H = 8
DIL_H, DIFF_H = 8, 4
PLE = 256
WINDOW = 128
COL_ROPE = Q_LORA + KV_LORA
COL_QC = COL_ROPE + MLA_ROPE
COL_KC = COL_QC + GQA_H * HD
COL_VC = COL_KC + 2 * HD
COL_GATE = COL_VC + 2 * HD
FGROUP = 256
FGROUPS = DM // FGROUP
EPS = 1e-6
LAM_INIT = 0.2
LRU_C = 8.0
MASKED = 1e30
LOG_TERMS = 8
LP_STEPS = 10 + LOG_TERMS
RING = 64
SLOTS = 4
BLOCKS = 8
AHEAD = 3
BANKS = 4

F32 = mybir.dt.float32
F32R = mybir.dt.float32r
I32 = mybir.dt.int32
ALU = mybir.AluOpType
ACT = mybir.ActivationFunctionType
AXX = mybir.AxisListType.X


def column_plan():
    at, n = {}, 0
    names = []
    for l in range(LAYERS):
        names += [(f"norm_mix_pre{l}", DT), (f"mla_q_norm{l}", QT), (f"mla_kv_norm{l}", 1),
                  (f"norm_mix_post{l}", DT), (f"norm_ffn_pre{l}", DT), (f"norm_ffn_post{l}", DT),
                  (f"norm_ple{l}", DT), (f"gqa_sink{l}", GQA_H), (f"ffn_norm_2{l}", DT)]
        names += [(f"ffn_conv_w_2{l}_{k}", 2 * FT2) for k in range(3)] + [(f"ffn_conv_b_2{l}", 2 * FT2)]
    names += [("attn_norm_20", DT), ("a_q_norm_20", 1), ("a_k_norm_20", 1), ("b_q_norm_20", 1),
              ("b_k_norm_20", 1), ("b_sub_norm_20", 1), ("rec_norm_20", DT)]
    names += [(f"rec_conv_w_20_{k}", DT) for k in range(4)]
    names += [(f"{v}0", DT) for v in ("rec_conv_b_2", "rec_gate_a_b_2", "rec_gate_x_b_2", "rec_a_param_2")]
    for name, tiles in names:
        at[name] = n
        n += tiles
    return at, n


COL, N_COLS = column_plan()


def unit_list():
    u = []

    def product(name, l, rows, c):
        for k in range(0, rows, DM):
            u.append((name, l, k, min(DM, rows - k), c, P))

    def gates_and_branch(name, l, rows, gate):
        for n in range(DT):
            product("w_in", l, DM, COL_GATE + gate * DM + n * P)
            product(name, l, rows, n * P)

    for l in range(LAYERS):
        gates_and_branch("w_branch_b", l, DM, 1)
        for c in [n * P for n in range(4)] + [COL_QC + n * P for n in range(4)] + [COL_KC, COL_VC, COL_ROPE]:
            product("w_in", l, DM, c)
        gates_and_branch("w_branch_c", l, GQA_H * HD, 2)
        for n in range(MLA_H // 2):
            u.append(("w_uq", l, 0, Q_LORA, n * 2 * MLA_QK, 2 * MLA_QK))
        u.append(("w_ukv", l, 0, KV_LORA, 0, MLA_H * P))
        gates_and_branch("w_branch_a", l, MLA_H * MLA_V, 0)
        for n in range(DT):
            product("w_out", l, DM, n * P)
        for n in range(FT1):
            product("w_ffn_gate", l, DM, n * P)
            product("w_ffn_up", l, DM, n * P)
        for n in range(DT):
            product("w_ffn_down", l, FFN1, n * P)
        for n in range(DT):
            product("w_ple_proj", l, PLE, n * P)
            product("w_ple_gate", l, DM, n * P)

    def conv_ffn(l):
        for n in range(FT2):
            product("ffn_w_up_2", l, DM, n * P)
            product("ffn_w_up_2", l, DM, FFN2 + n * P)
        for n in range(DT):
            product("ffn_w_down_2", l, FFN2, n * P)

    for n in range(3 * DM // P):
        product("attn_w_in_2", 0, DM, n * P)
    for n in range(DT):
        product("attn_w_out_2", 0, DM, n * P)
    conv_ffn(0)
    for n in range(2 * DT):
        product("rec_w_in_2", 0, DM, n * P)
    u.append(("rec_gate_a_w_2", 0, 0, 0, 0, 0))
    u.append(("rec_gate_x_w_2", 0, 0, 0, 0, 0))
    for n in range(DT):
        product("rec_w_out_2", 0, DM, n * P)
    conv_ffn(1)
    return u


UNITS = unit_list()
NU = len(UNITS)


class Stage:

    def __init__(self, kind, reps, units, tiles, per, *, u0, t0, base, rb=None, width=0, where=None, src=None, dst=None,
                 gain=None, n=0, stat=False, y=None, gy=None, t=0, made=None, kt=0, first=False, last=False, op=0, mode=None,
                 heads=0, comps=1, out=None, l=0, proj=None, rope=None, qk=None, att=None, norm=None, taps=0):
        self.kind, self.reps, self.units, self.tiles, self.per = kind, reps, units, tiles, per
        self.u0, self.t0, self.base = u0, t0, base
        self.rb, self.width, self.where = rb, width, where
        self.src, self.dst, self.gain, self.n, self.stat = src, dst, gain, n, stat
        self.y, self.gy, self.t, self.made, self.kt = y, gy, t, made, kt
        self.first, self.last, self.op, self.mode, self.heads, self.comps = first, last, op, mode, heads, comps
        self.out, self.l, self.proj, self.rope, self.qk, self.att = out, l, proj, rope, qk, att
        self.norm, self.taps = norm, taps

    def at(self, signal, k, r=0):
        return self.base.get(signal, 0) + r * self.per.get(signal, 0) + k

    def unit(self, j, r=0):
        return self.u0 + r * self.units + j

    def bank(self, k):
        return (self.t0 + k) % BANKS

    def use(self, k, r=0):
        return (self.t0 + k) // BANKS + r * (self.tiles // BANKS)


def plan():
    steps, count = [], {}
    at = [0, 0]

    def add(kind, reps=1, units=0, tiles=0, per=(), **opt):
        st = Stage(kind, reps, units, tiles, dict(per), u0=at[0], t0=at[1], base=dict(count), **opt)
        at[0] += reps * units
        at[1] += reps * tiles
        for k, v in st.per.items():
            count[k] = count.get(k, 0) + reps * v
        steps.append(st)
        return st

    def norm(rb, width, where="now"):
        return add("norm", per={k: 1 for k in ("norm_summed", "mean_square_ready", "factors_ready", "factors_spread", "factor_rows_ready")}, rb=rb, width=width, where=where)

    def operand(src, dst, gain, n, stat, y=None, gy=None, t=0, made=None):
        per = {"operand_hi_ready": n, "operand_ready": n}
        if stat:
            per |= {"square_ready": n, "sum_cleared": 1, "square_added": n}
        if y:
            per |= {"update_ready": n, "residual_updated": n}
        return add("operand", per=per, src=src, dst=dst, gain=gain, n=n, stat=stat, y=y, gy=gy, t=t, made=made)

    def need(kt):
        return count["operand_ready"] - kt

    def branch(kt, src, first, last):
        op, per = need(kt), {"gate_ready": 2} | ({} if first else {"product_ready": 2})
        if last:
            per |= {"operand_hi_ready": 2, "operand_ready": 2}
        return add("branch", 4, 4, 4, per, kt=kt, src=src, first=first, last=last, op=op)

    def out_y(src, kt, y):
        n = -(-kt // BLOCKS)
        add("zero", per={"sum_cleared": 1})
        return add("out_y", 2, 4 * n, 4, {"square_added": 4}, kt=kt, src=src, y=y, op=need(kt))

    def residual(src, kt, gain):
        n, op = -(-kt // BLOCKS), need(kt)
        per = {}
        if gain:
            add("zero", per={"sum_cleared": 1})
            per = {"operand_hi_ready": 4, "operand_ready": 4, "square_ready": 4, "square_added": 4}
        return add("residual", 2, 4 * n, 4, per, kt=kt, src=src, gain=gain, op=op)

    def attention(mode, heads, comps, out, **opt):
        n = heads * comps * ST
        per = {k: n for k in ("scores_ready", "max_ready", "neg_max_ready", "exp_ready", "inverse_ready", "probs_ready", "probs_turned", "turned_copied")}
        per |= {"head_multiplied": heads * comps}
        per |= {"gqa": {"sink_exp_ready": n, "sink_added": n}, "mla": {}, "dilated": {"counts_applied": n}, "diff": {"lambda_applied": n}}[mode]
        if mode != "mla":
            per["scores_read"] = n
        if mode != "diff":
            per |= {"operand_hi_ready": heads // 2, "operand_ready": heads // 2}
        return add("attention", tiles=heads, per=per, mode=mode, heads=heads, comps=comps, out=out, **opt)

    add("init", tiles=DT, per={"rows_turned": DT, "table_stepped": 16, "table_looked_up": 8, "dft_hi_ready": 1, "dft_lo_ready": 1})
    for l in range(LAYERS):
        operand("X", "H", f"norm_mix_pre{l}", DT, True, **(dict(made=steps[0]) if l == 0 else {}), **(dict(y="YP", gy=f"norm_ple{l - 1}") if l else {}))
        op = need(DT)
        n = norm("X", DM, "inner")
        f = add("fourier", tiles=FGROUPS * (ST + 2), per={"channels_transformed": 16, "tokens_transformed": 8, "operand_hi_ready": 8, "operand_ready": 8, "dft_loaded": 32}, op=op, norm=n)
        branch(DT, "OB", True, False)
        pr = add("proj", units=11, tiles=12, per={"keys_copied": 2, "values_turned": 1})
        attention("gqa", GQA_H, 1, "OC", l=l, proj=pr)
        branch(GQA_H // 2, "OC", False, False)
        operand("CQ", "CQ", f"mla_q_norm{l}", QT, True, made=pr)
        norm("Q", Q_LORA)
        operand("CQ", "CQ", f"mla_kv_norm{l}", 1, True, t=QT, made=pr)
        norm("K", KV_LORA)
        heads = add("mla_heads", units=5, tiles=20, per={"part_multiplied": 4 + 11}, op=need(QT + 1))
        rp = add("rope", tiles=MLA_H + 1, per={"rope_rotated": 9, "cos_applied": 9, "rope_added": 9, "rope_keys_spread": 1}, proj=pr, heads=heads)
        attention("mla", MLA_H, 1, "OA", l=l, rope=rp)
        branch(MLA_H // 2, "OA", False, True)
        out_y("MG", DT, "YH")
        norm("Y", DM)
        operand("X", "H", f"norm_ffn_pre{l}", DT, True, y="YH", gy=f"norm_mix_post{l}")
        op = need(DT)
        n = norm("X", DM, "inner")
        add("swiglu", FT1 // 2, 4, 4, {"gate_ready": 2, "product_ready": 2, "operand_hi_ready": 2, "operand_ready": 2}, op=op, norm=n)
        out_y("F1", FT1, "YH")
        norm("Y", DM)
        add("ple_in", tiles=2, per={"ple_loaded": 16, "ple_turned": 2, "operand_hi_ready": 2, "operand_ready": 2}, l=l)
        operand("X", "H", None, DT, False, y="YH", gy=f"norm_ffn_post{l}")
        add("zero", per={"sum_cleared": 1})
        add("ple", 4, 4, 4, {"product_ready": 2, "square_ready": 2, "square_added": 2}, op=need(DT + 2))
        norm("Y", DM)
    operand("X", "H", "attn_norm_20", DT, True, y="YP", gy=f"norm_ple{LAYERS - 1}")
    op = need(DT)
    n = norm("X", DM, "inner")
    add("tables2", per={"tables_loaded": 32, "tables_stepped": 7, "lambda_exp_ready": 1})
    add("qkv", 6, 4, 4, {"part_multiplied": 2}, op=op, norm=n)
    qk = add("qk_norm", tiles=16, per={"qk_square_ready": 16, "qk_square_summed": 16, "qk_factors_stepped": 3, "qk_normed": 16, "qk_turned": 16})
    attention("dilated", DIL_H, 1, "O2", l=0, qk=qk)
    diff = attention("diff", DIFF_H, 2, "U", l=0, qk=qk)
    add("sub_norm", tiles=4, att=diff, per={"out_square_ready": 4, "out_squares_summed": 1, "out_mean_ready": 1, "out_factors_ready": 1, "out_factors_spread": 4, "operand_hi_ready": 4, "operand_ready": 4})
    residual("O2", DT, "ffn_norm_20")

    def conv_ffn(l, gain):
        op = need(DT)
        n = norm("X", DM, "inner")
        add("zero_u", per={"zeros_set": 1}, taps=3)
        add("conv_ffn", FT2 // 2, 4, 4, {"conv_begun": 4, "conv_tap_added": 8, "gate_ready": 2, "product_ready": 2, "operand_hi_ready": 2, "operand_ready": 2}, l=l, op=op, norm=n)
        residual("F2", FT2, gain)

    conv_ffn(0, "rec_norm_20")
    op = need(DT)
    n = norm("X", DM, "inner")
    add("zero_u", per={"zeros_set": 1}, taps=4)
    add("rec_gate", 2, 4, 4, {"gate_ready": 4}, op=op, norm=n)
    add("rec_conv", 2, 4, 4, {"conv_begun": 4, "conv_tap_added": 12, "operand_hi_ready": 4, "operand_ready": 4})
    add("rec_lru", units=2, tiles=16, per={"part_multiplied": 14, "decay_abs_ready": 1, "decay_exp_ready": 1, "decay_stepped": LP_STEPS, "decay_ready": 8, "tanh_ready": 8, "decay_squared": 8, "decay_rest_ready": 8,
                                           "root_ready": 8, "gated_input_ready": 8, "scan_input_ready": 8, "scan_done": 8, "product_ready": 8, "operand_hi_ready": 8, "operand_ready": 8}, op=need(DT))
    residual("RO", DT, "ffn_norm_21")
    conv_ffn(1, None)
    add("out", tiles=8, per={"rows_turned": 8, "output_stored": 16 * ST})
    return steps


STEPS = plan()


def build(nc, wall, xin, pin, posi, posc, cols, consts, gmask, dft, dftc, dil, lamv, out_):
    with ExitStack() as ctx:
        KB = 1024
        base = [RING]

        def place(name, shape, dt=F32, at=None):
            size = int(np.prod(shape[1:])) * 4
            if at is None:
                at = base[0]
                base[0] += -(-size // 32) * 32
            assert at + size <= nc.sbuf_usable_end, name
            return nc.alloc_sbuf_tensor_at(name, shape, dt, offset=at)

        def sem(name):
            return ctx.enter_context(nc.semaphore(name))

        X = place("X", [P, DT, SEQ])
        h_at = base[0]
        HH, HL = place("HH", [P, DT, SEQ], F32R), place("HL", [P, DT, SEQ], F32R)
        YH = place("YH", [P, DT, SEQ], at=h_at + 16 * KB)
        HQ = place("HQ", [P, 16, SEQ], at=h_at)
        w_at = base[0]
        WRAW = place("WRAW", [P, SLOTS, BLOCKS * P])
        WLO = place("WLO", [P, SLOTS, BLOCKS * P], F32R, at=w_at)
        WHI = place("WHI", [P, SLOTS, BLOCKS * P], F32R)
        CONST, ONES = place("CONST", [P, P + MLA_QK + 1]), place("ONES", [P, 1])
        IDENT, ROT, INVF = CONST[:, 0:P], CONST[:, P:P + MLA_QK], CONST[:, P + MLA_QK:P + MLA_QK + 1]
        NEGH, VAR = place("NEGH", [P, 16]), place("VAR", [P, 16])
        COLS = place("COLS", [P, N_COLS])
        SG = place("SG", [P, 4, SEQ])
        SQ, TM = place("SQ", [P, 2, SEQ]), place("TM", [P, 2, SEQ])
        ACC = place("ACC", [P, SEQ])
        RBX, RBY = place("RBX", [P, SEQ]), place("RBY", [P, SEQ])
        RC = {k: place(f"RC{k}", [P, 16]) for k in "XYQK"}
        MX, NM, SM, RS, ES = (place(n, [P, 4]) for n in ("MX", "NM", "SM", "RS", "ES"))
        o_at = base[0]
        TDH, TDL = place("TDH", [P, 2, SEQ], F32R), place("TDL", [P, 2, SEQ], F32R)
        COS, SIN = place("COS", [P, SEQ]), place("SIN", [P, SEQ])
        GD = place("GD", [P, ST, 3 * P])
        s_at = base[0]
        DIL = place("DIL", [P, 3, SEQ], at=o_at)
        U = place("U", [P, 4, SEQ + 4], at=o_at + 6 * KB)
        UB = place("UB", [P, 4, SEQ], at=o_at + 6 * KB)
        LAMV = place("LAMV", [P, 4, HD], at=o_at + 15 * KB)
        LS, LT = place("LS", [P, 2], at=o_at + 16 * KB + 64), place("LT", [P, 2], at=o_at + 16 * KB + 96)
        LE = place("LE", [P, 2], at=o_at + 16 * KB + 128)
        SUBG = place("SUBG", [P, 1], at=o_at + 16 * KB + 192)
        GQ = place("GQ", [P, 2], at=o_at + 16 * KB + 160)
        LR = place("LR", [P, 4, DT], at=o_at + 16 * KB + 256)
        base[0] = nc.sbuf_usable_end

        def work(name, shape, at, dt=F32):
            return place(name, shape, dt, at=s_at + at * KB)

        XROWS = work("XROWS", [P, ST, DM], 0)
        POSI, POSC_I = work("POSI", [P, SEQ], 16, I32), work("POSC_I", [P, ST], 18, I32)
        POSF, POSC = work("POSF", [P, SEQ], 20), work("POSC", [P, ST], 22)
        ANG, TURN = work("ANG", [P, SEQ], 24), work("TURN", [P, SEQ], 26)
        GM, TDRAW = work("GM", [P, 3 * P], 30), work("TDRAW", [P, 2, SEQ], 32)
        DFT, PG = work("DFT", [P, 2, ST, SEQ], 0), work("PG", [P, 2, ST, SEQ], 16)
        OBH, OBL = work("OBH", [P, DT, SEQ], 32, F32R), work("OBL", [P, DT, SEQ], 48, F32R)
        MG = work("MG", [P, DT, SEQ], 80)
        CQ, QC, K2 = work("CQ", [P, 4, SEQ], 0), work("QC", [P, 4, SEQ], 30), work("K2", [P, 2, SEQ], 38)
        VCT, VR, KRAW = work("VCT", [P, SEQ], 42), work("VR", [P, ST, P], 44), work("KRAW", [P, SEQ], 12)
        RBQ, RBK = work("RBQ", [P, SEQ], 8), work("RBK", [P, SEQ], 10)
        PT = work("PT", [P, 2, ST, SEQ], 14)
        CQH, CQL = work("CQH", [P, 4, SEQ], 14, F32R), work("CQL", [P, 4, SEQ], 22, F32R)
        QA, KA, VA = work("QA", [P, MLA_H, SEQ], 30), work("KA", [P, MLA_H, SEQ], 46), work("VA", [P, ST, SEQ], 0)
        OCH, OCL = work("OCH", [P, 4, SEQ], 62, F32R), work("OCL", [P, 4, SEQ], 70, F32R)
        OAH, OAL = work("OAH", [P, 4, SEQ], 62, F32R), work("OAL", [P, 4, SEQ], 70, F32R)
        MGH, MGL = work("MGH", [P, DT, SEQ], 14, F32R), work("MGL", [P, DT, SEQ], 30, F32R)
        F1H, F1L = work("F1H", [P, FT1, SEQ], 0, F32R), work("F1L", [P, FT1, SEQ], 44, F32R)
        POH, POL, PROWS = work("POH", [P, 2, SEQ], 0, F32R), work("POL", [P, 2, SEQ], 4, F32R), work("PROWS", [P, ST, PLE], 8)
        YP = work("YP", [P, DT, SEQ], 16)
        QKV, PT2 = work("QKV", [P, ST, 3 * DM], 0), work("PT2", [P, 2, ST, SEQ], 48)
        VQ = work("VQ", [P, P], 48)
        O2H, O2L = work("O2H", [P, DT, SEQ], 64, F32R), work("O2L", [P, DT, SEQ], 80, F32R)
        F2H, F2L = work("F2H", [P, FT2, SEQ], 0, F32R), work("F2L", [P, FT2, SEQ], 48, F32R)
        GG, XR = work("GG", [P, DT, SEQ], 0), work("XR", [P, DT, SEQ], 16)
        XRH, XRL = work("XRH", [P, DT, SEQ], 32, F32R), work("XRL", [P, DT, SEQ], 48, F32R)
        RT, IT = work("RT", [P, DT, SEQ], 64), work("IT", [P, DT, SEQ], 80)
        ROH, ROL = work("ROH", [P, DT, SEQ], 32, F32R), work("ROL", [P, DT, SEQ], 48, F32R)
        YROWS = work("YROWS", [P, ST, DM], 0)

        pair = {"H": (HH, HL), "OB": (OBH, OBL), "OC": (OCH, OCL), "OA": (OAH, OAL), "MG": (MGH, MGL), "CQ": (CQH, CQL),
                "F1": (F1H, F1L), "O2": (O2H, O2L), "F2": (F2H, F2L), "RO": (ROH, ROL)}
        source = {"X": X, "CQ": CQ, "YH": YH, "YP": YP}
        RB = {"X": RBX, "Y": RBY, "Q": RBQ, "K": RBK}

        ps = [ctx.enter_context(nc.psum_tensor(f"ps{b}", [P, SEQ], F32)) for b in range(8)]
        score_ps, turn_ps, stat_ps = ps[4:6], ps[6:8], ps[7]

        raw = [sem(f"raw{s}") for s in range(SLOTS)]
        wt_hi, wt_lo = sem("wt_hi"), sem("wt_lo")
        unit_used = sem("unit_used")
        bank_free = [sem(f"bank_free{b}") for b in range(BANKS)]
        ld = sem("ld")
        cst = sem("cst")
        S = {}

        def sig(name):
            if name not in S:
                S[name] = sem(name)
            return S[name]

        for st in STEPS:
            for name in st.per:
                sig(name)

        def repeat(e, st, body, peel=0):
            for r in range(min(peel, st.reps)):
                body(r)
            left = st.reps - peel
            if left == 1:
                body(st.reps - 1)
            elif left > 1:
                with e.Fori(peel, st.reps) as r:
                    body(r)

        def tile_of(t, A):
            return A[:, t, :] if isinstance(t, int) else A[:, bass.ds(t, 1), :].rearrange("p o s -> p (o s)")

        def col(name, t=0):
            c = COL[name] + t
            return COLS[:, c:c + 1] if isinstance(c, int) else COLS[:, bass.ds(c, 1)]

        def spans(mode, t):
            if mode == "gqa":
                return max(0, t - 1), min(ST, t + 2)
            return (0, ST) if mode == "mla" else (0, t + 1)

        def queries(mode, kt):
            seen = [t for t in range(ST) if spans(mode, t)[0] <= kt < spans(mode, t)[1]]
            return seen[0], seen[-1] + 1

        def half(h, n=HD):
            return slice((h % 2) * n, (h % 2) * n + n)

        FOURIER_ORDER = [("rows", 0), ("norm", 0), ("rows", 1), ("cols", 0), ("rows", 2), ("cols", 1), ("rows", 3),
                         ("cols", 2), ("cols", 3)]

        def fourier_tile(what, g, k):
            n = 0
            for w, gg in FOURIER_ORDER:
                if (w, gg) == (what, g):
                    return n + k
                n += {"rows": ST, "cols": 2, "norm": 0}[w]

        block = ctx.enter_context(nc.Block())

        @block.sync
        def _(sp):
            for u in range(SLOTS):
                sp.dma_start(WRAW[:, u, :], wall[u]).then_inc(raw[u], 16)
            left = (NU - SLOTS) // SLOTS
            with sp.Fori(0, left) as i:
                for s in range(SLOTS):
                    sp.wait_ge(unit_used, i * SLOTS + s + 1)
                    sp.dma_start(WRAW[:, s, :], wall[bass.ds((i + 1) * SLOTS + s, 1)].rearrange("o p n -> (o p) n"))\
                      .then_inc(raw[s], 16)
            for u in range(SLOTS + left * SLOTS, NU):
                sp.wait_ge(unit_used, u - SLOTS + 1)
                sp.dma_start(WRAW[:, u % SLOTS, :], wall[u]).then_inc(raw[u % SLOTS], 16)

        @block.tensor
        def _(pe):
            def weights(u):
                pe.wait_ge(wt_lo, u + 1)

            def three(out_, w, w_at, x_hi, x_lo, first, last):
                pe.matmul(out_, WHI[w_at[0], w_at[1], w_at[2]], x_hi, start=first, stop=False)
                pe.matmul(out_, WHI[w_at[0], w_at[1], w_at[2]], x_lo, start=False, stop=False)
                return pe.matmul(out_, WLO[w_at[0], w_at[1], w_at[2]], x_hi, start=False, stop=last)

            def tile(st, j, k, r, src, kt, k0=0, ready=None, start=True, stop=True, final=None):
                weights(st.unit(j, r))
                s = st.unit(j) % SLOTS
                if start:
                    pe.wait_ge(bank_free[st.bank(k)], st.use(k, r))
                hi, lo = src
                for i in range(kt):
                    if ready is not None:
                        pe.wait_ge(S["operand_ready"], ready + k0 + i + 1)
                    mm = three(ps[st.bank(k)][:, :], None, (slice(None), s, slice(i * P, i * P + P)), hi[:, k0 + i, :],
                               lo[:, k0 + i, :], start and i == 0, stop and i == kt - 1)
                mm.then_inc(final or unit_used, 1)

            def norm(st):
                if st.at("factor_rows_ready", 0) > 0:
                    pe.wait_ge(S["factor_rows_ready"], st.at("factor_rows_ready", 0))
                pe.wait_ge(S["square_added"], st.at("square_added", 0))
                for s in range(ST):
                    mm = pe.matmul(stat_ps[:, s:s + 1], ACC[:, s * P:(s + 1) * P], ONES[:, 0:1], start=True, stop=True)
                mm.then_inc(S["norm_summed"], 1)
                pe.wait_ge(S["factors_ready"], st.at("factors_ready", 1))
                for s in range(ST):
                    mm = pe.transpose(stat_ps[:, s * P:(s + 1) * P], RC[st.rb][:, s:s + 1].to_broadcast([P, P]), IDENT[:, :])
                mm.then_inc(S["factors_spread"], 1)

            def init(st):
                pe.wait_ge(ld, 16 * 8)
                pe.wait_ge(cst, 3)
                for t in range(DT):
                    if st.use(t) > 0:
                        pe.wait_ge(bank_free[st.bank(t)], st.use(t))
                    for s in range(ST):
                        mm = pe.transpose(ps[st.bank(t)][:, s * P:(s + 1) * P], XROWS[:, s, t * P:(t + 1) * P], IDENT[:, :])
                    mm.then_inc(S["rows_turned"], 1)

            def fourier(st):
                for what, g in FOURIER_ORDER:
                    if what == "norm":
                        norm(st.norm)
                    elif what == "rows":
                        for s in range(ST):
                            k = fourier_tile("rows", g, s)
                            pe.wait_ge(bank_free[st.bank(k)], st.use(k))
                            if g == 0 and s == 0:
                                pe.wait_ge(S["dft_lo_ready"], STEPS[0].at("dft_lo_ready", 1))
                            for c in range(2):
                                t = 2 * g + c
                                if s == 0:
                                    pe.wait_ge(S["operand_ready"], st.op + t + 1)
                                o, at = ps[st.bank(k)][:, :], slice(s * P, (s + 1) * P)
                                pe.matmul(o, HH[:, t, at], TDH[:, c, :], start=c == 0, stop=False)
                                pe.matmul(o, HH[:, t, at], TDL[:, c, :], start=False, stop=False)
                                mm = pe.matmul(o, HL[:, t, at], TDH[:, c, :], start=False, stop=c == 1)
                            mm.then_inc(S["channels_transformed"], 1)
                    else:
                        if g == 0:
                            pe.wait_ge(S["dft_loaded"], st.at("dft_loaded", 32))
                        for c in range(2):
                            k = fourier_tile("cols", g, c)
                            pe.wait_ge(bank_free[st.bank(k)], st.use(k))
                            pe.wait_ge(bank_free[st.bank(fourier_tile("rows", g, ST - 1))], st.use(fourier_tile("rows", g, ST - 1)) + 1)
                            pe.wait_ge(bank_free[st.bank(fourier_tile("rows", g, ST - 2))], st.use(fourier_tile("rows", g, ST - 2)) + 1)
                            pe.wait_ge(bank_free[st.bank(fourier_tile("rows", g, ST - 3))], st.use(fourier_tile("rows", g, ST - 3)) + 1)
                            pe.wait_ge(bank_free[st.bank(fourier_tile("rows", g, ST - 4))], st.use(fourier_tile("rows", g, ST - 4)) + 1)
                            for s in range(ST):
                                for part in range(2):
                                    mm = pe.matmul(ps[st.bank(k)][:, :],
                                                   PG[:, g % 2, s, part * FGROUP + c * P:part * FGROUP + (c + 1) * P],
                                                   DFT[:, part, s, :], start=s + part == 0, stop=s == ST - 1 and part == 1)
                            mm.then_inc(S["tokens_transformed"], 1)

            def branch(st):
                def body(r):
                    for j in range(4):
                        if j % 2 == 0:
                            tile(st, j, j, r, pair["H"], DT)
                        else:
                            tile(st, j, j, r, pair[st.src], st.kt, ready=st.op if isinstance(r, int) and r == 0 else None)
                repeat(pe, st, body, 1)

            def proj(st):
                for j in range(11):
                    tile(st, j, j, 0, pair["H"], DT)
                pe.wait_ge(bank_free[st.bank(9)], st.use(9) + 1)
                pe.wait_ge(bank_free[st.bank(11)], st.use(11))
                for s in range(ST):
                    mm = pe.transpose(ps[st.bank(11)][:, s * P:(s + 1) * P], VCT[:, s * P:(s + 1) * P], IDENT[:, :])
                mm.then_inc(S["values_turned"], 1)

            def mla_heads(st):
                hi, lo = pair["CQ"]
                k = 0
                for j in range(4):
                    weights(st.unit(j))
                    s = st.unit(j) % SLOTS
                    for c in range(2):
                        pe.wait_ge(bank_free[st.bank(k)], st.use(k))
                        for i in range(QT):
                            if k == 0:
                                pe.wait_ge(S["operand_ready"], st.op + i + 1)
                            at = i * 2 * MLA_QK + c * MLA_QK
                            mm = three(ps[st.bank(k)][0:MLA_QK, :], None, (slice(None), s, slice(at, at + MLA_QK)),
                                       hi[:, i, :], lo[:, i, :], i == 0, i == QT - 1)
                        mm.then_inc(S["part_multiplied"] if c == 0 else unit_used, 1)
                        k += 1
                weights(st.unit(4))
                s = st.unit(4) % SLOTS
                pe.wait_ge(S["operand_ready"], st.op + QT + 1)
                for h in range(MLA_H):
                    pe.wait_ge(bank_free[st.bank(k)], st.use(k))
                    three(ps[st.bank(k)][0:MLA_NOPE, :], None, (slice(None), s, slice(h * P, h * P + MLA_NOPE)),
                          hi[:, QT, :], lo[:, QT, :], True, True).then_inc(S["part_multiplied"], 1)
                    k += 1
                for t in range(ST):
                    pe.wait_ge(bank_free[st.bank(k)], st.use(k))
                    at = slice(t * P, (t + 1) * P)
                    whi = WHI[:, s, :].rearrange("p (h c) -> p h c", c=P)[:, :, MLA_NOPE:P]
                    wlo = WLO[:, s, :].rearrange("p (h c) -> p h c", c=P)[:, :, MLA_NOPE:P]
                    o = ps[st.bank(k)][:, :]
                    pe.matmul(o, hi[:, QT, at], whi, start=True, stop=False)
                    pe.matmul(o, lo[:, QT, at], whi, start=False, stop=False)
                    pe.matmul(o, hi[:, QT, at], wlo, start=False, stop=True).then_inc(S["part_multiplied"] if t < ST - 1 else unit_used, 1)
                    k += 1

            def rope(st):
                for n in range(MLA_H + 1):
                    pe.wait_ge(bank_free[st.bank(n)], st.use(n))
                    if n == 0:
                        pr = st.proj
                        pe.wait_ge(bank_free[pr.bank(10)], pr.use(10) + 1)
                        pe.matmul(ps[st.bank(n)][0:MLA_QK, :], ROT[MLA_NOPE:MLA_QK, :], KRAW[MLA_NOPE:MLA_QK, :],
                                  start=True, stop=True).then_inc(S["rope_rotated"], 1)
                    else:
                        pe.wait_ge(bank_free[st.heads.bank(n - 1)], st.heads.use(n - 1) + 1)
                        pe.matmul(ps[st.bank(n)][0:MLA_QK, :], ROT[0:MLA_QK, :], QA[0:MLA_QK, n - 1, :],
                                  start=True, stop=True).then_inc(S["rope_rotated"], 1)

            def attention(st):
                mode = st.mode
                items = [(h, c, t) for h in range(st.heads) for c in range(st.comps) for t in range(ST)]
                pt = PT if mode in ("gqa", "mla") else PT2

                def operands(h, c, t):
                    a, b = spans(mode, t)
                    at, ks = slice(t * P, (t + 1) * P), slice(a * P, b * P)
                    if mode == "gqa":
                        kv = h // (GQA_H // 2)
                        return QC[half(h), h // 2, at], K2[half(h), (kv + h) % 2, ks]
                    if mode == "mla":
                        return QA[0:MLA_QK, h, at], KA[0:MLA_QK, h, ks]
                    if mode == "dilated":
                        return HQ[half(h), h // 2, at], HQ[half(h), 4 + h // 2, ks]
                    return HQ[half(c), 8 + h, at], HQ[half(c), 12 + h, ks]

                def values(h, kt):
                    if mode == "gqa":
                        kv = h // (GQA_H // 2)
                        return VR[:, kt, kv * HD:(kv + 1) * HD]
                    if mode == "mla":
                        return VA[:, kt, h * MLA_V:(h + 1) * MLA_V]
                    if mode == "dilated":
                        return QKV[:, kt, DM + h * HD:DM + (h + 1) * HD]
                    return QKV[:, kt, 5 * SEQ + h * P:5 * SEQ + (h + 1) * P]

                pe.wait_ge(S["factor_rows_ready"], st.at("factor_rows_ready", 0))
                if mode == "gqa":
                    pe.wait_ge(bank_free[st.proj.bank(11)], st.proj.use(11) + 1)
                    pe.wait_ge(bank_free[st.proj.bank(7)], st.proj.use(7) + 1)
                    pe.wait_ge(S["keys_copied"], st.proj.at("keys_copied", 2))
                if mode == "mla":
                    pe.wait_ge(S["rope_added"], st.rope.at("rope_added", 9))
                    pe.wait_ge(S["rope_keys_spread"], st.rope.at("rope_keys_spread", 1))
                for i in range(len(items) + 3):
                    if i < len(items):
                        h, c, t = items[i]
                        free = "exp_ready" if mode == "mla" else "scores_read"
                        if i >= 2:
                            pe.wait_ge(S[free], st.at(free, i - 1))
                        else:
                            if st.at("exp_ready", 0) > 0:
                                pe.wait_ge(S["exp_ready"], st.at("exp_ready", 0))
                        if mode == "dilated":
                            pe.wait_ge(bank_free[st.qk.bank(h // 2)], st.qk.use(h // 2) + 1)
                            pe.wait_ge(bank_free[st.qk.bank(4 + h // 2)], st.qk.use(4 + h // 2) + 1)
                        if mode == "diff":
                            pe.wait_ge(bank_free[st.qk.bank(8 + h)], st.qk.use(8 + h) + 1)
                            pe.wait_ge(bank_free[st.qk.bank(12 + h)], st.qk.use(12 + h) + 1)
                        q, k = operands(h, c, t)
                        a, b = spans(mode, t)
                        pe.matmul(score_ps[i % 2][:, 0:(b - a) * P], q, k, start=True, stop=True).then_inc(S["scores_ready"], 1)
                    if 2 <= i < len(items) + 2:
                        n = i - 2
                        h, c, t = items[n]
                        a, b = spans(mode, t)
                        pe.wait_ge(S["probs_ready"], st.at("probs_ready", n + 1))
                        if st.at("turned_copied", max(0, n - 1)) > 0:
                            pe.wait_ge(S["turned_copied"], st.at("turned_copied", max(0, n - 1)))
                        for k in range(b - a):
                            mm = pe.transpose(turn_ps[n % 2][:, k * P:(k + 1) * P], SG[:, n % 4, k * P:(k + 1) * P], IDENT[:, :])
                        mm.then_inc(S["probs_turned"], 1)
                    if i >= 3 and (i - 3) % ST == ST - 1:
                        n = i - 3
                        h, c, _t = items[n]
                        pe.wait_ge(S["turned_copied"], st.at("turned_copied", n + 1))
                        if c == 0:
                            pe.wait_ge(bank_free[st.bank(h)], st.use(h))
                        rows = P if mode == "diff" else HD
                        for kt in range(ST):
                            a, b = queries(mode, kt)
                            mm = pe.matmul(ps[st.bank(h)][0:rows, a * P:b * P], values(h, kt),
                                           pt[:, (n // ST) % 2, kt, a * P:b * P], start=kt == 0 and c == 0,
                                           stop=kt == ST - 1 and c == st.comps - 1, skip_group_check=True)
                        mm.then_inc(S["head_multiplied"], 1)

            def out_y(st):
                n = st.units // 4
                def body(r):
                    for j in range(st.units):
                        k0 = (j % n) * BLOCKS
                        tile(st, j, j // n, r, pair[st.src], min(BLOCKS, st.kt - k0), k0,
                             st.op if isinstance(r, int) and r == 0 and j < n else None, j % n == 0, j % n == n - 1)
                repeat(pe, st, body, 1)

            def loop_h(st):
                def body(r):
                    first = isinstance(r, int) and r == 0
                    for j in range(4):
                        tile(st, j, j, r, pair["H"], DT, ready=st.op if first and j == 0 and st.norm is not None else None)
                        if first and j == 0 and st.norm is not None:
                            norm(st.norm)
                repeat(pe, st, body, 1)

            def qkv(st):
                def body(r):
                    first = isinstance(r, int) and r == 0
                    for m in range(2):
                        weights(st.unit(2 * m + 1, r))
                        s0 = st.unit(2 * m) % SLOTS
                        for s in range(ST):
                            k = 2 * m + s // 2
                            if s % 2 == 0:
                                pe.wait_ge(bank_free[st.bank(k)], st.use(k, r))
                            o = ps[st.bank(k)][:, (s % 2) * 2 * P:(s % 2 + 1) * 2 * P].rearrange("p (a c) -> p a c", a=2)
                            for t in range(DT):
                                if first and m == 0 and s == 0:
                                    pe.wait_ge(S["operand_ready"], st.op + t + 1)
                                at = slice(s * P, (s + 1) * P)
                                whi, wlo = (w[:, s0:s0 + 2, t * P:(t + 1) * P] for w in (WHI, WLO))
                                pe.matmul(o, HH[:, t, at], whi, start=t == 0, stop=False)
                                pe.matmul(o, HH[:, t, at], wlo, start=False, stop=False)
                                mm = pe.matmul(o, HL[:, t, at], whi, start=False, stop=t == DT - 1)
                            if s == 1:
                                mm.then_inc(S["part_multiplied"], 1)
                        mm.then_inc(unit_used, 2)
                        if first and m == 0:
                            norm(st.norm)
                repeat(pe, st, body, 1)

            def qk_norm(st):
                for f in range(16):
                    pe.wait_ge(bank_free[st.bank(f)], st.use(f))
                    pe.wait_ge(S["qk_normed"], st.at("qk_normed", (f // 4) * 4 + 4))
                    c0 = (f // 4) * SEQ + (SEQ if f >= 8 else 0) + (f % 4) * P
                    for s in range(ST):
                        mm = pe.transpose(ps[st.bank(f)][:, s * P:(s + 1) * P], QKV[:, s, c0:c0 + P], IDENT[:, :])
                    mm.then_inc(S["qk_turned"], 1)

            def sub_norm(st):
                pe.wait_ge(S["out_square_ready"], st.at("out_square_ready", 4))
                pe.wait_ge(S["turned_copied"], st.at("turned_copied", 0))
                for h in range(DIFF_H):
                    for s in range(ST):
                        mm = pe.matmul(stat_ps[:, h * ST + s:h * ST + s + 1], PT2[:, 0, h, s * P:(s + 1) * P], ONES[:, 0:1],
                                       start=True, stop=True)
                mm.then_inc(S["out_squares_summed"], 1)
                pe.wait_ge(S["out_factors_ready"], st.at("out_factors_ready", 1))
                for h in range(DIFF_H):
                    pe.wait_ge(bank_free[st.bank(h)], st.use(h))
                    for s in range(ST):
                        mm = pe.transpose(ps[st.bank(h)][:, s * P:(s + 1) * P],
                                          RC["Y"][:, h * ST + s:h * ST + s + 1].to_broadcast([P, P]), IDENT[:, :])
                    mm.then_inc(S["out_factors_spread"], 1)

            def ple_in(st):
                pe.wait_ge(S["ple_loaded"], st.at("ple_loaded", 16))
                for t in range(2):
                    if st.use(t) > 0:
                        pe.wait_ge(bank_free[st.bank(t)], st.use(t))
                    for s in range(ST):
                        mm = pe.transpose(ps[st.bank(t)][:, s * P:(s + 1) * P], PROWS[:, s, t * P:(t + 1) * P], IDENT[:, :])
                    mm.then_inc(S["ple_turned"], 1)

            def ple(st):
                def body(r):
                    first = isinstance(r, int) and r == 0
                    for j in range(4):
                        if j % 2 == 0:
                            tile(st, j, j, r, (POH, POL), 2, ready=st.op if first else None)
                        else:
                            tile(st, j, j, r, pair["H"], DT, ready=st.op + 2 if first else None)
                repeat(pe, st, body, 1)

            def rec_lru(st):
                k = 0
                for j in range(2):
                    weights(st.unit(j))
                    s = st.unit(j) % SLOTS
                    for n in range(DT):
                        pe.wait_ge(bank_free[st.bank(k)], st.use(k))
                        if j == 0:
                            pe.wait_ge(S["operand_ready"], st.op + n + 1)
                        three(ps[st.bank(k)][:, :], None, (slice(None), s, slice(n * P, (n + 1) * P)), XRH[:, n, :], XRL[:, n, :],
                              True, True).then_inc(S["part_multiplied"] if n < DT - 1 else unit_used, 1)
                        k += 1

            def out(st):
                for k in range(DT):
                    s, hf = k // 2, k % 2
                    pe.wait_ge(bank_free[st.bank(k)], st.use(k))
                    if k == 0:
                        for b in range(BANKS):
                            pe.wait_ge(bank_free[st.bank(b)], st.use(b))
                    for c in range(4):
                        mm = pe.transpose(ps[st.bank(k)][:, c * P:(c + 1) * P], X[:, hf * 4 + c, s * P:(s + 1) * P], IDENT[:, :])
                    mm.then_inc(S["rows_turned"], 1)

            does = dict(init=init, fourier=fourier, branch=branch, proj=proj, mla_heads=mla_heads, rope=rope,
                        attention=attention, out_y=out_y, residual=out_y, swiglu=loop_h, conv_ffn=loop_h, rec_gate=loop_h,
                        rec_conv=loop_h, qkv=qkv, qk_norm=qk_norm, sub_norm=sub_norm, ple_in=ple_in, ple=ple,
                        rec_lru=rec_lru, out=out)
            for st in STEPS:
                if st.kind == "norm" and st.where == "now":
                    norm(st)
                elif st.kind in does:
                    does[st.kind](st)

        @block.scalar
        def _(act):
            def split_of(st, j, r=0):
                n = st.unit(j) + AHEAD
                s = n % SLOTS
                if isinstance(r, int) and n + r * st.units >= NU:
                    return
                act.wait_ge(raw[s], 16 * (n // SLOTS + 1) + r * (16 * (st.units // SLOTS)) if st.units % SLOTS == 0
                            else 16 * (n // SLOTS + 1))
                act.activation(WHI[:, s, :], WRAW[:, s, :], ACT.Copy).then_inc(wt_hi, 1)

            def square(st, src, i, r=0, done="square_ready", slot=None):
                if st.at("square_added", i - 1) > 0:
                    act.wait_ge(S["square_added"], st.at("square_added", i - 1, r))
                act.activation(SQ[:, i % 2 if slot is None else slot, :], src, ACT.Square)\
                   .then_inc(S[done] if isinstance(done, str) else done, 1)

            def init(st):
                for dst, src in ((XROWS[:, :, :], xin.rearrange("o (s p) d -> p (o s) d", p=P)),
                                 (CONST[:, :], consts), (COLS[:, :], cols),
                                 (POSI[:, :], posi.broadcast_to([P, SEQ])), (POSC_I[:, :], posc), (GM[:, :], gmask),
                                 (TDRAW[:, 0, :], dftc[0]), (TDRAW[:, 1, :], dftc[1])):
                    act.dma_start(dst, src).then_inc(ld, 16)
                for u in range(AHEAD):
                    act.wait_ge(raw[u], 16)
                    act.activation(WHI[:, u, :], WRAW[:, u, :], ACT.Copy).then_inc(wt_hi, 1)
                act.wait_ge(ld, 16 * 8)
                act.activation(TDH[:, :, :], TDRAW[:, :, :], ACT.Copy).then_inc(S["dft_hi_ready"], 1)
                act.wait_ge(S["table_stepped"], st.at("table_stepped", 3))
                for t in range(ST):
                    a, b = spans("gqa", t)
                    act.activation(GD[:, t, 0:(b - a) * P], POSF[:, a * P:b * P], ACT.Abs, bias=POSC[:, t:t + 1]).then_inc(S["table_looked_up"], 1)
                act.wait_ge(S["table_stepped"], st.at("table_stepped", 11))
                act.activation(SIN[:, :], ANG[:, :], ACT.Sin).then_inc(S["table_looked_up"], 1)
                act.activation(TURN[:, :], ANG[:, :], ACT.Abs).then_inc(S["table_looked_up"], 1)
                act.wait_ge(S["table_stepped"], st.at("table_stepped", 12))
                act.activation(COS[:, :], TURN[:, :], ACT.Sin).then_inc(S["table_looked_up"], 1)

            def operand(st):
                src, (hi, lo) = source[st.src], pair[st.dst]
                if st.made is not None and st.made.kind == "init":
                    for b in range(BANKS):
                        act.wait_ge(bank_free[b], DT // BANKS)
                if st.made is not None and st.made.kind == "proj":
                    for k in range(4):
                        act.wait_ge(bank_free[st.made.bank(k)], st.made.use(k) + 1)
                for i in range(st.n):
                    t = st.t + i
                    if st.y:
                        act.wait_ge(S["residual_updated"], st.at("residual_updated", i + 1))
                    scale = dict(scale=col(st.gain, i)) if st.gain else {}
                    act.activation(hi[:, t, :], src[:, t, :], ACT.Copy, **scale).then_inc(S["operand_hi_ready"], 1)
                    if st.stat:
                        square(st, src[:, t, :], i)

            def norm(st):
                act.wait_ge(S["factors_spread"], st.at("factors_spread", 1))
                act.activation(RB[st.rb][:, :], stat_ps[:, :], ACT.Copy).then_inc(S["factor_rows_ready"], 1)

            def fourier(st):
                for part in range(2):
                    act.dma_start(DFT[:, part, :, :], dft[part].rearrange("(s p) n -> p s n", p=P)).then_inc(S["dft_loaded"], 16)
                n_cols = 0
                for what, g in FOURIER_ORDER:
                    if what == "rows":
                        if g >= 2:
                            act.wait_ge(S["tokens_transformed"], st.at("tokens_transformed", 2 * (g - 1)))
                        for s in range(ST):
                            k = fourier_tile("rows", g, s)
                            act.wait_ge(S["channels_transformed"], st.at("channels_transformed", g * ST + s + 1))
                            act.activation(PG[:, g % 2, s, :], ps[st.bank(k)][:, :], ACT.Copy, scale=RC["X"][:, s:s + 1])\
                               .then_inc(bank_free[st.bank(k)], 1)
                    elif what == "cols":
                        for c in range(2):
                            k = fourier_tile("cols", g, c)
                            act.wait_ge(S["tokens_transformed"], st.at("tokens_transformed", n_cols + 1))
                            act.wait_ge(S["operand_ready"], st.at("operand_ready", n_cols - 1))
                            act.activation(TM[:, c, :], ps[st.bank(k)][:, :], ACT.Copy).then_inc(bank_free[st.bank(k)], 1)
                            act.wait_ge(bank_free[st.bank(k)], st.use(k) + 1)
                            act.activation(OBH[:, n_cols, :], TM[:, c, :], ACT.Copy).then_inc(S["operand_hi_ready"], 1)
                            n_cols += 1

            def branch(st):
                def body(r):
                    for j in range(4):
                        if j % 2 == 0:
                            act.wait_ge(bank_free[st.bank(j)], st.use(j, r) + 1)
                            act.activation(SG[:, j // 2, :], SG[:, j // 2, :], ACT.Sigmoid).then_inc(S["gate_ready"], 1)
                        elif st.last:
                            act.wait_ge(S["product_ready"], st.at("product_ready", 1 + j // 2, r))
                            act.activation(tile_of(r * 2 + j // 2, MGH), tile_of(r * 2 + j // 2, MG), ACT.Copy)\
                               .then_inc(S["operand_hi_ready"], 1)
                        split_of(st, j, r)
                repeat(act, st, body)

            def proj(st):
                for j in range(11):
                    act.wait_ge(unit_used, st.unit(j))
                    split_of(st, j)
                act.wait_ge(S["values_turned"], st.at("values_turned", 1))
                act.activation(VR[:, :, :], ps[st.bank(11)][:, :].rearrange("p (a c) -> p a c", a=ST), ACT.Copy)\
                   .then_inc(bank_free[st.bank(11)], 1)

            def mla_heads(st):
                for j in range(4):
                    act.wait_ge(unit_used, st.unit(j))
                    split_of(st, j)
                act.wait_ge(unit_used, st.unit(4))
                split_of(st, 4)
                for t in range(ST):
                    k = 2 * 4 + MLA_H + t
                    if t < ST - 1:
                        act.wait_ge(S["part_multiplied"], st.at("part_multiplied", 4 + MLA_H + t + 1))
                    else:
                        act.wait_ge(unit_used, st.unit(4) + 1)
                    act.activation(VA[:, t, :], ps[st.bank(k)][:, :], ACT.Copy, scale=RC["K"][:, t:t + 1])\
                       .then_inc(bank_free[st.bank(k)], 1)

            def rope(st):
                act.wait_ge(S["rope_added"], st.at("rope_added", 1))
                src = KRAW[MLA_NOPE:MLA_QK, :].rearrange("p (o s) -> p o s", o=1).to_broadcast([MLA_ROPE, MLA_H, SEQ])
                act.activation(KA[MLA_NOPE:MLA_QK, :, :], src, ACT.Copy).then_inc(S["rope_keys_spread"], 1)

            def attention(st):
                mode = st.mode
                pt = PT if mode in ("gqa", "mla") else PT2
                items = [(h, c, t) for h in range(st.heads) for c in range(st.comps) for t in range(ST)]
                hi = pair[st.out][0] if mode != "diff" else None
                for i in range(len(items) + 2):
                    if i < len(items):
                        h, c, t = items[i]
                        a, b = spans(mode, t)
                        w = (b - a) * P
                        s = i % 4
                        act.wait_ge(S["neg_max_ready"], st.at("neg_max_ready", i + 1))
                        if mode == "mla":
                            if i >= 4:
                                act.wait_ge(S["probs_turned"], st.at("probs_turned", i - 3))
                            act.activation(SG[:, s, 0:w], score_ps[i % 2][:, 0:w], ACT.Exp, bias=NM[:, s:s + 1],
                                           scale=MLA_QK ** -0.5, accum_out=SM[:, s:s + 1]).then_inc(S["exp_ready"], 1)
                        else:
                            act.activation(SG[:, s, 0:w], SG[:, s, 0:w], ACT.Exp, bias=NM[:, s:s + 1],
                                           accum_out=SM[:, s:s + 1]).then_inc(S["exp_ready"], 1)
                        if mode == "gqa":
                            act.activation(ES[:, s:s + 1], col(f"gqa_sink{st.l}", h), ACT.Exp, bias=NM[:, s:s + 1]).then_inc(S["sink_exp_ready"], 1)
                    if i >= 2:
                        n = i - 2
                        h, c, t = items[n]
                        a, b = spans(mode, t)
                        g = n // ST
                        act.wait_ge(S["probs_turned"], st.at("probs_turned", n + 1))
                        if g >= 2:
                            act.wait_ge(S["head_multiplied"], st.at("head_multiplied", g - 1))
                        act.activation(pt[:, g % 2, a:b, t * P:(t + 1) * P],
                                       turn_ps[n % 2][:, 0:(b - a) * P].rearrange("p (a c) -> p a c", a=b - a), ACT.Copy)\
                           .then_inc(S["turned_copied"], 1)
                    if mode != "diff":
                        for p in range(st.heads // 2):
                            if i == min((2 * p + 2) * ST + 5, len(items) + 1):
                                act.wait_ge(bank_free[st.bank(2 * p)], st.use(2 * p) + 1)
                                act.wait_ge(bank_free[st.bank(2 * p + 1)], st.use(2 * p + 1) + 1)
                                act.activation(hi[:, p, :], TM[:, p % 2, :], ACT.Copy).then_inc(S["operand_hi_ready"], 1)

            def out_y(st):
                n = st.units // 4
                def body(r):
                    for j in range(st.units):
                        k = j // n
                        act.wait_ge(unit_used, st.unit(j if j % n == n - 1 else j - 1, r) + 1)
                        if j % n == n - 1:
                            act.wait_ge(S["square_added"], st.at("square_added", k - 1, r))
                            act.activation(tile_of(r * 4 + k, source[st.y]), ps[st.bank(k)][:, :], ACT.Copy)
                            act.activation(SQ[:, k % 2, :], ps[st.bank(k)][:, :], ACT.Square).then_inc(bank_free[st.bank(k)], 1)
                        split_of(st, j, r)
                repeat(act, st, body)

            def residual(st):
                n = st.units // 4
                def body(r):
                    for j in range(st.units):
                        k = j // n
                        if j % n == n - 1 and st.gain:
                            act.wait_ge(bank_free[st.bank(k)], st.use(k, r) + 1)
                            act.wait_ge(S["square_added"], st.at("square_added", k - 1, r))
                            t = r * 4 + k
                            act.activation(tile_of(t, HH), tile_of(t, X), ACT.Copy, scale=col(st.gain, t)).then_inc(S["operand_hi_ready"], 1)
                            act.activation(SQ[:, k % 2, :], tile_of(t, X), ACT.Square).then_inc(S["square_ready"], 1)
                        else:
                            act.wait_ge(unit_used, st.unit(j, r))
                        split_of(st, j, r)
                repeat(act, st, body, 0 if st.u0 + st.reps * st.units + AHEAD < NU else st.reps)

            def swiglu(st):
                def body(r):
                    for j in range(4):
                        if j % 2 == 0:
                            act.wait_ge(bank_free[st.bank(j)], st.use(j, r) + 1)
                            act.activation(SG[:, j // 2, :], SG[:, j // 2, :], ACT.Silu).then_inc(S["gate_ready"], 1)
                        else:
                            act.wait_ge(S["product_ready"], st.at("product_ready", 1 + j // 2, r))
                            act.activation(tile_of(r * 2 + j // 2, F1H), TM[:, j // 2, :], ACT.Copy).then_inc(S["operand_hi_ready"], 1)
                        split_of(st, j, r)
                repeat(act, st, body)

            def ple_in(st):
                act.dma_start(PROWS[:, :, :], pin[st.l].rearrange("o (s p) d -> p (o s) d", p=P)).then_inc(S["ple_loaded"], 16)
                for t in range(2):
                    act.wait_ge(S["ple_turned"], st.at("ple_turned", t + 1))
                    act.activation(TM[:, t, :], ps[st.bank(t)][:, :], ACT.Copy).then_inc(bank_free[st.bank(t)], 1)
                    act.wait_ge(bank_free[st.bank(t)], st.use(t) + 1)
                    act.activation(POH[:, t, :], TM[:, t, :], ACT.Copy).then_inc(S["operand_hi_ready"], 1)

            def ple(st):
                def body(r):
                    for j in range(4):
                        k = j // 2
                        act.wait_ge(unit_used, st.unit(j, r) + 1)
                        if j % 2 == 0:
                            act.wait_ge(S["product_ready"], st.at("product_ready", k - 1, r))
                        act.activation(SG[:, j, :], ps[st.bank(j)][:, :], ACT.Sigmoid if j % 2 else ACT.Copy)\
                           .then_inc(bank_free[st.bank(j)], 1)
                        if j % 2:
                            act.wait_ge(S["product_ready"], st.at("product_ready", k + 1, r))
                            square(st, tile_of(r * 2 + k, YP), k, r)
                        split_of(st, j, r)
                repeat(act, st, body)

            def tables2(st):
                act.dma_start(DIL[:, :, :], dil).then_inc(S["tables_loaded"], 16)
                act.dma_start(LAMV[:, :, :], lamv.broadcast_to([P, 4 * HD]).rearrange("p (a c) -> p a c", a=4)).then_inc(S["tables_loaded"], 16)
                act.wait_ge(S["tables_stepped"], st.at("tables_stepped", 2))
                act.activation(LE[:, :], LT[:, :], ACT.Exp).then_inc(S["lambda_exp_ready"], 1)

            def qkv(st):
                def body(r):
                    for m in range(2):
                        for s in range(ST):
                            k = 2 * m + s // 2
                            if s == 0:
                                act.wait_ge(S["part_multiplied"], st.at("part_multiplied", m + 1, r))
                            if s == 2:
                                act.wait_ge(unit_used, st.unit(2 * m + 1, r) + 1)
                            c = (r * 2 + m) * 2 * P
                            dst = QKV[:, s, c:c + 2 * P] if isinstance(c, int) else QKV[:, s, bass.ds(c, 2 * P)]
                            a = act.activation(dst, ps[st.bank(k)][:, (s % 2) * 2 * P:(s % 2 + 1) * 2 * P], ACT.Copy,
                                               scale=RC["X"][:, s:s + 1])
                            if s % 2:
                                a.then_inc(bank_free[st.bank(k)], 1)
                        split_of(st, 2 * m, r)
                        split_of(st, 2 * m + 1, r)
                repeat(act, st, body)

            def qk_norm(st):
                for k in range(BANKS):
                    act.wait_ge(bank_free[k], st.t0 // BANKS)
                for n in range(16):
                    c, s = n // 4, n % 4
                    c0 = c * SEQ + (SEQ if c >= 2 else 0)
                    if n >= 2:
                        act.wait_ge(S["qk_square_summed"], st.at("qk_square_summed", n - 1))
                    act.activation(SQ[:, n % 2, :], QKV[:, s, c0:c0 + SEQ], ACT.Square).then_inc(S["qk_square_ready"], 1)
                act.wait_ge(S["qk_factors_stepped"], st.at("qk_factors_stepped", 1))
                act.activation(VQ[:, :], VQ[:, :], ACT.Sqrt).then_inc(S["qk_factors_stepped"], 1)
                for f in range(16):
                    act.wait_ge(S["qk_turned"], st.at("qk_turned", f + 1))
                    g = (GQ[:, 0:1], col("a_k_norm_20"), GQ[:, 1:2], col("b_k_norm_20"))[f // 4]
                    act.activation(HQ[:, f, :], ps[st.bank(f)][:, :], ACT.Copy, scale=g).then_inc(bank_free[st.bank(f)], 1)

            def sub_norm(st):
                for h in range(DIFF_H):
                    act.wait_ge(bank_free[st.att.bank(h)], st.att.use(h) + 1)
                    act.activation(PT2[:, 0, h, :], UB[:, h, :], ACT.Square).then_inc(S["out_square_ready"], 1)
                for h in range(DIFF_H):
                    act.wait_ge(bank_free[st.bank(h)], st.use(h) + 1)
                    act.activation(O2H[:, 4 + h, :], UB[:, h, :], ACT.Copy).then_inc(S["operand_hi_ready"], 1)

            def conv_tail(st, k, r, w, bias, taps):
                act.wait_ge(bank_free[st.bank(k)], st.use(k, r) + 1)
                act.activation(SG[:, k, :], U[:, k, taps - 1:taps - 1 + SEQ], ACT.Identity, scale=w, bias=bias).then_inc(S["conv_begun"], 1)

            def conv_ffn(st):
                def body(r):
                    for j in range(4):
                        t = r * 2 + j // 2 + (FT2 if j % 2 else 0)
                        conv_tail(st, j, r, col(f"ffn_conv_w_2{st.l}_2", t), col(f"ffn_conv_b_2{st.l}", t), 3)
                        if j % 2 == 0:
                            act.wait_ge(S["conv_tap_added"], st.at("conv_tap_added", 2 * j + 2, r))
                            act.activation(SG[:, j, :], SG[:, j, :], ACT.Gelu_apprx_tanh).then_inc(S["gate_ready"], 1)
                        else:
                            act.wait_ge(S["product_ready"], st.at("product_ready", 1 + j // 2, r))
                            act.activation(tile_of(r * 2 + j // 2, F2H), SG[:, j, :], ACT.Copy).then_inc(S["operand_hi_ready"], 1)
                        split_of(st, j, r)
                repeat(act, st, body)

            def rec_gate(st):
                def body(r):
                    for j in range(4):
                        act.wait_ge(bank_free[st.bank(j)], st.use(j, r) + 1)
                        g = tile_of(r * 4 + j, GG)
                        act.activation(g, g, ACT.Gelu_apprx_tanh).then_inc(S["gate_ready"], 1)
                        split_of(st, j, r)
                repeat(act, st, body)

            def rec_conv(st):
                def body(r):
                    for j in range(4):
                        t = r * 4 + j
                        conv_tail(st, j, r, col("rec_conv_w_20_3", t), col("rec_conv_b_20", t), 4)
                        act.wait_ge(S["conv_tap_added"], st.at("conv_tap_added", 3 * j + 3, r))
                        act.activation(tile_of(t, XRH), tile_of(t, XR), ACT.Copy).then_inc(S["operand_hi_ready"], 1)
                        split_of(st, j, r)
                repeat(act, st, body)

            def rec_lru(st):
                A = HQ
                act.wait_ge(S["decay_abs_ready"], st.at("decay_abs_ready", 1))
                act.activation(LR[:, 1, :], LR[:, 0, :], ACT.Exp, scale=-1.0).then_inc(S["decay_exp_ready"], 1)
                for j in range(2):
                    dst, bias = ((RT, "rec_gate_a_b_20"), (IT, "rec_gate_x_b_20"))[j]
                    for n in range(DT):
                        k = j * DT + n
                        if n < DT - 1:
                            act.wait_ge(S["part_multiplied"], st.at("part_multiplied", j * (DT - 1) + n + 1))
                        else:
                            act.wait_ge(unit_used, st.unit(j) + 1)
                        act.activation(dst[:, n, :], ps[st.bank(k)][:, :], ACT.Sigmoid, bias=col(bias, n))\
                           .then_inc(bank_free[st.bank(k)], 1)
                    split_of(st, j)
                act.wait_ge(S["decay_stepped"], st.at("decay_stepped", LP_STEPS))
                for n in range(DT):
                    if n == 0:
                        act.wait_ge(bank_free[st.bank(15)], st.use(15) + 1)
                    act.activation(A[:, n, :], RT[:, n, :], ACT.Exp, scale=LR[:, 3, n:n + 1]).then_inc(S["decay_ready"], 1)
                    act.activation(RT[:, n, :], RT[:, n, :], ACT.Tanh, scale=LR[:, 3, n:n + 1]).then_inc(S["tanh_ready"], 1)
                    if n >= 2:
                        act.wait_ge(S["decay_rest_ready"], st.at("decay_rest_ready", n - 1))
                    act.wait_ge(S["decay_ready"], st.at("decay_ready", n + 1))
                    act.activation(SQ[:, n % 2, :], A[:, n, :], ACT.Square).then_inc(S["decay_squared"], 1)
                for n in range(DT):
                    act.wait_ge(S["decay_rest_ready"], st.at("decay_rest_ready", n + 1))
                    act.activation(RT[:, n, :], RT[:, n, :], ACT.Sqrt, scale=-1.0).then_inc(S["root_ready"], 1)
                for n in range(DT):
                    act.wait_ge(S["product_ready"], st.at("product_ready", n + 1))
                    act.activation(ROH[:, n, :], GG[:, n, :], ACT.Copy).then_inc(S["operand_hi_ready"], 1)

            def out(st):
                for k in range(DT):
                    s, hf = k // 2, k % 2
                    act.wait_ge(S["rows_turned"], st.at("rows_turned", k + 1))
                    act.activation(YROWS[:, s, hf * SEQ:(hf + 1) * SEQ], ps[st.bank(k)][:, :], ACT.Copy)\
                       .then_inc(bank_free[st.bank(k)], 1)
                    if hf:
                        act.wait_ge(bank_free[st.bank(k - 1)], st.use(k - 1) + 1)
                        act.wait_ge(bank_free[st.bank(k)], st.use(k) + 1)
                        act.dma_start(out_v[s], YROWS[:, s, :]).then_inc(S["output_stored"], 16)
                act.wait_ge(S["output_stored"], 16 * ST)

            out_v = out_.rearrange("o (s p) d -> (o s) p d", p=P)
            does = dict(init=init, operand=operand, norm=norm, fourier=fourier, branch=branch, proj=proj, mla_heads=mla_heads,
                        rope=rope, attention=attention, out_y=out_y, residual=residual, swiglu=swiglu, ple_in=ple_in,
                        ple=ple, tables2=tables2, qkv=qkv, qk_norm=qk_norm, sub_norm=sub_norm, conv_ffn=conv_ffn,
                        rec_gate=rec_gate, rec_conv=rec_conv, rec_lru=rec_lru, out=out)
            for st in STEPS:
                if st.kind in does:
                    does[st.kind](st)

        @block.vector
        def _(dve):
            def init(st):
                dve.memset(ONES[:, :], 1.0).then_inc(cst, 1)
                dve.memset(NEGH[:, :], -0.5).then_inc(cst, 1)
                dve.memset(MX[:, :], 0.0).then_inc(cst, 1)
                dve.wait_ge(ld, 16 * 8)
                for t in range(DT):
                    dve.wait_ge(S["rows_turned"], st.at("rows_turned", t + 1))
                    dve.tensor_copy(X[:, t, :], ps[st.bank(t)][:, :]).then_inc(bank_free[st.bank(t)], 1)
                dve.wait_ge(S["dft_hi_ready"], st.at("dft_hi_ready", 1))
                dve.tensor_tensor(TDL[:, :, :], TDRAW[:, :, :], TDH[:, :, :].bitcast(F32), ALU.subtract).then_inc(S["dft_lo_ready"], 1)
                n = 0

                def step(ins):
                    nonlocal n
                    ins.then_inc(S["table_stepped"], 1)
                    n += 1
                    dve.wait_ge(S["table_stepped"], st.at("table_stepped", n))
                step(dve.tensor_copy(POSF[:, :], POSI[:, :]))
                step(dve.tensor_copy(POSC[:, :], POSC_I[:, :]))
                step(dve.tensor_scalar(POSC[:, :], POSC[:, :], -1.0, None, ALU.mult))
                magic = 1.5 * 2.0 ** 23
                c1 = 6.28125
                c2 = float(np.float32(int((2 * np.pi - c1) * 2 ** 20)) / np.float32(2 ** 20))
                c3 = float(np.float32(2 * np.pi - c1 - c2))
                step(dve.tensor_scalar(ANG[:, :], POSF[:, :], INVF[:, 0:1], None, ALU.mult))
                step(dve.tensor_scalar(TURN[:, :], ANG[:, :], float(np.float32(1 / (2 * np.pi))), None, ALU.mult))
                step(dve.tensor_scalar(TURN[:, :], TURN[:, :], magic, None, ALU.add))
                step(dve.tensor_scalar(TURN[:, :], TURN[:, :], magic, None, ALU.subtract))
                for c in (c1, c2, c3):
                    step(dve.scalar_tensor_tensor(ANG[:, :], TURN[:, :], -c, ANG[:, :], ALU.mult, ALU.add))
                step(dve.tensor_scalar(ANG[:, :], ANG[:, :], 3.1415925, -3.1415925, ALU.min, ALU.max))
                dve.wait_ge(S["table_looked_up"], st.at("table_looked_up", ST + 2))
                step(dve.tensor_scalar(TURN[:, :], TURN[:, :], -1.0, float(np.float32(np.pi / 2)), ALU.mult, ALU.add))
                dve.wait_ge(S["table_looked_up"], st.at("table_looked_up", ST + 3))
                for t in range(ST):
                    a, b = spans("gqa", t)
                    at = (a - t + 1) * P
                    step(dve.tensor_tensor(GD[:, t, 0:(b - a) * P], GD[:, t, 0:(b - a) * P], GM[:, at:at + (b - a) * P], ALU.add))

            def operand(st):
                src, (hi, lo) = source[st.src], pair[st.dst]
                if st.y:
                    dve.wait_ge(S["factor_rows_ready"], st.at("factor_rows_ready", 0))
                    dve.wait_ge(S["operand_ready"], st.at("operand_ready", 0))
                for i in range(st.n + 1):
                    if st.y and i < st.n:
                        dve.scalar_tensor_tensor(TM[:, i % 2, :], source[st.y][:, i, :], col(st.gy, i), RBY[:, :], ALU.mult,
                                                 ALU.mult).then_inc(S["update_ready"], 1)
                        dve.wait_ge(S["update_ready"], st.at("update_ready", i + 1))
                        dve.tensor_tensor(X[:, i, :], X[:, i, :], TM[:, i % 2, :], ALU.add).then_inc(S["residual_updated"], 1)
                    if i:
                        t = st.t + i - 1
                        dve.wait_ge(S["operand_hi_ready"], st.at("operand_hi_ready", i))
                        h = hi[:, t, :].bitcast(F32)
                        if st.gain:
                            dve.scalar_tensor_tensor(lo[:, t, :], src[:, t, :], col(st.gain, i - 1), h, ALU.mult, ALU.subtract)\
                               .then_inc(S["operand_ready"], 1)
                        else:
                            dve.tensor_tensor(lo[:, t, :], src[:, t, :], h, ALU.subtract).then_inc(S["operand_ready"], 1)

            def norm(st):
                n = DIFF_H * ST if st.kind == "sub_norm" else ST
                dve.wait_ge(S["norm_summed"], st.at("norm_summed", 1))
                if st.at("factor_rows_ready", 0) > 0:
                    dve.wait_ge(S["factor_rows_ready"], st.at("factor_rows_ready", 0))
                dve.tensor_scalar(VAR[:, 0:ST], stat_ps[:, 0:ST], 1.0 / st.width, EPS, ALU.mult, ALU.add).then_inc(S["mean_square_ready"], 1)

            def zero(st):
                dve.memset(ACC[:, :], 0.0).then_inc(S["sum_cleared"], 1)

            def add_square(st, k, r, slot):
                dve.wait_ge(S["square_added"], st.at("square_added", k, r))
                dve.wait_ge(S["sum_cleared"], st.at("sum_cleared", 0))
                dve.tensor_tensor(ACC[:, :], ACC[:, :], SQ[:, slot, :], ALU.add).then_inc(S["square_added"], 1)

            def remainder(st, dst, src, k, r, gain=None):
                hi, lo = dst
                dve.wait_ge(S["operand_hi_ready"], st.at("operand_hi_ready", k, r))
                if gain is None:
                    dve.tensor_tensor(lo, src, hi.bitcast(F32), ALU.subtract).then_inc(S["operand_ready"], 1)
                else:
                    dve.scalar_tensor_tensor(lo, src, gain, hi.bitcast(F32), ALU.mult, ALU.subtract).then_inc(S["operand_ready"], 1)

            def fourier(st):
                for n in range(2 * FGROUPS):
                    remainder(st, (OBH[:, n, :], OBL[:, n, :]), TM[:, n % 2, :], n + 1, 0)

            def scaled(st, k, r, dst, src=None, rb=None, const=None):
                src = ps[st.bank(k)][:, :] if src is None else src
                rb = RBX[:, :] if rb is None else rb
                if const is None:
                    ins = dve.tensor_tensor(dst, src, rb, ALU.mult)
                else:
                    ins = dve.scalar_tensor_tensor(dst, src, const, rb, ALU.mult, ALU.mult)
                ins.then_inc(bank_free[st.bank(k)], 1)

            def branch(st):
                dve.wait_ge(S["factor_rows_ready"], st.at("factor_rows_ready", 0))
                def body(r):
                    for j in range(4):
                        dve.wait_ge(unit_used, st.unit(j, r) + 1)
                        if j % 2 == 0:
                            scaled(st, j, r, SG[:, j // 2, :])
                            continue
                        t = r * 2 + j // 2
                        dve.wait_ge(S["gate_ready"], st.at("gate_ready", 1 + j // 2, r))
                        if st.first:
                            scaled(st, j, r, tile_of(t, MG), rb=SG[:, j // 2, :])
                            continue
                        scaled(st, j, r, TM[:, j // 2, :], rb=SG[:, j // 2, :])
                        dve.wait_ge(bank_free[st.bank(j)], st.use(j, r) + 1)
                        dve.tensor_tensor(tile_of(t, MG), tile_of(t, MG), TM[:, j // 2, :], ALU.add).then_inc(S["product_ready"], 1)
                        if st.last:
                            remainder(st, (tile_of(t, MGH), tile_of(t, MGL)), tile_of(t, MG), 1 + j // 2, r)
                repeat(dve, st, body)

            def proj(st):
                dst = [(CQ[:, t, :], None) for t in range(4)] + [(QC[:, t, :], HD ** -0.5) for t in range(4)]
                dst += [(K2[:, 0, :], None), (VCT[:, :], None)]
                if st.at("factor_rows_ready", 0) > 0:
                    dve.wait_ge(S["factor_rows_ready"], st.at("factor_rows_ready", 0))
                for k, (d, c) in enumerate(dst):
                    dve.wait_ge(unit_used, st.unit(k) + 1)
                    scaled(st, k, 0, d, const=c)
                dve.wait_ge(unit_used, st.unit(10) + 1)
                scaled(st, 10, 0, KRAW[MLA_NOPE:MLA_QK, :], ps[st.bank(10)][0:MLA_ROPE, :], RBX[0:MLA_ROPE, :])
                dve.wait_ge(bank_free[st.bank(8)], st.use(8) + 1)
                for h in range(2):
                    dve.tensor_copy(K2[half(h), 1, :], K2[half(1 - h), 0, :]).then_inc(S["keys_copied"], 1)

            def mla_heads(st):
                for h in range(MLA_H):
                    if h % 2 == 0:
                        dve.wait_ge(S["part_multiplied"], st.at("part_multiplied", h // 2 + 1))
                    else:
                        dve.wait_ge(unit_used, st.unit(h // 2) + 1)
                    scaled(st, h, 0, QA[0:MLA_QK, h, :], ps[st.bank(h)][0:MLA_QK, :], RBQ[0:MLA_QK, :])
                for h in range(MLA_H):
                    k = MLA_H + h
                    dve.wait_ge(S["part_multiplied"], st.at("part_multiplied", 4 + h + 1))
                    scaled(st, k, 0, KA[0:MLA_NOPE, h, :], ps[st.bank(k)][0:MLA_NOPE, :], RBK[0:MLA_NOPE, :])

            def rope(st):
                at = slice(MLA_NOPE, MLA_QK)
                for n in range(MLA_H + 1):
                    dve.wait_ge(S["rope_rotated"], st.at("rope_rotated", n + 1))
                    dve.tensor_tensor(TM[at, n % 2, :], ps[st.bank(n)][at, :], SIN[at, :], ALU.mult).then_inc(bank_free[st.bank(n)], 1)
                    dve.wait_ge(bank_free[st.bank(n)], st.use(n) + 1)
                    dve.wait_ge(S["cos_applied"], st.at("cos_applied", n + 1))
                    x = KRAW[at, :] if n == 0 else QA[at, n - 1, :]
                    dve.tensor_tensor(x, x, TM[at, n % 2, :], ALU.add).then_inc(S["rope_added"], 1)

            def attention(st):
                mode = st.mode
                items = [(h, c, t) for h in range(st.heads) for c in range(st.comps) for t in range(ST)]
                for i in range(len(items) + 3):
                    if i < len(items):
                        h, c, t = items[i]
                        a, b = spans(mode, t)
                        w, s = (b - a) * P, i % 4
                        m, nm = MX[:, s:s + 1], NM[:, s:s + 1]
                        dve.wait_ge(S["scores_ready"], st.at("scores_ready", i + 1))
                        if mode == "mla":
                            dve.tensor_reduce(m, score_ps[i % 2][:, 0:w], AXX, ALU.max).then_inc(S["max_ready"], 1)
                            dve.wait_ge(S["max_ready"], st.at("max_ready", i + 1))
                            dve.tensor_scalar(nm, m, -MLA_QK ** -0.5, None, ALU.mult).then_inc(S["neg_max_ready"], 1)
                        else:
                            if mode == "gqa":
                                dist, slope = GD[:, t, 0:w], 2.0 ** (-8.0 * (h + 1) / GQA_H)
                            else:
                                at = (ST - 1 - t) * P
                                dist = DIL[:, 0 if mode == "dilated" else 2, at:at + w]
                                n = h if mode == "dilated" else DIL_H + h
                                slope = 2.0 ** (-8.0 * (n + 1) / (DIL_H + DIFF_H))
                            if i >= 4:
                                dve.wait_ge(S["probs_turned"], st.at("probs_turned", i - 3))
                            p = SG[:, s, 0:w]
                            dve.scalar_tensor_tensor(p, dist, -float(np.float32(slope)), score_ps[i % 2][:, 0:w], ALU.mult,
                                                     ALU.add).then_inc(S["scores_read"], 1)
                            dve.wait_ge(S["scores_read"], st.at("scores_read", i + 1))
                            dve.tensor_reduce(m, p, AXX, ALU.max).then_inc(S["max_ready"], 1)
                            dve.wait_ge(S["max_ready"], st.at("max_ready", i + 1))
                            if mode == "gqa":
                                dve.tensor_scalar(nm, m, col(f"gqa_sink{st.l}", h), -1.0, ALU.max, ALU.mult).then_inc(S["neg_max_ready"], 1)
                            else:
                                dve.tensor_scalar(nm, m, -1.0, None, ALU.mult).then_inc(S["neg_max_ready"], 1)
                    if 1 <= i <= len(items):
                        n = i - 1
                        h, c, t = items[n]
                        a, b = spans(mode, t)
                        w, s = (b - a) * P, n % 4
                        sm, rs = SM[:, s:s + 1], RS[:, s:s + 1]
                        dve.wait_ge(S["exp_ready"], st.at("exp_ready", n + 1))
                        if mode == "gqa":
                            dve.wait_ge(S["sink_exp_ready"], st.at("sink_exp_ready", n + 1))
                            dve.tensor_tensor(sm, sm, ES[:, s:s + 1], ALU.add).then_inc(S["sink_added"], 1)
                            dve.wait_ge(S["sink_added"], st.at("sink_added", n + 1))
                        if mode == "dilated":
                            at = (ST - 1 - t) * P
                            dve.tensor_tensor_reduce(SG[:, s, 0:w], SG[:, s, 0:w], DIL[:, 1, at:at + w], 1.0, 0.0, ALU.mult,
                                                     ALU.add, sm).then_inc(S["counts_applied"], 1)
                            dve.wait_ge(S["counts_applied"], st.at("counts_applied", n + 1))
                        dve.reciprocal(rs, sm).then_inc(S["inverse_ready"], 1)
                        if mode == "diff":
                            dve.wait_ge(S["inverse_ready"], st.at("inverse_ready", n + 1))
                            dve.tensor_tensor(rs, rs, LS[:, c:c + 1], ALU.mult).then_inc(S["lambda_applied"], 1)
                    for h in range(st.heads):
                        if i == min(((h + 1) * st.comps) * ST + 4, len(items) + 2):
                            dve.wait_ge(S["head_multiplied"], st.at("head_multiplied", (h + 1) * st.comps))
                            if mode == "diff":
                                dve.tensor_copy(UB[:, h, :], ps[st.bank(h)][:, :]).then_inc(bank_free[st.bank(h)], 1)
                                continue
                            if h % 2 == 0:
                                dve.wait_ge(S["operand_ready"], st.at("operand_ready", h // 2 - 1))
                            dve.tensor_copy(TM[half(h), (h // 2) % 2, :], ps[st.bank(h)][0:HD, :]).then_inc(bank_free[st.bank(h)], 1)
                    if mode != "diff":
                        hi, lo = pair[st.out]
                        for p in range(st.heads // 2):
                            if i == min((2 * p + 2) * ST + 6, len(items) + 2):
                                remainder(st, (hi[:, p, :], lo[:, p, :]), TM[:, p % 2, :], p + 1, 0)

            def out_y(st):
                n = st.units // 4
                def body(r):
                    for k in range(4):
                        dve.wait_ge(bank_free[st.bank(k)], st.use(k, r) + 1)
                        add_square(st, k, r, k % 2)
                repeat(dve, st, body)

            def residual(st):
                n = st.units // 4
                def body(r):
                    for k in range(4):
                        t = r * 4 + k
                        dve.wait_ge(unit_used, st.unit(n * k + n - 1, r) + 1)
                        dve.tensor_tensor(tile_of(t, X), tile_of(t, X), ps[st.bank(k)][:, :], ALU.add).then_inc(bank_free[st.bank(k)], 1)
                        if st.gain:
                            remainder(st, (tile_of(t, HH), tile_of(t, HL)), tile_of(t, X), k + 1, r, col(st.gain, t))
                            dve.wait_ge(S["square_ready"], st.at("square_ready", k + 1, r))
                            add_square(st, k, r, k % 2)
                repeat(dve, st, body)

            def swiglu(st):
                dve.wait_ge(S["factor_rows_ready"], st.at("factor_rows_ready", 0))
                def body(r):
                    for j in range(4):
                        k = j // 2
                        dve.wait_ge(unit_used, st.unit(j, r) + 1)
                        if j % 2 == 0:
                            scaled(st, j, r, SG[:, k, :])
                            continue
                        scaled(st, j, r, TM[:, k, :])
                        dve.wait_ge(bank_free[st.bank(j)], st.use(j, r) + 1)
                        dve.wait_ge(S["gate_ready"], st.at("gate_ready", 1 + k, r))
                        dve.tensor_tensor(TM[:, k, :], TM[:, k, :], SG[:, k, :], ALU.mult).then_inc(S["product_ready"], 1)
                        remainder(st, (tile_of(r * 2 + k, F1H), tile_of(r * 2 + k, F1L)), TM[:, k, :], 1 + k, r)
                repeat(dve, st, body)

            def ple_in(st):
                for t in range(2):
                    remainder(st, (POH[:, t, :], POL[:, t, :]), TM[:, t, :], t + 1, 0)

            def ple(st):
                def body(r):
                    for k in range(2):
                        dve.wait_ge(bank_free[st.bank(2 * k)], st.use(2 * k, r) + 1)
                        dve.wait_ge(bank_free[st.bank(2 * k + 1)], st.use(2 * k + 1, r) + 1)
                        dve.tensor_tensor(tile_of(r * 2 + k, YP), SG[:, 2 * k, :], SG[:, 2 * k + 1, :], ALU.mult).then_inc(S["product_ready"], 1)
                        dve.wait_ge(S["square_ready"], st.at("square_ready", k + 1, r))
                        add_square(st, k, r, k)
                repeat(dve, st, body)

            def tables2(st):
                dve.wait_ge(S["tables_loaded"], st.at("tables_loaded", 32))
                for n in range(2):
                    dve.tensor_tensor_reduce(LAMV[:, 2 * n, :], LAMV[:, 2 * n, :], LAMV[:, 2 * n + 1, :], 1.0, 0.0, ALU.mult,
                                             ALU.add, LT[:, n:n + 1]).then_inc(S["tables_stepped"], 1)
                dve.wait_ge(S["lambda_exp_ready"], st.at("lambda_exp_ready", 1))
                dve.tensor_tensor(LS[:, 1:2], LE[:, 1:2], LE[:, 0:1], ALU.subtract).then_inc(S["tables_stepped"], 1)
                dve.wait_ge(S["tables_stepped"], st.at("tables_stepped", 3))
                dve.tensor_scalar(LS[:, 1:2], LS[:, 1:2], LAM_INIT, None, ALU.subtract).then_inc(S["tables_stepped"], 1)
                dve.memset(LS[:, 0:1], 1.0).then_inc(S["tables_stepped"], 1)
                dve.tensor_scalar(SUBG[:, :], col("b_sub_norm_20"), 1.0 - LAM_INIT, None, ALU.mult).then_inc(S["tables_stepped"], 1)
                dve.tensor_scalar(GQ[:, 0:1], col("a_q_norm_20"), HD ** -0.5, None, ALU.mult)
                dve.tensor_scalar(GQ[:, 1:2], col("b_q_norm_20"), HD ** -0.5, None, ALU.mult).then_inc(S["tables_stepped"], 1)

            def qk_norm(st):
                for n in range(16):
                    dve.wait_ge(S["qk_square_ready"], st.at("qk_square_ready", n + 1))
                    dve.tensor_reduce(VQ[:, n * 8:(n + 1) * 8], SQ[:, n % 2, :].rearrange("p (a c) -> p a c", c=HD), AXX, ALU.add)\
                       .then_inc(S["qk_square_summed"], 1)
                dve.wait_ge(S["qk_square_summed"], st.at("qk_square_summed", 16))
                dve.tensor_scalar(VQ[:, :], VQ[:, :], 1.0 / HD, EPS, ALU.mult, ALU.add).then_inc(S["qk_factors_stepped"], 1)
                dve.wait_ge(S["qk_factors_stepped"], st.at("qk_factors_stepped", 2))
                dve.reciprocal(VQ[:, :], VQ[:, :]).then_inc(S["qk_factors_stepped"], 1)
                dve.wait_ge(S["qk_factors_stepped"], st.at("qk_factors_stepped", 3))
                for n in range(16):
                    c, s = n // 4, n % 4
                    c0 = c * SEQ + (SEQ if c >= 2 else 0)
                    v = QKV[:, s, c0:c0 + SEQ].rearrange("p (a c) -> p a c", c=HD)
                    f = VQ[:, n * 8:(n + 1) * 8].rearrange("p (a o) -> p a o", o=1).to_broadcast([P, 8, HD])
                    dve.tensor_tensor(v, v, f, ALU.mult).then_inc(S["qk_normed"], 1)

            def sub_norm(st):
                dve.wait_ge(S["out_squares_summed"], st.at("out_squares_summed", 1))
                dve.tensor_scalar(VAR[:, :], stat_ps[:, 0:DIFF_H * ST], 1.0 / P, EPS, ALU.mult, ALU.add).then_inc(S["out_mean_ready"], 1)
                for h in range(DIFF_H):
                    dve.wait_ge(S["out_factors_spread"], st.at("out_factors_spread", h + 1))
                    dve.scalar_tensor_tensor(UB[:, h, :], UB[:, h, :], SUBG[:, 0:1], ps[st.bank(h)][:, :], ALU.mult, ALU.mult)\
                       .then_inc(bank_free[st.bank(h)], 1)
                    remainder(st, (O2H[:, 4 + h, :], O2L[:, 4 + h, :]), UB[:, h, :], h + 1, 0)

            def zero_u(st):
                dve.memset(U[:, :, 0:4], 0.0).then_inc(S["zeros_set"], 1)

            def conv(st, k, r, dst, w, taps):
                dve.wait_ge(S["conv_begun"], st.at("conv_begun", k + 1, r))
                n = taps - 1
                src = SG[:, k, :]
                for m in range(n):
                    d = dst if m == n - 1 else SG[:, k, :]
                    dve.scalar_tensor_tensor(d, U[:, k, n - 1 - m:n - 1 - m + SEQ], w(n - 1 - m), src, ALU.mult, ALU.add)\
                       .then_inc(S["conv_tap_added"], 1)
                    if m < n - 1:
                        dve.wait_ge(S["conv_tap_added"], st.at("conv_tap_added", n * k + m + 1, r))

            def conv_ffn(st):
                dve.wait_ge(S["factor_rows_ready"], st.at("factor_rows_ready", 0))
                dve.wait_ge(S["zeros_set"], st.at("zeros_set", 0))
                def body(r):
                    for j in range(4):
                        t = r * 2 + j // 2
                        c = t + (FT2 if j % 2 else 0)
                        dve.wait_ge(unit_used, st.unit(j, r) + 1)
                        scaled(st, j, r, U[:, j, 2:2 + SEQ])
                        conv(st, j, r, SG[:, j, :], lambda m: col(f"ffn_conv_w_2{st.l}_{m}", c), 3)
                        if j % 2:
                            dve.wait_ge(S["conv_tap_added"], st.at("conv_tap_added", 2 * j + 2, r))
                            dve.wait_ge(S["gate_ready"], st.at("gate_ready", 1 + j // 2, r))
                            dve.tensor_tensor(SG[:, j, :], SG[:, j, :], SG[:, j - 1, :], ALU.mult).then_inc(S["product_ready"], 1)
                            remainder(st, (tile_of(t, F2H), tile_of(t, F2L)), SG[:, j, :], 1 + j // 2, r)
                repeat(dve, st, body)

            def rec_gate(st):
                dve.wait_ge(S["factor_rows_ready"], st.at("factor_rows_ready", 0))
                def body(r):
                    for j in range(4):
                        dve.wait_ge(unit_used, st.unit(j, r) + 1)
                        scaled(st, j, r, tile_of(r * 4 + j, GG))
                repeat(dve, st, body)

            def rec_conv(st):
                dve.wait_ge(S["factor_rows_ready"], st.at("factor_rows_ready", 0))
                dve.wait_ge(S["zeros_set"], st.at("zeros_set", 0))
                def body(r):
                    for j in range(4):
                        t = r * 4 + j
                        dve.wait_ge(unit_used, st.unit(j, r) + 1)
                        scaled(st, j, r, U[:, j, 3:3 + SEQ])
                        conv(st, j, r, tile_of(t, XR), lambda m: col(f"rec_conv_w_20_{m}", t), 4)
                        dve.wait_ge(S["conv_tap_added"], st.at("conv_tap_added", 3 * j + 3, r))
                        remainder(st, (tile_of(t, XRH), tile_of(t, XRL)), tile_of(t, XR), 1 + j, r)
                repeat(dve, st, body)

            def rec_lru(st):
                a = COLS[:, COL["rec_a_param_20"]:COL["rec_a_param_20"] + DT]
                n = 0

                def step(ins):
                    nonlocal n
                    ins.then_inc(S["decay_stepped"], 1)
                    n += 1
                    dve.wait_ge(S["decay_stepped"], st.at("decay_stepped", n))
                step(dve.tensor_scalar(LR[:, 1, :], a, -1.0, None, ALU.mult))
                step(dve.tensor_scalar(LR[:, 3, :], LR[:, 1, :], 0.0, None, ALU.max))
                dve.tensor_tensor(LR[:, 0, :], LR[:, 1, :], a, ALU.max).then_inc(S["decay_abs_ready"], 1)
                dve.wait_ge(S["decay_exp_ready"], st.at("decay_exp_ready", 1))
                step(dve.tensor_scalar(LR[:, 0, :], LR[:, 1, :], 2.0, None, ALU.add))
                step(dve.reciprocal(LR[:, 0, :], LR[:, 0, :]))
                step(dve.tensor_tensor(LR[:, 0, :], LR[:, 0, :], LR[:, 1, :], ALU.mult))
                step(dve.tensor_tensor(LR[:, 1, :], LR[:, 0, :], LR[:, 0, :], ALU.mult))
                terms = LOG_TERMS
                step(dve.tensor_scalar(LR[:, 2, :], LR[:, 1, :], 1.0 / (2 * terms + 1), None, ALU.mult))
                for m in range(terms - 1, 0, -1):
                    step(dve.scalar_tensor_tensor(LR[:, 2, :], LR[:, 2, :], 1.0 / (2 * m + 1), LR[:, 1, :], ALU.add, ALU.mult))
                step(dve.tensor_scalar(LR[:, 2, :], LR[:, 2, :], 1.0, 2.0, ALU.add, ALU.mult))
                step(dve.tensor_tensor(LR[:, 2, :], LR[:, 2, :], LR[:, 0, :], ALU.mult))
                step(dve.tensor_tensor(LR[:, 3, :], LR[:, 3, :], LR[:, 2, :], ALU.add))
                step(dve.tensor_scalar(LR[:, 3, :], LR[:, 3, :], -LRU_C, None, ALU.mult))
                A = HQ
                for k in range(8, 16):
                    dve.wait_ge(bank_free[st.bank(k)], st.use(k) + 1)
                for k in range(DT):
                    dve.wait_ge(S["tanh_ready"], st.at("tanh_ready", k + 1))
                    dve.wait_ge(S["decay_squared"], st.at("decay_squared", k + 1))
                    dve.scalar_tensor_tensor(RT[:, k, :], SQ[:, k % 2, :], 1.0, RT[:, k, :], ALU.add, ALU.mult).then_inc(S["decay_rest_ready"], 1)
                    dve.tensor_tensor(IT[:, k, :], IT[:, k, :], XR[:, k, :], ALU.mult).then_inc(S["gated_input_ready"], 1)
                for k in range(DT):
                    dve.wait_ge(S["root_ready"], st.at("root_ready", k + 1))
                    dve.wait_ge(S["gated_input_ready"], st.at("gated_input_ready", k + 1))
                    dve.tensor_tensor(IT[:, k, :], IT[:, k, :], RT[:, k, :], ALU.mult).then_inc(S["scan_input_ready"], 1)
                    dve.wait_ge(S["scan_input_ready"], st.at("scan_input_ready", k + 1))
                    dve.tensor_tensor_scan(RT[:, k, :], A[:, k, :], IT[:, k, :], 0.0, ALU.mult, ALU.add).then_inc(S["scan_done"], 1)
                    dve.wait_ge(S["scan_done"], st.at("scan_done", k + 1))
                    dve.tensor_tensor(GG[:, k, :], GG[:, k, :], RT[:, k, :], ALU.mult).then_inc(S["product_ready"], 1)
                    if k:
                        remainder(st, (ROH[:, k - 1, :], ROL[:, k - 1, :]), GG[:, k - 1, :], k, 0)
                remainder(st, (ROH[:, DT - 1, :], ROL[:, DT - 1, :]), GG[:, DT - 1, :], DT, 0)

            does = dict(init=init, operand=operand, norm=norm, zero=zero, fourier=fourier, branch=branch, proj=proj,
                        mla_heads=mla_heads, rope=rope, attention=attention, out_y=out_y, residual=residual, swiglu=swiglu,
                        ple_in=ple_in, ple=ple, tables2=tables2, qk_norm=qk_norm, sub_norm=sub_norm, zero_u=zero_u,
                        conv_ffn=conv_ffn, rec_gate=rec_gate, rec_conv=rec_conv, rec_lru=rec_lru)
            for st in STEPS:
                if st.kind in does:
                    does[st.kind](st)

        @block.gpsimd
        def _(pool):
            def remainder_of(st, j, r=0):
                n = st.unit(j) + AHEAD
                if isinstance(r, int) and n + r * st.units >= NU:
                    return
                s = n % SLOTS
                pool.wait_ge(wt_hi, n + 1 + r * st.units)
                pool.tensor_tensor(WLO[:, s, :], WRAW[:, s, :], WHI[:, s, :].bitcast(F32), ALU.subtract).then_inc(wt_lo, 1)

            def init(st):
                for u in range(AHEAD):
                    pool.wait_ge(wt_hi, u + 1)
                    pool.tensor_tensor(WLO[:, u, :], WRAW[:, u, :], WHI[:, u, :].bitcast(F32), ALU.subtract).then_inc(wt_lo, 1)
                pool.wait_ge(cst, 3)

            def units(st):
                def body(r):
                    for j in range(st.units):
                        remainder_of(st, j, r)
                last = st.u0 + st.reps * st.units + AHEAD >= NU
                repeat(pool, st, body, st.reps if last else 0)

            def operand(st):
                if not st.stat:
                    return
                pool.memset(ACC[:, :], 0.0).then_inc(S["sum_cleared"], 1)
                pool.wait_ge(S["sum_cleared"], st.at("sum_cleared", 1))
                for i in range(st.n):
                    pool.wait_ge(S["square_ready"], st.at("square_ready", i + 1))
                    if i:
                        pool.wait_ge(S["square_added"], st.at("square_added", i))
                    pool.tensor_tensor(ACC[:, :], ACC[:, :], SQ[:, i % 2, :], ALU.add).then_inc(S["square_added"], 1)

            def norm(st):
                pool.wait_ge(S["mean_square_ready"], st.at("mean_square_ready", 1))
                pool.tensor_tensor(RC[st.rb][:, 0:ST], VAR[:, 0:ST], NEGH[:, 0:ST], ALU.pow).then_inc(S["factors_ready"], 1)

            def rope(st):
                at = slice(MLA_NOPE, MLA_QK)
                pool.wait_ge(wt_lo, st.u0 + AHEAD)
                for n in range(MLA_H + 1):
                    pool.wait_ge(S["rope_rotated"], st.at("rope_rotated", n + 1))
                    x = KRAW[at, :] if n == 0 else QA[at, n - 1, :]
                    pool.tensor_tensor(x, x, COS[at, :], ALU.mult).then_inc(S["cos_applied"], 1)
                pool.wait_ge(S["cos_applied"], st.at("cos_applied", MLA_H + 1))

            def attention(st):
                items = [(h, c, t) for h in range(st.heads) for c in range(st.comps) for t in range(ST)]
                for n, (h, c, t) in enumerate(items):
                    a, b = spans(st.mode, t)
                    done = "lambda_applied" if st.mode == "diff" else "inverse_ready"
                    pool.wait_ge(S[done], st.at(done, n + 1))
                    p = SG[:, n % 4, 0:(b - a) * P]
                    pool.tensor_scalar(p, p, RS[:, n % 4:n % 4 + 1], 1.0, ALU.mult, ALU.mult).then_inc(S["probs_ready"], 1)

            def sub_norm(st):
                pool.wait_ge(S["out_mean_ready"], st.at("out_mean_ready", 1))
                pool.tensor_tensor(RC["Y"][:, :], VAR[:, :], NEGH[:, :], ALU.pow).then_inc(S["out_factors_ready"], 1)

            does = dict(init=init, operand=operand, norm=norm, rope=rope, attention=attention, sub_norm=sub_norm)
            for st in STEPS:
                if st.kind in does:
                    does[st.kind](st)
                elif st.units:
                    units(st)


def packed_weights(inputs):
    w = np.zeros((NU, P, BLOCKS * P), np.float32)
    for n, (name, layer, r0, rows, c0, cols) in enumerate(UNITS):
        a = inputs[name][layer]
        if rows == 0:
            w[n] = a.transpose(1, 0, 2).reshape(P, BLOCKS * P)
        else:
            a = a[r0:r0 + rows, c0:c0 + cols]
            w[n, :, :rows // P * cols] = a.reshape(rows // P, P, cols).transpose(1, 0, 2).reshape(P, -1)
    return w


def packed_columns(inputs):
    cols = np.zeros((P, N_COLS), np.float32)
    for name, c in COL.items():
        tap = None
        if name.count("conv_w"):
            name, tap = name.rsplit("_", 1)
        a = inputs[name[:-1]][int(name[-1])]
        if tap is not None:
            a = a[int(tap)]
        if name.startswith("gqa_sink"):
            cols[:, c:c + GQA_H] = a[None, :]
        elif a.size < P:
            cols[:, c] = np.concatenate([a, a])
        else:
            cols[:, c:c + a.size // P] = a.reshape(-1, P).T
    return cols


def tables():
    f = np.float32
    ident = np.eye(P, dtype=f)
    rot = np.zeros((P, MLA_QK), f)
    hf = MLA_ROPE // 2
    for j in range(hf):
        rot[MLA_NOPE + hf + j, MLA_NOPE + j] = -1.0
        rot[MLA_NOPE + j, MLA_NOPE + hf + j] = 1.0
    inv = np.zeros((P, 1), f)
    inv[MLA_NOPE:MLA_QK, 0] = np.tile(f(10000.0) ** (-np.arange(hf, dtype=f) / f(hf)), 2)
    consts = np.concatenate([ident, rot, inv], 1)
    q, j = np.arange(P)[:, None], np.arange(3 * P)[None, :]
    gmask = np.where(np.abs(j - P - q) <= WINDOW, 0.0, MASKED).astype(f)
    n = np.arange(SEQ)
    ang = 2 * np.pi * ((n[:, None] * n[None, :]) % SEQ) / SEQ
    scale = 1.0 / np.sqrt(SEQ * FGROUP)
    dft = (np.stack([np.cos(ang), np.sin(ang)]) * scale).astype(f)
    m = np.arange(FGROUP)
    ang = 2 * np.pi * ((m[:, None] * m[None, :]) % FGROUP) / FGROUP
    dftc = np.concatenate([np.cos(ang), -np.sin(ang)], 1).astype(f).reshape(2, P, 2 * FGROUP)
    delta = np.arange(P)[:, None] + (ST - 1) * P - np.arange(SEQ)[None, :]
    seen = (delta >= 0) * ((delta <= P) * 1 + (delta % 4 == 0) * 1 + (delta % 16 == 0) * 1)
    dil = np.stack([np.where(seen > 0, delta, MASKED), seen, np.where(delta >= 0, delta, MASKED)], 1).astype(f)
    return consts, gmask, dft, dftc, dil


def kernel(**inputs):
    from concourse import bacc
    from concourse.bass_utils import run_bass_kernel_spmd

    inputs = {k: np.asarray(v) for k, v in inputs.items()}
    consts, gmask, dft, dftc, dil = tables()
    pos = inputs["positions"]
    lamv = np.concatenate([inputs[f"b_lam_{v}_2"] for v in ("q1", "k1", "q2", "k2")], 1)
    arrays = dict(wall=packed_weights(inputs), xin=inputs["x"], pin=inputs["p"], posi=pos,
                  posc=np.ascontiguousarray(pos.reshape(ST, P).T), cols=packed_columns(inputs), consts=consts, gmask=gmask,
                  dft=dft, dftc=dftc, dil=dil, lamv=lamv)
    nc = bacc.Bacc("TRN2", target_bir_lowering=False, num_devices=1, dynamic_dma_scratch_size=RING)
    aps = {k: nc.dram_tensor(k, v.shape, mybir.dt.from_np(v.dtype), kind="ExternalInput").ap() for k, v in arrays.items()}
    y = nc.dram_tensor("y", (1, SEQ, DM), F32, kind="ExternalOutput").ap()
    build(nc, out_=y, **aps)
    got = run_bass_kernel_spmd(nc, [arrays], core_ids=[0])
    return got.results[0]["y"]
```

```python
from contextlib import ExitStack

import numpy as np
import concourse.bass as bass
from concourse import mybir

P = 128
SEQ = 512
ST = SEQ // P
DM = 1024
DT = DM // P
LAYERS = 2
FFN1 = 2816
FT1 = FFN1 // P
FFN2 = 3 * DM
FT2 = FFN2 // P
MLA_H, MLA_QK, MLA_NOPE, MLA_ROPE, MLA_V = 8, 96, 64, 32, 64
Q_LORA, KV_LORA = 384, 128
QT = Q_LORA // P
HD = 64
GQA_H = 8
DIL_H, DIFF_H = 8, 4
PLE = 256
WINDOW = 128
COL_ROPE = Q_LORA + KV_LORA
COL_QC = COL_ROPE + MLA_ROPE
COL_KC = COL_QC + GQA_H * HD
COL_VC = COL_KC + 2 * HD
COL_GATE = COL_VC + 2 * HD
FGROUP = 256
FGROUPS = DM // FGROUP
EPS = 1e-6
LAM_INIT = 0.2
LRU_C = 8.0
MASKED = 1e30
LOG_TERMS = 8
LP_STEPS = 10 + LOG_TERMS
RING = 64
DEPTH = 3
TURNED = 8
LOADS = 6
SLOTS = 4
BLOCKS = 8
AHEAD = 3
BANKS = 4

F32 = mybir.dt.float32
F32R = mybir.dt.float32r
I32 = mybir.dt.int32
ALU = mybir.AluOpType
ACT = mybir.ActivationFunctionType
AXX = mybir.AxisListType.X


def column_plan():
    at, n = {}, 0
    names = []
    for l in range(LAYERS):
        names += [(f"norm_mix_pre{l}", DT), (f"mla_q_norm{l}", QT), (f"mla_kv_norm{l}", 1),
                  (f"norm_mix_post{l}", DT), (f"norm_ffn_pre{l}", DT), (f"norm_ffn_post{l}", DT),
                  (f"norm_ple{l}", DT), (f"gqa_sink{l}", GQA_H), (f"ffn_norm_2{l}", DT)]
        names += [(f"ffn_conv_w_2{l}_{k}", 2 * FT2) for k in range(3)] + [(f"ffn_conv_b_2{l}", 2 * FT2)]
    names += [("attn_norm_20", DT), ("a_q_norm_20", 1), ("a_k_norm_20", 1), ("b_q_norm_20", 1),
              ("b_k_norm_20", 1), ("b_sub_norm_20", 1), ("rec_norm_20", DT)]
    names += [(f"rec_conv_w_20_{k}", DT) for k in range(4)]
    names += [(f"{v}0", DT) for v in ("rec_conv_b_2", "rec_gate_a_b_2", "rec_gate_x_b_2", "rec_a_param_2")]
    for name, tiles in names:
        at[name] = n
        n += tiles
    return at, n


COL, N_COLS = column_plan()


def unit_list():
    u = []

    def product(name, l, rows, c):
        for k in range(0, rows, DM):
            u.append((name, l, k, min(DM, rows - k), c, P))

    def gates_and_branch(name, l, rows, gate):
        for n in range(DT):
            product("w_in", l, DM, COL_GATE + gate * DM + n * P)
            product(name, l, rows, n * P)

    for l in range(LAYERS):
        gates_and_branch("w_branch_b", l, DM, 1)
        for c in [n * P for n in range(4)] + [COL_QC + n * P for n in range(4)] + [COL_KC, COL_VC, COL_ROPE]:
            product("w_in", l, DM, c)
        gates_and_branch("w_branch_c", l, GQA_H * HD, 2)
        for n in range(MLA_H // 2):
            u.append(("w_uq", l, 0, Q_LORA, n * 2 * MLA_QK, 2 * MLA_QK))
        u.append(("w_ukv", l, 0, KV_LORA, 0, MLA_H * P))
        gates_and_branch("w_branch_a", l, MLA_H * MLA_V, 0)
        for n in range(DT):
            product("w_out", l, DM, n * P)
        for n in range(FT1):
            product("w_ffn_gate", l, DM, n * P)
            product("w_ffn_up", l, DM, n * P)
        for n in range(DT):
            product("w_ffn_down", l, FFN1, n * P)
        for n in range(DT):
            product("w_ple_proj", l, PLE, n * P)
            product("w_ple_gate", l, DM, n * P)

    def conv_ffn(l):
        for n in range(FT2):
            product("ffn_w_up_2", l, DM, n * P)
            product("ffn_w_up_2", l, DM, FFN2 + n * P)
        for n in range(DT):
            product("ffn_w_down_2", l, FFN2, n * P)

    for n in [*range(8), *range(12, 20), *range(8, 12), *range(20, 24)]:
        product("attn_w_in_2", 0, DM, n * P)
    for n in range(DT):
        product("attn_w_out_2", 0, DM, n * P)
    conv_ffn(0)
    for n in range(DT, 2 * DT):
        product("rec_w_in_2", 0, DM, n * P)
    u.append(("rec_gate_a_w_2", 0, 0, 0, 0, 0))
    u.append(("rec_gate_x_w_2", 0, 0, 0, 0, 0))
    for n in range(DT):
        product("rec_w_in_2", 0, DM, n * P)
    for n in range(DT):
        product("rec_w_out_2", 0, DM, n * P)
    conv_ffn(1)
    return u


UNITS = unit_list()
NU = len(UNITS)


class Stage:

    def __init__(self, kind, reps, units, tiles, per, *, u0, t0, base, rb=None, width=0, where=None, src=None, dst=None,
                 gain=None, n=0, stat=False, y=None, gy=None, t=0, made=None, kt=0, first=False, last=False, op=0, mode=None,
                 heads=0, comps=1, out=None, l=0, proj=None, rope=None, qk=None, att=None, norm=None, taps=0):
        self.kind, self.reps, self.units, self.tiles, self.per = kind, reps, units, tiles, per
        self.u0, self.t0, self.base = u0, t0, base
        self.rb, self.width, self.where = rb, width, where
        self.src, self.dst, self.gain, self.n, self.stat = src, dst, gain, n, stat
        self.y, self.gy, self.t, self.made, self.kt = y, gy, t, made, kt
        self.first, self.last, self.op, self.mode, self.heads, self.comps = first, last, op, mode, heads, comps
        self.out, self.l, self.proj, self.rope, self.qk, self.att = out, l, proj, rope, qk, att
        self.norm, self.taps = norm, taps

    def at(self, signal, k, r=0):
        return self.base.get(signal, 0) + r * self.per.get(signal, 0) + k

    def unit(self, j, r=0):
        return self.u0 + r * self.units + j

    def bank(self, k):
        return (self.t0 + k) % BANKS

    def use(self, k, r=0):
        return (self.t0 + k) // BANKS + r * (self.tiles // BANKS)


def plan():
    steps, count = [], {}
    at = [0, 0]

    def add(kind, reps=1, units=0, tiles=0, per=(), **opt):
        st = Stage(kind, reps, units, tiles, dict(per), u0=at[0], t0=at[1], base=dict(count), **opt)
        at[0] += reps * units
        at[1] += reps * tiles
        for k, v in st.per.items():
            count[k] = count.get(k, 0) + reps * v
        steps.append(st)
        return st

    def norm(rb, width, where="now"):
        return add("norm", per={k: 1 for k in ("norm_summed", "mean_square_ready", "factors_ready", "factors_spread", "factor_rows_ready")}, rb=rb, width=width, where=where)

    def operand(src, dst, gain, n, stat, y=None, gy=None, t=0, made=None):
        per = {"operand_hi_ready": n, "operand_ready": n}
        if stat:
            per |= {"square_ready": n, "sum_cleared": 1, "square_added": n}
        if y:
            per |= {"update_ready": n, "residual_updated": n}
        return add("operand", per=per, src=src, dst=dst, gain=gain, n=n, stat=stat, y=y, gy=gy, t=t, made=made)

    def need(kt):
        return count["operand_ready"] - kt

    def branch(kt, src, first, last, op=None, norms=()):
        op, per = need(kt) if op is None else op, {"gate_ready": 2} | ({} if first else {"product_ready": 2})
        if last:
            per |= {"operand_hi_ready": 2, "operand_ready": 2}
        return add("branch", 4, 4, 4, per, kt=kt, src=src, first=first, last=last, op=op, norm=norms)

    def out_y(src, kt, y):
        n = -(-kt // BLOCKS)
        add("zero", per={"sum_cleared": 1})
        return add("out_y", 2, 4 * n, 4, {"square_added": 4}, kt=kt, src=src, y=y, op=need(kt))

    def residual(src, kt, gain):
        n, op = -(-kt // BLOCKS), need(kt)
        per = {}
        if gain:
            add("zero", per={"sum_cleared": 1})
            per = {"operand_hi_ready": 4, "operand_ready": 4, "square_ready": 4, "square_added": 4}
        return add("residual", 2, 4 * n, 4, per, kt=kt, src=src, gain=gain, op=op)

    def attention(mode, heads, comps, out, **opt):
        n = heads * comps * ST
        per = {k: n for k in ("scores_ready", "neg_max_ready", "exp_ready", "inverse_ready", "probs_ready", "probs_turned", "turned_copied")}
        per |= {"item_multiplied": n}
        per |= {"gqa": {"sink_exp_ready": n, "sink_added": n}, "mla": {"max_ready": n}, "dilated": {"bias_scaled": heads}, "diff": {"lambda_applied": n}}[mode]
        if mode != "mla":
            per |= {"scores_read": n, "bias_ready": heads * (ST if mode == "gqa" else 1)}
        if mode != "diff":
            per |= {"operand_hi_ready": heads // 2, "operand_ready": heads // 2}
        return add("attention", tiles=heads, per=per, mode=mode, heads=heads, comps=comps, out=out, **opt)

    add("init", tiles=DT, per={"rows_turned": DT, "dft_hi_ready": 1, "dft_lo_ready": 1})
    for l in range(LAYERS):
        operand("X", "H", f"norm_mix_pre{l}", DT, True, **(dict(made=steps[0]) if l == 0 else {}), **(dict(y="YP", gy=f"norm_ple{l - 1}") if l else {}))
        op = need(DT)
        n = norm("X", DM, "inner")
        f = add("fourier", tiles=FGROUPS * (ST + 2), per={"channels_transformed": 16, "tokens_transformed": 8, "operand_hi_ready": 8, "operand_ready": 8, "dft_loaded": 32}, op=op, norm=n)
        if l == 0:
            add("tables1", per={"table_stepped": 16, "table_looked_up": 8})
        branch(DT, "OB", True, False)
        pr = add("proj", units=11, tiles=12, per={"keys_copied": 2, "values_turned": 1})
        attention("gqa", GQA_H, 1, "OC", l=l, proj=pr)
        need_oc = need(GQA_H // 2)
        operand("CQ", "CQ", f"mla_q_norm{l}", QT, True, made=pr)
        nq = norm("Q", Q_LORA, "inner")
        operand("CQ", "CQ", f"mla_kv_norm{l}", 1, True, t=QT, made=pr)
        nk = norm("K", KV_LORA, "inner")
        need_cq = need(QT + 1)
        branch(GQA_H // 2, "OC", False, False, need_oc, (nq, nk))
        heads = add("mla_heads", units=5, tiles=20, per={"part_multiplied": 4 + 11}, op=need_cq)
        rp = add("rope", tiles=MLA_H + 1, per={"rope_rotated": 9, "cos_applied": 9, "rope_added": 9, "rope_keys_spread": 1}, proj=pr, heads=heads)
        attention("mla", MLA_H, 1, "OA", l=l, rope=rp)
        branch(MLA_H // 2, "OA", False, True)
        out_y("MG", DT, "YH")
        norm("Y", DM)
        operand("X", "H", f"norm_ffn_pre{l}", DT, True, y="YH", gy=f"norm_mix_post{l}")
        op = need(DT)
        n = norm("X", DM, "inner")
        add("swiglu", FT1 // 2, 4, 4, {"gate_ready": 2, "product_ready": 2, "operand_hi_ready": 2, "operand_ready": 2}, op=op, norm=n)
        out_y("F1", FT1, "YH")
        norm("Y", DM)
        add("ple_in", tiles=2, per={"ple_loaded": 16, "ple_turned": 2, "operand_hi_ready": 2, "operand_ready": 2}, l=l)
        operand("X", "H", None, DT, False, y="YH", gy=f"norm_ffn_post{l}")
        add("zero", per={"sum_cleared": 1})
        add("ple", 4, 4, 4, {"product_ready": 2, "square_ready": 2, "square_added": 2}, op=need(DT + 2))
        norm("Y", DM)
    operand("X", "H", "attn_norm_20", DT, True, y="YP", gy=f"norm_ple{LAYERS - 1}")
    op = need(DT)
    n = norm("X", DM, "inner")
    add("tables2", per={"tables_loaded": 32, "tables_stepped": 7, "lambda_exp_ready": 1})
    add("qkv", 4, 4, 4, {"part_multiplied": 2}, op=op, norm=n)
    add("qkv", 1, 8, 8, {"part_multiplied": 4, "qk_square_ready": 16, "qk_square_summed": 16}, n=8, op=op)
    qk = add("qk_norm", tiles=16, per={"qk_factors_stepped": 3, "qk_normed": 16, "qk_turned": 16})
    attention("dilated", DIL_H, 1, "O2", l=0, qk=qk)
    diff = attention("diff", DIFF_H, 2, "U", l=0, qk=qk)
    add("sub_norm", tiles=4, att=diff, per={"out_square_ready": 4, "out_squares_summed": 1, "out_mean_ready": 1, "out_factors_ready": 1, "out_factors_spread": 4, "operand_hi_ready": 4, "operand_ready": 4})
    residual("O2", DT, "ffn_norm_20")

    def conv_ffn(l, gain):
        op = need(DT)
        n = norm("X", DM, "inner")
        add("zero_u", per={"zeros_set": 1}, taps=3)
        add("conv_ffn", FT2 // 2, 4, 4, {"conv_begun": 4, "conv_tap_added": 8, "gate_ready": 2, "product_ready": 2, "operand_hi_ready": 2, "operand_ready": 2}, l=l, op=op, norm=n)
        residual("F2", FT2, gain)

    conv_ffn(0, "rec_norm_20")
    op = need(DT)
    n = norm("X", DM, "inner")
    add("zero_u", per={"zeros_set": 1}, taps=4)
    add("rec_conv", 2, 4, 4, {"conv_begun": 4, "conv_tap_added": 12, "operand_hi_ready": 4, "operand_ready": 4}, op=op, norm=n)
    add("rec_lru", units=2 + DT, tiles=3 * DT, per={"part_multiplied": 14, "gate_ready": DT, "decay_abs_ready": 1, "decay_exp_ready": 1, "decay_stepped": LP_STEPS, "decay_ready": 8, "tanh_ready": 8, "decay_squared": 8, "decay_rest_ready": 8,
                                           "root_ready": 8, "gated_input_ready": 8, "scan_input_ready": 8, "scan_done": 8, "product_ready": 8, "operand_hi_ready": 8, "operand_ready": 8}, op=need(DT))
    residual("RO", DT, "ffn_norm_21")
    conv_ffn(1, None)
    add("out", tiles=8, per={"rows_turned": 8, "output_stored": 16 * ST})
    return steps


STEPS = plan()


def build(nc, wall, xin, pin, posi, posc, cols, consts, gmask, dft, dftc, dil, lamv, out_):
    with ExitStack() as ctx:
        KB = 1024
        base = [RING]

        def place(name, shape, dt=F32, at=None):
            size = int(np.prod(shape[1:])) * 4
            if at is None:
                at = base[0]
                base[0] += -(-size // 32) * 32
            assert at + size <= nc.sbuf_usable_end, name
            return nc.alloc_sbuf_tensor_at(name, shape, dt, offset=at)

        def sem(name):
            return ctx.enter_context(nc.semaphore(name))

        X = place("X", [P, DT, SEQ])
        h_at = base[0]
        HH, HL = place("HH", [P, DT, SEQ], F32R), place("HL", [P, DT, SEQ], F32R)
        YH = place("YH", [P, DT, SEQ], at=h_at + 16 * KB)
        HQ = place("HQ", [P, 16, SEQ], at=h_at)
        w_at = base[0]
        WRAW = place("WRAW", [P, SLOTS, BLOCKS * P])
        WLO = place("WLO", [P, SLOTS, BLOCKS * P], F32R, at=w_at)
        WHI = place("WHI", [P, SLOTS, BLOCKS * P], F32R)
        CONST, ONES = place("CONST", [P, P + MLA_QK + 1]), place("ONES", [P, 1])
        IDENT, ROT, INVF = CONST[:, 0:P], CONST[:, P:P + MLA_QK], CONST[:, P + MLA_QK:P + MLA_QK + 1]
        NEGH, VAR = place("NEGH", [P, 16]), place("VAR", [P, 16])
        COLS = place("COLS", [P, N_COLS])
        SG = place("SG", [P, 4, SEQ])
        SQ, TM = place("SQ", [P, 2, SEQ]), place("TM", [P, 2, SEQ])
        ACC = place("ACC", [P, SEQ])
        RBX, RBY = place("RBX", [P, SEQ]), place("RBY", [P, SEQ])
        RC = {k: place(f"RC{k}", [P, 16]) for k in "XYQK"}
        MX, NM, SM, RS, ES = (place(n, [P, 4]) for n in ("MX", "NM", "SM", "RS", "ES"))
        o_at = base[0]
        TDH, TDL = place("TDH", [P, 2, SEQ], F32R), place("TDL", [P, 2, SEQ], F32R)
        COS, SIN = place("COS", [P, SEQ]), place("SIN", [P, SEQ])
        GD = place("GD", [P, ST, 3 * P])
        s_at = base[0]
        DIL = place("DIL", [P, 3, SEQ], at=o_at)
        U = place("U", [P, 4, SEQ + 4], at=o_at + 6 * KB)
        UB = place("UB", [P, 4, SEQ], at=o_at + 6 * KB)
        LAMV = place("LAMV", [P, 4, HD], at=o_at + 15 * KB)
        LS, LT = place("LS", [P, 2], at=o_at + 16 * KB + 64), place("LT", [P, 2], at=o_at + 16 * KB + 96)
        LE = place("LE", [P, 2], at=o_at + 16 * KB + 128)
        SUBG = place("SUBG", [P, 1], at=o_at + 16 * KB + 192)
        GQ = place("GQ", [P, 2], at=o_at + 16 * KB + 160)
        LR = place("LR", [P, 4, DT], at=o_at + 16 * KB + 256)
        base[0] = nc.sbuf_usable_end

        def work(name, shape, at, dt=F32):
            return place(name, shape, dt, at=s_at + at * KB)

        XROWS = work("XROWS", [P, ST, DM], 0)
        POSI, POSC_I = work("POSI", [P, SEQ], 64, I32), work("POSC_I", [P, ST], 66, I32)
        POSF, POSC = work("POSF", [P, SEQ], 68), work("POSC", [P, ST], 70)
        ANG, TURN = work("ANG", [P, SEQ], 72), work("TURN", [P, SEQ], 74)
        GM, TDRAW = work("GM", [P, 3 * P], 76), work("TDRAW", [P, 2, SEQ], 32)
        DFT, PG = work("DFT", [P, 2, ST, SEQ], 0), work("PG", [P, 2, ST, SEQ], 16)
        OBH, OBL = work("OBH", [P, DT, SEQ], 32, F32R), work("OBL", [P, DT, SEQ], 48, F32R)
        MG = work("MG", [P, DT, SEQ], 80)
        CQ, QC, K2 = work("CQ", [P, 4, SEQ], 0), work("QC", [P, 4, SEQ], 30), work("K2", [P, 2, SEQ], 38)
        VCT, VR, KRAW = work("VCT", [P, SEQ], 42), work("VR", [P, ST, P], 44), work("KRAW", [P, SEQ], 12)
        RBQ, RBK = work("RBQ", [P, SEQ], 8), work("RBK", [P, SEQ], 10)
        PT, BT = work("PT", [P, TURNED, SEQ], 14), work("BT", [P, 2, ST, 3 * P], 46)
        CQH, CQL = work("CQH", [P, 4, SEQ], 14, F32R), work("CQL", [P, 4, SEQ], 22, F32R)
        QA, KA, VA = work("QA", [P, MLA_H, SEQ], 30), work("KA", [P, MLA_H, SEQ], 46), work("VA", [P, ST, SEQ], 0)
        OCH, OCL = work("OCH", [P, 4, SEQ], 62, F32R), work("OCL", [P, 4, SEQ], 70, F32R)
        OAH, OAL = work("OAH", [P, 4, SEQ], 62, F32R), work("OAL", [P, 4, SEQ], 70, F32R)
        MGH, MGL = work("MGH", [P, DT, SEQ], 14, F32R), work("MGL", [P, DT, SEQ], 30, F32R)
        F1H, F1L = work("F1H", [P, FT1, SEQ], 0, F32R), work("F1L", [P, FT1, SEQ], 44, F32R)
        POH, POL, PROWS = work("POH", [P, 2, SEQ], 0, F32R), work("POL", [P, 2, SEQ], 4, F32R), work("PROWS", [P, ST, PLE], 8)
        YP = work("YP", [P, DT, SEQ], 16)
        QKV, PT2 = work("QKV", [P, ST, 3 * DM], 0), work("PT2", [P, TURNED, SEQ], 48)
        BT2 = work("BT2", [P, 2, SEQ], 96)
        VQ = work("VQ", [P, P], 48)
        O2H, O2L = work("O2H", [P, DT, SEQ], 64, F32R), work("O2L", [P, DT, SEQ], 80, F32R)
        F2H, F2L = work("F2H", [P, FT2, SEQ], 0, F32R), work("F2L", [P, FT2, SEQ], 48, F32R)
        GG, XR = work("GG", [P, DT, SEQ], 0), work("XR", [P, DT, SEQ], 16)
        XRH, XRL = work("XRH", [P, DT, SEQ], 32, F32R), work("XRL", [P, DT, SEQ], 48, F32R)
        RT, IT = work("RT", [P, DT, SEQ], 64), work("IT", [P, DT, SEQ], 80)
        DECAY = work("DECAY", [P, DT, SEQ], 32)
        ROH, ROL = work("ROH", [P, DT, SEQ], 16, F32R), work("ROL", [P, DT, SEQ], 48, F32R)
        YROWS = work("YROWS", [P, ST, DM], 0)

        pair = {"H": (HH, HL), "OB": (OBH, OBL), "OC": (OCH, OCL), "OA": (OAH, OAL), "MG": (MGH, MGL), "CQ": (CQH, CQL),
                "F1": (F1H, F1L), "O2": (O2H, O2L), "F2": (F2H, F2L), "RO": (ROH, ROL)}
        source = {"X": X, "CQ": CQ, "YH": YH, "YP": YP}
        RB = {"X": RBX, "Y": RBY, "Q": RBQ, "K": RBK}

        ps = [ctx.enter_context(nc.psum_tensor(f"ps{b}", [P, SEQ], F32)) for b in range(8)]
        score_ps, turn_ps, stat_ps = ps[4:6], ps[6:8], ps[7]

        raw = [sem(f"raw{s}") for s in range(SLOTS)]
        wt_hi, wt_lo = sem("wt_hi"), sem("wt_lo")
        unit_used = sem("unit_used")
        bank_free = [sem(f"bank_free{b}") for b in range(BANKS)]
        x_in = sem("x_in")
        const_in = sem("const_in")
        ld = sem("ld")
        cst = sem("cst")
        S = {}

        def sig(name):
            if name not in S:
                S[name] = sem(name)
            return S[name]

        for st in STEPS:
            for name in st.per:
                sig(name)

        def repeat(e, st, body, peel=0):
            for r in range(min(peel, st.reps)):
                body(r)
            left = st.reps - peel
            if left == 1:
                body(st.reps - 1)
            elif left > 1:
                with e.Fori(peel, st.reps) as r:
                    body(r)

        def tile_of(t, A):
            return A[:, t, :] if isinstance(t, int) else A[:, bass.ds(t, 1), :].rearrange("p o s -> p (o s)")

        def col(name, t=0):
            c = COL[name] + t
            return COLS[:, c:c + 1] if isinstance(c, int) else COLS[:, bass.ds(c, 1)]

        def spans(mode, t):
            if mode == "gqa":
                return max(0, t - 1), min(ST, t + 2)
            return (0, ST) if mode == "mla" else (0, t + 1)

        def attention_items(st):
            return [(h, c, t) for h in range(st.heads) for t in range(ST) for c in range(st.comps)]

        def half(h, n=HD):
            return slice((h % 2) * n, (h % 2) * n + n)

        def on_pool(st, i):
            return st.y is not None and not st.gain

        FOURIER_ORDER = [("rows", 0), ("norm", 0), ("rows", 1), ("cols", 0), ("rows", 2), ("cols", 1), ("rows", 3),
                         ("cols", 2), ("cols", 3)]

        def fourier_tile(what, g, k):
            n = 0
            for w, gg in FOURIER_ORDER:
                if (w, gg) == (what, g):
                    return n + k
                n += {"rows": ST, "cols": 2, "norm": 0}[w]

        block = ctx.enter_context(nc.Block())

        @block.sync
        def _(sp):
            sp.wait_ge(x_in, 16)
            for u in range(SLOTS):
                sp.dma_start(WRAW[:, u, :], wall[u]).then_inc(raw[u], 16)
            left = (NU - SLOTS) // SLOTS
            with sp.Fori(0, left) as i:
                for s in range(SLOTS):
                    sp.wait_ge(unit_used, i * SLOTS + s + 1)
                    sp.dma_start(WRAW[:, s, :], wall[bass.ds((i + 1) * SLOTS + s, 1)].rearrange("o p n -> (o p) n"))\
                      .then_inc(raw[s], 16)
            for u in range(SLOTS + left * SLOTS, NU):
                sp.wait_ge(unit_used, u - SLOTS + 1)
                sp.dma_start(WRAW[:, u % SLOTS, :], wall[u]).then_inc(raw[u % SLOTS], 16)

        @block.tensor
        def _(pe):
            def weights(u):
                pe.wait_ge(wt_lo, u + 1)

            def three(out_, w_at, x_hi, x_lo, first, last):
                pe.matmul(out_, WHI[w_at], x_hi, start=first, stop=False)
                pe.matmul(out_, WHI[w_at], x_lo, start=False, stop=False)
                return pe.matmul(out_, WLO[w_at], x_hi, start=False, stop=last)

            def tile(st, j, k, r, src, kt, k0=0, ready=None, start=True, stop=True):
                weights(st.unit(j, r))
                s = st.unit(j) % SLOTS
                if start:
                    pe.wait_ge(bank_free[st.bank(k)], st.use(k, r))
                hi, lo = src
                for i in range(kt):
                    if ready is not None:
                        pe.wait_ge(S["operand_ready"], ready + k0 + i + 1)
                    mm = three(ps[st.bank(k)][:, :], (slice(None), s, slice(i * P, i * P + P)), hi[:, k0 + i, :],
                               lo[:, k0 + i, :], start and i == 0, stop and i == kt - 1)
                mm.then_inc(unit_used, 1)

            def norm(st):
                if st.at("factor_rows_ready", 0) > 0:
                    pe.wait_ge(S["factor_rows_ready"], st.at("factor_rows_ready", 0))
                pe.wait_ge(S["square_added"], st.at("square_added", 0))
                for s in range(ST):
                    mm = pe.matmul(stat_ps[:, s:s + 1], ACC[:, s * P:(s + 1) * P], ONES[:, 0:1], start=True, stop=True)
                mm.then_inc(S["norm_summed"], 1)
                pe.wait_ge(S["factors_ready"], st.at("factors_ready", 1))
                for s in range(ST):
                    mm = pe.transpose(stat_ps[:, s * P:(s + 1) * P], RC[st.rb][:, s:s + 1].to_broadcast([P, P]), IDENT[:, :])
                mm.then_inc(S["factors_spread"], 1)

            def init(st):
                pe.wait_ge(const_in, 16)
                pe.wait_ge(x_in, 16)
                pe.wait_ge(cst, 3)
                for t in range(DT):
                    if st.use(t) > 0:
                        pe.wait_ge(bank_free[st.bank(t)], st.use(t))
                    for s in range(ST):
                        mm = pe.transpose(ps[st.bank(t)][:, s * P:(s + 1) * P], XROWS[:, s, t * P:(t + 1) * P], IDENT[:, :])
                    mm.then_inc(S["rows_turned"], 1)

            def fourier(st):
                for what, g in FOURIER_ORDER:
                    if what == "norm":
                        norm(st.norm)
                    elif what == "rows":
                        for s in range(ST):
                            k = fourier_tile("rows", g, s)
                            pe.wait_ge(bank_free[st.bank(k)], st.use(k))
                            if g == 0 and s == 0:
                                pe.wait_ge(S["dft_lo_ready"], STEPS[0].at("dft_lo_ready", 1))
                            for c in range(2):
                                t = 2 * g + c
                                if s == 0:
                                    pe.wait_ge(S["operand_ready"], st.op + t + 1)
                                o, at = ps[st.bank(k)][:, :], slice(s * P, (s + 1) * P)
                                pe.matmul(o, HH[:, t, at], TDH[:, c, :], start=c == 0, stop=False)
                                pe.matmul(o, HH[:, t, at], TDL[:, c, :], start=False, stop=False)
                                mm = pe.matmul(o, HL[:, t, at], TDH[:, c, :], start=False, stop=c == 1)
                            mm.then_inc(S["channels_transformed"], 1)
                    else:
                        if g == 0:
                            pe.wait_ge(S["dft_loaded"], st.at("dft_loaded", 32))
                        for c in range(2):
                            k = fourier_tile("cols", g, c)
                            pe.wait_ge(bank_free[st.bank(k)], st.use(k))
                            pe.wait_ge(bank_free[st.bank(fourier_tile("rows", g, ST - 1))], st.use(fourier_tile("rows", g, ST - 1)) + 1)
                            pe.wait_ge(bank_free[st.bank(fourier_tile("rows", g, ST - 2))], st.use(fourier_tile("rows", g, ST - 2)) + 1)
                            pe.wait_ge(bank_free[st.bank(fourier_tile("rows", g, ST - 3))], st.use(fourier_tile("rows", g, ST - 3)) + 1)
                            pe.wait_ge(bank_free[st.bank(fourier_tile("rows", g, ST - 4))], st.use(fourier_tile("rows", g, ST - 4)) + 1)
                            for s in range(ST):
                                for part in range(2):
                                    mm = pe.matmul(ps[st.bank(k)][:, :],
                                                   PG[:, g % 2, s, part * FGROUP + c * P:part * FGROUP + (c + 1) * P],
                                                   DFT[:, part, s, :], start=s + part == 0, stop=s == ST - 1 and part == 1)
                            mm.then_inc(S["tokens_transformed"], 1)

            def branch(st):
                def body(r):
                    for j in range(4):
                        if j % 2 == 0:
                            tile(st, j, j, r, pair["H"], DT)
                        else:
                            tile(st, j, j, r, pair[st.src], st.kt, ready=st.op if isinstance(r, int) and r == 0 else None)
                        if isinstance(r, int) and r == 0 and j < len(st.norm):
                            norm(st.norm[j])
                repeat(pe, st, body, 1)

            def proj(st):
                for j in range(11):
                    tile(st, j, j, 0, pair["H"], DT)
                pe.wait_ge(bank_free[st.bank(9)], st.use(9) + 1)
                pe.wait_ge(bank_free[st.bank(11)], st.use(11))
                for s in range(ST):
                    mm = pe.transpose(ps[st.bank(11)][:, s * P:(s + 1) * P], VCT[:, s * P:(s + 1) * P], IDENT[:, :])
                mm.then_inc(S["values_turned"], 1)

            def mla_heads(st):
                hi, lo = pair["CQ"]
                k = 0
                for j in range(4):
                    weights(st.unit(j))
                    s = st.unit(j) % SLOTS
                    for c in range(2):
                        pe.wait_ge(bank_free[st.bank(k)], st.use(k))
                        for i in range(QT):
                            if k == 0:
                                pe.wait_ge(S["operand_ready"], st.op + i + 1)
                            at = i * 2 * MLA_QK + c * MLA_QK
                            mm = three(ps[st.bank(k)][0:MLA_QK, :], (slice(None), s, slice(at, at + MLA_QK)),
                                       hi[:, i, :], lo[:, i, :], i == 0, i == QT - 1)
                        mm.then_inc(S["part_multiplied"] if c == 0 else unit_used, 1)
                        k += 1
                weights(st.unit(4))
                s = st.unit(4) % SLOTS
                pe.wait_ge(S["operand_ready"], st.op + QT + 1)
                for h in range(MLA_H):
                    pe.wait_ge(bank_free[st.bank(k)], st.use(k))
                    three(ps[st.bank(k)][0:MLA_NOPE, :], (slice(None), s, slice(h * P, h * P + MLA_NOPE)),
                          hi[:, QT, :], lo[:, QT, :], True, True).then_inc(S["part_multiplied"], 1)
                    k += 1
                for t in range(ST):
                    pe.wait_ge(bank_free[st.bank(k)], st.use(k))
                    at = slice(t * P, (t + 1) * P)
                    whi = WHI[:, s, :].rearrange("p (h c) -> p h c", c=P)[:, :, MLA_NOPE:P]
                    wlo = WLO[:, s, :].rearrange("p (h c) -> p h c", c=P)[:, :, MLA_NOPE:P]
                    o = ps[st.bank(k)][:, :]
                    pe.matmul(o, hi[:, QT, at], whi, start=True, stop=False)
                    pe.matmul(o, lo[:, QT, at], whi, start=False, stop=False)
                    pe.matmul(o, hi[:, QT, at], wlo, start=False, stop=True).then_inc(S["part_multiplied"] if t < ST - 1 else unit_used, 1)
                    k += 1

            def rope(st):
                for n in range(MLA_H + 1):
                    pe.wait_ge(bank_free[st.bank(n)], st.use(n))
                    if n == 0:
                        pr = st.proj
                        pe.wait_ge(bank_free[pr.bank(10)], pr.use(10) + 1)
                        pe.matmul(ps[st.bank(n)][0:MLA_QK, :], ROT[MLA_NOPE:MLA_QK, :], KRAW[MLA_NOPE:MLA_QK, :],
                                  start=True, stop=True).then_inc(S["rope_rotated"], 1)
                    else:
                        pe.wait_ge(bank_free[st.heads.bank(n - 1)], st.heads.use(n - 1) + 1)
                        pe.matmul(ps[st.bank(n)][0:MLA_QK, :], ROT[0:MLA_QK, :], QA[0:MLA_QK, n - 1, :],
                                  start=True, stop=True).then_inc(S["rope_rotated"], 1)

            def attention(st):
                mode = st.mode
                items = attention_items(st)
                pt = PT if mode in ("gqa", "mla") else PT2

                def operands(h, c, t):
                    a, b = spans(mode, t)
                    at, ks = slice(t * P, (t + 1) * P), slice(a * P, b * P)
                    if mode == "gqa":
                        kv = h // (GQA_H // 2)
                        return QC[half(h), h // 2, at], K2[half(h), (kv + h) % 2, ks]
                    if mode == "mla":
                        return QA[0:MLA_QK, h, at], KA[0:MLA_QK, h, ks]
                    if mode == "dilated":
                        return HQ[half(h), h // 2, at], HQ[half(h), 4 + h // 2, ks]
                    return HQ[half(c), 8 + h, at], HQ[half(c), 12 + h, ks]

                def values(h, kt):
                    if mode == "gqa":
                        kv = h // (GQA_H // 2)
                        return VR[:, kt, kv * HD:(kv + 1) * HD]
                    if mode == "mla":
                        return VA[:, kt, h * MLA_V:(h + 1) * MLA_V]
                    if mode == "dilated":
                        return QKV[:, kt, 4 * SEQ + h * HD:4 * SEQ + (h + 1) * HD]
                    return QKV[:, kt, 5 * SEQ + h * P:5 * SEQ + (h + 1) * P]

                pe.wait_ge(S["factor_rows_ready"], st.at("factor_rows_ready", 0))
                if mode == "gqa":
                    pe.wait_ge(bank_free[st.proj.bank(11)], st.proj.use(11) + 1)
                    pe.wait_ge(bank_free[st.proj.bank(7)], st.proj.use(7) + 1)
                    pe.wait_ge(S["keys_copied"], st.proj.at("keys_copied", 2))
                if mode == "mla":
                    pe.wait_ge(S["rope_added"], st.rope.at("rope_added", 9))
                    pe.wait_ge(S["rope_keys_spread"], st.rope.at("rope_keys_spread", 1))
                for i in range(len(items) + DEPTH + 1):
                    if i < len(items):
                        h, c, t = items[i]
                        free = "exp_ready" if mode == "mla" else "scores_read"
                        if i >= 2:
                            pe.wait_ge(S[free], st.at(free, i - 1))
                        else:
                            if st.at("exp_ready", 0) > 0:
                                pe.wait_ge(S["exp_ready"], st.at("exp_ready", 0))
                        if mode == "dilated":
                            pe.wait_ge(bank_free[st.qk.bank(h // 2)], st.qk.use(h // 2) + 1)
                            pe.wait_ge(bank_free[st.qk.bank(4 + h // 2)], st.qk.use(4 + h // 2) + 1)
                        if mode == "diff":
                            pe.wait_ge(bank_free[st.qk.bank(8 + h)], st.qk.use(8 + h) + 1)
                            pe.wait_ge(bank_free[st.qk.bank(12 + h)], st.qk.use(12 + h) + 1)
                        q, k = operands(h, c, t)
                        a, b = spans(mode, t)
                        pe.matmul(score_ps[i % 2][:, 0:(b - a) * P], q, k, start=True, stop=True).then_inc(S["scores_ready"], 1)
                    if DEPTH <= i < len(items) + DEPTH:
                        n = i - DEPTH
                        h, c, t = items[n]
                        a, b = spans(mode, t)
                        pe.wait_ge(S["probs_ready"], st.at("probs_ready", n + 1))
                        if st.at("turned_copied", max(0, n - 1)) > 0:
                            pe.wait_ge(S["turned_copied"], st.at("turned_copied", max(0, n - 1)))
                        for k in range(b - a):
                            mm = pe.transpose(turn_ps[n % 2][:, k * P:(k + 1) * P], SG[:, n % 4, k * P:(k + 1) * P], IDENT[:, :])
                        mm.then_inc(S["probs_turned"], 1)
                    if i > DEPTH:
                        n = i - DEPTH - 1
                        h, c, t = items[n]
                        a, b = spans(mode, t)
                        pe.wait_ge(S["turned_copied"], st.at("turned_copied", n + 1))
                        if c + t == 0:
                            pe.wait_ge(bank_free[st.bank(h)], st.use(h))
                        rows, at = P if mode == "diff" else HD, slice(t * P, (t + 1) * P)
                        for kt in range(a, b):
                            mm = pe.matmul(ps[st.bank(h)][0:rows, at], values(h, kt), pt[:, n % TURNED, (kt - a) * P:(kt - a + 1) * P],
                                           start=kt == a and c == 0, stop=kt == b - 1 and c == st.comps - 1,
                                           skip_group_check=True)
                        mm.then_inc(S["item_multiplied"], 1)

            def out_y(st):
                n = st.units // 4
                def body(r):
                    for j in range(st.units):
                        k0 = (j % n) * BLOCKS
                        tile(st, j, j // n, r, pair[st.src], min(BLOCKS, st.kt - k0), k0,
                             st.op if isinstance(r, int) and r == 0 and j < n else None, j % n == 0, j % n == n - 1)
                repeat(pe, st, body, 1)

            def loop_h(st):
                def body(r):
                    first = isinstance(r, int) and r == 0
                    for j in range(4):
                        tile(st, j, j, r, pair["H"], DT, ready=st.op if first and j == 0 and st.norm is not None else None)
                        if first and j == 0 and st.norm is not None:
                            norm(st.norm)
                repeat(pe, st, body, 1)

            def qkv(st):
                def body(r):
                    first = isinstance(r, int) and r == 0 and st.norm is not None
                    for m in range(st.units // 2):
                        weights(st.unit(2 * m + 1, r))
                        s0 = st.unit(2 * m) % SLOTS
                        for s in range(ST):
                            k = 2 * m + s // 2
                            if s % 2 == 0:
                                pe.wait_ge(bank_free[st.bank(k)], st.use(k, r))
                            o = ps[st.bank(k)][:, (s % 2) * 2 * P:(s % 2 + 1) * 2 * P].rearrange("p (a c) -> p a c", a=2)
                            for t in range(DT):
                                if first and m == 0 and s == 0:
                                    pe.wait_ge(S["operand_ready"], st.op + t + 1)
                                at = slice(s * P, (s + 1) * P)
                                whi, wlo = (w[:, s0:s0 + 2, t * P:(t + 1) * P] for w in (WHI, WLO))
                                pe.matmul(o, HH[:, t, at], whi, start=t == 0, stop=False)
                                pe.matmul(o, HH[:, t, at], wlo, start=False, stop=False)
                                mm = pe.matmul(o, HL[:, t, at], whi, start=False, stop=t == DT - 1)
                            if s == 1:
                                mm.then_inc(S["part_multiplied"], 1)
                        mm.then_inc(unit_used, 2)
                        if first and m == 0:
                            norm(st.norm)
                repeat(pe, st, body, 1)

            def qk_norm(st):
                for f in range(16):
                    pe.wait_ge(bank_free[st.bank(f)], st.use(f))
                    pe.wait_ge(S["qk_normed"], st.at("qk_normed", (f // 4) * 4 + 4))
                    c0 = f * P
                    for s in range(ST):
                        mm = pe.transpose(ps[st.bank(f)][:, s * P:(s + 1) * P], QKV[:, s, c0:c0 + P], IDENT[:, :])
                    mm.then_inc(S["qk_turned"], 1)

            def sub_norm(st):
                pe.wait_ge(S["out_square_ready"], st.at("out_square_ready", 4))
                pe.wait_ge(S["turned_copied"], st.at("turned_copied", 0))
                for h in range(DIFF_H):
                    for s in range(ST):
                        mm = pe.matmul(stat_ps[:, h * ST + s:h * ST + s + 1], PT2[:, h, s * P:(s + 1) * P], ONES[:, 0:1],
                                       start=True, stop=True)
                mm.then_inc(S["out_squares_summed"], 1)
                pe.wait_ge(S["out_factors_ready"], st.at("out_factors_ready", 1))
                for h in range(DIFF_H):
                    pe.wait_ge(bank_free[st.bank(h)], st.use(h))
                    for s in range(ST):
                        mm = pe.transpose(ps[st.bank(h)][:, s * P:(s + 1) * P],
                                          RC["Y"][:, h * ST + s:h * ST + s + 1].to_broadcast([P, P]), IDENT[:, :])
                    mm.then_inc(S["out_factors_spread"], 1)

            def ple_in(st):
                pe.wait_ge(S["ple_loaded"], st.at("ple_loaded", 16))
                for t in range(2):
                    if st.use(t) > 0:
                        pe.wait_ge(bank_free[st.bank(t)], st.use(t))
                    for s in range(ST):
                        mm = pe.transpose(ps[st.bank(t)][:, s * P:(s + 1) * P], PROWS[:, s, t * P:(t + 1) * P], IDENT[:, :])
                    mm.then_inc(S["ple_turned"], 1)

            def ple(st):
                def body(r):
                    first = isinstance(r, int) and r == 0
                    for j in range(4):
                        if j % 2 == 0:
                            tile(st, j, j, r, (POH, POL), 2, ready=st.op if first else None)
                        else:
                            tile(st, j, j, r, pair["H"], DT, ready=st.op + 2 if first else None)
                repeat(pe, st, body, 1)

            def rec_lru(st):
                k = 0
                for j in range(2):
                    weights(st.unit(j))
                    s = st.unit(j) % SLOTS
                    for n in range(DT):
                        pe.wait_ge(bank_free[st.bank(k)], st.use(k))
                        if j == 0:
                            pe.wait_ge(S["operand_ready"], st.op + n + 1)
                        three(ps[st.bank(k)][:, :], (slice(None), s, slice(n * P, (n + 1) * P)), XRH[:, n, :], XRL[:, n, :],
                              True, True).then_inc(S["part_multiplied"] if n < DT - 1 else unit_used, 1)
                        k += 1
                for n in range(DT):
                    tile(st, 2 + n, 16 + n, 0, pair["H"], DT)

            def out(st):
                for k in range(DT):
                    s, hf = k // 2, k % 2
                    pe.wait_ge(bank_free[st.bank(k)], st.use(k))
                    if k == 0:
                        for b in range(BANKS):
                            pe.wait_ge(bank_free[st.bank(b)], st.use(b))
                    for c in range(4):
                        mm = pe.transpose(ps[st.bank(k)][:, c * P:(c + 1) * P], X[:, hf * 4 + c, s * P:(s + 1) * P], IDENT[:, :])
                    mm.then_inc(S["rows_turned"], 1)

            does = dict(init=init, fourier=fourier, branch=branch, proj=proj, mla_heads=mla_heads, rope=rope,
                        attention=attention, out_y=out_y, residual=out_y, swiglu=loop_h, conv_ffn=loop_h, rec_conv=loop_h, qkv=qkv, qk_norm=qk_norm, sub_norm=sub_norm, ple_in=ple_in, ple=ple,
                        rec_lru=rec_lru, out=out)
            for st in STEPS:
                if st.kind == "norm" and st.where == "now":
                    norm(st)
                elif st.kind in does:
                    does[st.kind](st)

        @block.scalar
        def _(act):
            def split_of(st, j, r=0):
                n = st.unit(j) + AHEAD
                s = n % SLOTS
                if isinstance(r, int) and n + r * st.units >= NU:
                    return
                act.wait_ge(raw[s], 16 * (n // SLOTS + 1) + r * (16 * (st.units // SLOTS)) if st.units % SLOTS == 0
                            else 16 * (n // SLOTS + 1))
                act.activation(WHI[:, s, :], WRAW[:, s, :], ACT.Copy).then_inc(wt_hi, 1)

            def square(st, src, i, r=0, done="square_ready", slot=None):
                if st.at("square_added", i - 1) > 0:
                    act.wait_ge(S["square_added"], st.at("square_added", i - 1, r))
                act.activation(SQ[:, i % 2 if slot is None else slot, :], src, ACT.Square)\
                   .then_inc(S[done] if isinstance(done, str) else done, 1)

            def init(st):
                act.dma_start(CONST[:, :], consts).then_inc(const_in, 16)
                act.dma_start(XROWS[:, :, :], xin.rearrange("o (s p) d -> p (o s) d", p=P)).then_inc(x_in, 16)
                for dst, src in ((COLS[:, :], cols), (TDRAW[:, 0, :], dftc[0]), (TDRAW[:, 1, :], dftc[1]),
                                 (POSI[:, :], posi.broadcast_to([P, SEQ])), (POSC_I[:, :], posc), (GM[:, :], gmask)):
                    act.dma_start(dst, src).then_inc(ld, 16)
                act.wait_ge(ld, 16 * LOADS)
                act.activation(TDH[:, :, :], TDRAW[:, :, :], ACT.Copy).then_inc(S["dft_hi_ready"], 1)

            def tables1(st):
                act.wait_ge(S["table_stepped"], st.at("table_stepped", 3))
                for t in range(ST):
                    a, b = spans("gqa", t)
                    act.activation(GD[:, t, 0:(b - a) * P], POSF[:, a * P:b * P], ACT.Abs, bias=POSC[:, t:t + 1])\
                       .then_inc(S["table_looked_up"], 1)
                act.wait_ge(S["table_stepped"], st.at("table_stepped", 11))
                act.activation(SIN[:, :], ANG[:, :], ACT.Sin).then_inc(S["table_looked_up"], 1)
                act.activation(TURN[:, :], ANG[:, :], ACT.Abs).then_inc(S["table_looked_up"], 1)
                act.wait_ge(S["table_stepped"], st.at("table_stepped", 12))
                act.activation(COS[:, :], TURN[:, :], ACT.Sin).then_inc(S["table_looked_up"], 1)

            def operand(st):
                src, (hi, lo) = source[st.src], pair[st.dst]
                if st.made is not None and st.made.kind == "init":
                    for b in range(BANKS):
                        act.wait_ge(bank_free[b], DT // BANKS)
                if st.made is not None and st.made.kind == "proj":
                    for k in range(4):
                        act.wait_ge(bank_free[st.made.bank(k)], st.made.use(k) + 1)
                for i in range(st.n):
                    t = st.t + i
                    if st.y:
                        act.wait_ge(S["residual_updated"], st.at("residual_updated", i + 1))
                    scale = dict(scale=col(st.gain, i)) if st.gain else {}
                    act.activation(hi[:, t, :], src[:, t, :], ACT.Copy, **scale).then_inc(S["operand_hi_ready"], 1)
                    if st.stat:
                        square(st, src[:, t, :], i)

            def norm(st):
                act.wait_ge(S["factors_spread"], st.at("factors_spread", 1))
                act.activation(RB[st.rb][:, :], stat_ps[:, :], ACT.Copy).then_inc(S["factor_rows_ready"], 1)

            def fourier(st):
                for part in range(2):
                    act.dma_start(DFT[:, part, :, :], dft[part].rearrange("(s p) n -> p s n", p=P)).then_inc(S["dft_loaded"], 16)
                if st.u0 == 0:
                    for u in range(AHEAD):
                        act.wait_ge(raw[u], 16)
                        act.activation(WHI[:, u, :], WRAW[:, u, :], ACT.Copy).then_inc(wt_hi, 1)
                n_cols = 0
                for what, g in FOURIER_ORDER:
                    if what == "rows":
                        if g >= 2:
                            act.wait_ge(S["tokens_transformed"], st.at("tokens_transformed", 2 * (g - 1)))
                        for s in range(ST):
                            k = fourier_tile("rows", g, s)
                            act.wait_ge(S["channels_transformed"], st.at("channels_transformed", g * ST + s + 1))
                            act.activation(PG[:, g % 2, s, :], ps[st.bank(k)][:, :], ACT.Copy, scale=RC["X"][:, s:s + 1])\
                               .then_inc(bank_free[st.bank(k)], 1)
                    elif what == "cols":
                        for c in range(2):
                            k = fourier_tile("cols", g, c)
                            act.wait_ge(S["tokens_transformed"], st.at("tokens_transformed", n_cols + 1))
                            act.wait_ge(S["operand_ready"], st.at("operand_ready", n_cols - 1))
                            act.activation(TM[:, c, :], ps[st.bank(k)][:, :], ACT.Copy).then_inc(bank_free[st.bank(k)], 1)
                            act.wait_ge(bank_free[st.bank(k)], st.use(k) + 1)
                            act.activation(OBH[:, n_cols, :], TM[:, c, :], ACT.Copy).then_inc(S["operand_hi_ready"], 1)
                            n_cols += 1

            def branch(st):
                def body(r):
                    for j in range(4):
                        if j % 2 == 0:
                            act.wait_ge(bank_free[st.bank(j)], st.use(j, r) + 1)
                            act.activation(SG[:, j // 2, :], SG[:, j // 2, :], ACT.Sigmoid).then_inc(S["gate_ready"], 1)
                        elif st.last:
                            act.wait_ge(S["product_ready"], st.at("product_ready", 1 + j // 2, r))
                            act.activation(tile_of(r * 2 + j // 2, MGH), tile_of(r * 2 + j // 2, MG), ACT.Copy)\
                               .then_inc(S["operand_hi_ready"], 1)
                        split_of(st, j, r)
                repeat(act, st, body)

            def proj(st):
                for j in range(11):
                    act.wait_ge(unit_used, st.unit(j))
                    split_of(st, j)
                act.wait_ge(S["values_turned"], st.at("values_turned", 1))
                act.activation(VR[:, :, :], ps[st.bank(11)][:, :].rearrange("p (a c) -> p a c", a=ST), ACT.Copy)\
                   .then_inc(bank_free[st.bank(11)], 1)

            def mla_heads(st):
                for j in range(4):
                    act.wait_ge(unit_used, st.unit(j))
                    split_of(st, j)
                act.wait_ge(unit_used, st.unit(4))
                split_of(st, 4)
                for t in range(ST):
                    k = 2 * 4 + MLA_H + t
                    if t < ST - 1:
                        act.wait_ge(S["part_multiplied"], st.at("part_multiplied", 4 + MLA_H + t + 1))
                    else:
                        act.wait_ge(unit_used, st.unit(4) + 1)
                    act.activation(VA[:, t, :], ps[st.bank(k)][:, :], ACT.Copy, scale=RC["K"][:, t:t + 1])\
                       .then_inc(bank_free[st.bank(k)], 1)

            def rope(st):
                act.wait_ge(S["rope_added"], st.at("rope_added", 1))
                src = KRAW[MLA_NOPE:MLA_QK, :].rearrange("p (o s) -> p o s", o=1).to_broadcast([MLA_ROPE, MLA_H, SEQ])
                act.activation(KA[MLA_NOPE:MLA_QK, :, :], src, ACT.Copy).then_inc(S["rope_keys_spread"], 1)

            def attention(st):
                mode = st.mode
                pt = PT if mode in ("gqa", "mla") else PT2
                items = attention_items(st)
                hi = pair[st.out][0] if mode != "diff" else None
                for i in range(len(items) + DEPTH):
                    if i < len(items):
                        h, c, t = items[i]
                        a, b = spans(mode, t)
                        w = (b - a) * P
                        s = i % 4
                        act.wait_ge(S["neg_max_ready"], st.at("neg_max_ready", i + 1))
                        if mode == "mla":
                            if i >= 4:
                                act.wait_ge(S["probs_turned"], st.at("probs_turned", i - 3))
                            act.activation(SG[:, s, 0:w], score_ps[i % 2][:, 0:w], ACT.Exp, bias=NM[:, s:s + 1],
                                           scale=MLA_QK ** -0.5, accum_out=SM[:, s:s + 1]).then_inc(S["exp_ready"], 1)
                        else:
                            act.activation(SG[:, s, 0:w], SG[:, s, 0:w], ACT.Exp, bias=NM[:, s:s + 1],
                                           accum_out=SM[:, s:s + 1]).then_inc(S["exp_ready"], 1)
                        if mode == "gqa":
                            act.activation(ES[:, s:s + 1], col(f"gqa_sink{st.l}", h), ACT.Exp, bias=NM[:, s:s + 1]).then_inc(S["sink_exp_ready"], 1)
                    if i >= DEPTH:
                        n = i - DEPTH
                        h, c, t = items[n]
                        a, b = spans(mode, t)
                        act.wait_ge(S["probs_turned"], st.at("probs_turned", n + 1))
                        if n >= TURNED:
                            act.wait_ge(S["item_multiplied"], st.at("item_multiplied", n - TURNED + 1))
                        act.activation(pt[:, n % TURNED, 0:(b - a) * P], turn_ps[n % 2][:, 0:(b - a) * P], ACT.Copy)\
                           .then_inc(S["turned_copied"], 1)
                    if mode != "diff":
                        for p in range(st.heads // 2):
                            if i == min((2 * p + 2) * ST + DEPTH + 3, len(items) + DEPTH - 1):
                                act.wait_ge(bank_free[st.bank(2 * p)], st.use(2 * p) + 1)
                                act.wait_ge(bank_free[st.bank(2 * p + 1)], st.use(2 * p + 1) + 1)
                                act.activation(hi[:, p, :], TM[:, p % 2, :], ACT.Copy).then_inc(S["operand_hi_ready"], 1)

            def out_y(st):
                n = st.units // 4
                def body(r):
                    for j in range(st.units):
                        k = j // n
                        act.wait_ge(unit_used, st.unit(j if j % n == n - 1 else j - 1, r) + 1)
                        if j % n == n - 1:
                            act.wait_ge(S["square_added"], st.at("square_added", k - 1, r))
                            act.activation(tile_of(r * 4 + k, source[st.y]), ps[st.bank(k)][:, :], ACT.Copy)
                            act.activation(SQ[:, k % 2, :], ps[st.bank(k)][:, :], ACT.Square).then_inc(bank_free[st.bank(k)], 1)
                        split_of(st, j, r)
                repeat(act, st, body)

            def residual(st):
                n = st.units // 4
                def body(r):
                    for j in range(st.units):
                        k = j // n
                        if j % n == n - 1 and st.gain:
                            act.wait_ge(bank_free[st.bank(k)], st.use(k, r) + 1)
                            act.wait_ge(S["square_added"], st.at("square_added", k - 1, r))
                            t = r * 4 + k
                            act.activation(tile_of(t, HH), tile_of(t, X), ACT.Copy, scale=col(st.gain, t)).then_inc(S["operand_hi_ready"], 1)
                            act.activation(SQ[:, k % 2, :], tile_of(t, X), ACT.Square).then_inc(S["square_ready"], 1)
                        else:
                            act.wait_ge(unit_used, st.unit(j, r))
                        split_of(st, j, r)
                repeat(act, st, body, 0 if st.u0 + st.reps * st.units + AHEAD < NU else st.reps)

            def swiglu(st):
                def body(r):
                    for j in range(4):
                        if j % 2 == 0:
                            act.wait_ge(bank_free[st.bank(j)], st.use(j, r) + 1)
                            act.activation(SG[:, j // 2, :], SG[:, j // 2, :], ACT.Silu).then_inc(S["gate_ready"], 1)
                        else:
                            act.wait_ge(S["product_ready"], st.at("product_ready", 1 + j // 2, r))
                            act.activation(tile_of(r * 2 + j // 2, F1H), TM[:, j // 2, :], ACT.Copy).then_inc(S["operand_hi_ready"], 1)
                        split_of(st, j, r)
                repeat(act, st, body)

            def ple_in(st):
                act.dma_start(PROWS[:, :, :], pin[st.l].rearrange("o (s p) d -> p (o s) d", p=P)).then_inc(S["ple_loaded"], 16)
                for t in range(2):
                    act.wait_ge(S["ple_turned"], st.at("ple_turned", t + 1))
                    act.activation(TM[:, t, :], ps[st.bank(t)][:, :], ACT.Copy).then_inc(bank_free[st.bank(t)], 1)
                    act.wait_ge(bank_free[st.bank(t)], st.use(t) + 1)
                    act.activation(POH[:, t, :], TM[:, t, :], ACT.Copy).then_inc(S["operand_hi_ready"], 1)

            def ple(st):
                def body(r):
                    for j in range(4):
                        k = j // 2
                        act.wait_ge(unit_used, st.unit(j, r) + 1)
                        if j % 2 == 0:
                            act.wait_ge(S["product_ready"], st.at("product_ready", k - 1, r))
                        act.activation(SG[:, j, :], ps[st.bank(j)][:, :], ACT.Sigmoid if j % 2 else ACT.Copy)\
                           .then_inc(bank_free[st.bank(j)], 1)
                        if j % 2:
                            act.wait_ge(S["product_ready"], st.at("product_ready", k + 1, r))
                            square(st, tile_of(r * 2 + k, YP), k, r)
                        split_of(st, j, r)
                repeat(act, st, body)

            def tables2(st):
                act.dma_start(DIL[:, :, :], dil).then_inc(S["tables_loaded"], 16)
                act.dma_start(LAMV[:, :, :], lamv.broadcast_to([P, 4 * HD]).rearrange("p (a c) -> p a c", a=4)).then_inc(S["tables_loaded"], 16)
                act.wait_ge(S["tables_stepped"], st.at("tables_stepped", 2))
                act.activation(LE[:, :], LT[:, :], ACT.Exp).then_inc(S["lambda_exp_ready"], 1)

            def qkv(st):
                def body(r):
                    for m in range(st.units // 2):
                        split_of(st, 2 * m, r)
                        for s in range(ST):
                            k = 2 * m + s // 2
                            if s == 0:
                                act.wait_ge(S["part_multiplied"], st.at("part_multiplied", m + 1, r))
                            if s == 2:
                                act.wait_ge(unit_used, st.unit(2 * m + 1, r) + 1)
                            c = (st.n + r * 2 + m) * 2 * P
                            dst = QKV[:, s, c:c + 2 * P] if isinstance(c, int) else QKV[:, s, bass.ds(c, 2 * P)]
                            a = act.activation(dst, ps[st.bank(k)][:, (s % 2) * 2 * P:(s % 2 + 1) * 2 * P], ACT.Copy,
                                               scale=RC["X"][:, s:s + 1])
                            if s % 2:
                                a.then_inc(bank_free[st.bank(k)], 1)
                        split_of(st, 2 * m + 1, r)
                        if st.n:
                            if m == 0:
                                for k in range(BANKS):
                                    act.wait_ge(bank_free[st.bank(k)], st.use(k))
                            for n in range(4 * m, 4 * m + 4):
                                if n >= 2:
                                    act.wait_ge(S["qk_square_summed"], st.at("qk_square_summed", n - 1))
                                c0 = (n // 4) * SEQ
                                act.activation(SQ[:, n % 2, :], QKV[:, n % 4, c0:c0 + SEQ], ACT.Square).then_inc(S["qk_square_ready"], 1)
                repeat(act, st, body)

            def qk_norm(st):
                for k in range(BANKS):
                    act.wait_ge(bank_free[k], st.t0 // BANKS)
                act.wait_ge(S["qk_factors_stepped"], st.at("qk_factors_stepped", 1))
                act.activation(VQ[:, :], VQ[:, :], ACT.Sqrt).then_inc(S["qk_factors_stepped"], 1)
                for f in range(16):
                    act.wait_ge(S["qk_turned"], st.at("qk_turned", f + 1))
                    g = (GQ[:, 0:1], col("a_k_norm_20"), GQ[:, 1:2], col("b_k_norm_20"))[f // 4]
                    act.activation(HQ[:, f, :], ps[st.bank(f)][:, :], ACT.Copy, scale=g).then_inc(bank_free[st.bank(f)], 1)

            def sub_norm(st):
                for h in range(DIFF_H):
                    act.wait_ge(bank_free[st.att.bank(h)], st.att.use(h) + 1)
                    act.activation(PT2[:, h, :], UB[:, h, :], ACT.Square).then_inc(S["out_square_ready"], 1)
                for h in range(DIFF_H):
                    act.wait_ge(bank_free[st.bank(h)], st.use(h) + 1)
                    act.activation(O2H[:, 4 + h, :], UB[:, h, :], ACT.Copy).then_inc(S["operand_hi_ready"], 1)

            def conv_tail(st, k, r, w, bias, taps):
                act.wait_ge(bank_free[st.bank(k)], st.use(k, r) + 1)
                act.activation(SG[:, k, :], U[:, k, taps - 1:taps - 1 + SEQ], ACT.Identity, scale=w, bias=bias).then_inc(S["conv_begun"], 1)

            def conv_ffn(st):
                def body(r):
                    for j in range(4):
                        t = r * 2 + j // 2 + (FT2 if j % 2 else 0)
                        conv_tail(st, j, r, col(f"ffn_conv_w_2{st.l}_2", t), col(f"ffn_conv_b_2{st.l}", t), 3)
                        if j % 2 == 0:
                            act.wait_ge(S["conv_tap_added"], st.at("conv_tap_added", 2 * j + 2, r))
                            act.activation(SG[:, j, :], SG[:, j, :], ACT.Gelu_apprx_tanh).then_inc(S["gate_ready"], 1)
                        else:
                            act.wait_ge(S["product_ready"], st.at("product_ready", 1 + j // 2, r))
                            act.activation(tile_of(r * 2 + j // 2, F2H), SG[:, j, :], ACT.Copy).then_inc(S["operand_hi_ready"], 1)
                        split_of(st, j, r)
                repeat(act, st, body)

            def rec_conv(st):
                def body(r):
                    for j in range(4):
                        t = r * 4 + j
                        conv_tail(st, j, r, col("rec_conv_w_20_3", t), col("rec_conv_b_20", t), 4)
                        act.wait_ge(S["conv_tap_added"], st.at("conv_tap_added", 3 * j + 3, r))
                        act.activation(tile_of(t, XRH), tile_of(t, XR), ACT.Copy).then_inc(S["operand_hi_ready"], 1)
                        split_of(st, j, r)
                repeat(act, st, body)

            def rec_lru(st):
                act.wait_ge(S["decay_abs_ready"], st.at("decay_abs_ready", 1))
                act.activation(LR[:, 1, :], LR[:, 0, :], ACT.Exp, scale=-1.0).then_inc(S["decay_exp_ready"], 1)
                for j in range(2):
                    dst, bias = ((RT, "rec_gate_a_b_20"), (IT, "rec_gate_x_b_20"))[j]
                    for n in range(DT):
                        k = j * DT + n
                        if n < DT - 1:
                            act.wait_ge(S["part_multiplied"], st.at("part_multiplied", j * (DT - 1) + n + 1))
                        else:
                            act.wait_ge(unit_used, st.unit(j) + 1)
                        act.activation(dst[:, n, :], ps[st.bank(k)][:, :], ACT.Sigmoid, bias=col(bias, n))\
                           .then_inc(bank_free[st.bank(k)], 1)
                    split_of(st, j)
                act.wait_ge(S["decay_stepped"], st.at("decay_stepped", LP_STEPS))
                for n in range(DT):
                    if n == 0:
                        act.wait_ge(bank_free[st.bank(15)], st.use(15) + 1)
                    act.activation(DECAY[:, n, :], RT[:, n, :], ACT.Exp, scale=LR[:, 3, n:n + 1]).then_inc(S["decay_ready"], 1)
                    act.activation(RT[:, n, :], RT[:, n, :], ACT.Tanh, scale=LR[:, 3, n:n + 1]).then_inc(S["tanh_ready"], 1)
                    if n >= 2:
                        act.wait_ge(S["decay_rest_ready"], st.at("decay_rest_ready", n - 1))
                    act.wait_ge(S["decay_ready"], st.at("decay_ready", n + 1))
                    act.activation(SQ[:, n % 2, :], DECAY[:, n, :], ACT.Square).then_inc(S["decay_squared"], 1)
                    if n in (1, 4, 7):
                        split_of(st, 2 + n // 3)
                for n in range(DT):
                    act.wait_ge(S["decay_rest_ready"], st.at("decay_rest_ready", n + 1))
                    act.activation(RT[:, n, :], RT[:, n, :], ACT.Sqrt, scale=-1.0).then_inc(S["root_ready"], 1)
                split_of(st, 5)
                for n in range(DT + 1):
                    if n < DT:
                        act.wait_ge(bank_free[st.bank(16 + n)], st.use(16 + n) + 1)
                        act.activation(GG[:, n, :], GG[:, n, :], ACT.Gelu_apprx_tanh).then_inc(S["gate_ready"], 1)
                    if n:
                        act.wait_ge(S["product_ready"], st.at("product_ready", n))
                        act.activation(ROH[:, n - 1, :], GG[:, n - 1, :], ACT.Copy).then_inc(S["operand_hi_ready"], 1)
                    if n < 4:
                        split_of(st, 6 + n)

            def out(st):
                for k in range(DT):
                    s, hf = k // 2, k % 2
                    act.wait_ge(S["rows_turned"], st.at("rows_turned", k + 1))
                    act.activation(YROWS[:, s, hf * SEQ:(hf + 1) * SEQ], ps[st.bank(k)][:, :], ACT.Copy)\
                       .then_inc(bank_free[st.bank(k)], 1)
                    if hf:
                        act.wait_ge(bank_free[st.bank(k - 1)], st.use(k - 1) + 1)
                        act.wait_ge(bank_free[st.bank(k)], st.use(k) + 1)
                        act.dma_start(out_v[s], YROWS[:, s, :]).then_inc(S["output_stored"], 16)
                act.wait_ge(S["output_stored"], 16 * ST)

            out_v = out_.rearrange("o (s p) d -> (o s) p d", p=P)
            does = dict(init=init, tables1=tables1, operand=operand, norm=norm, fourier=fourier, branch=branch, proj=proj, mla_heads=mla_heads,
                        rope=rope, attention=attention, out_y=out_y, residual=residual, swiglu=swiglu, ple_in=ple_in,
                        ple=ple, tables2=tables2, qkv=qkv, qk_norm=qk_norm, sub_norm=sub_norm, conv_ffn=conv_ffn,
                        rec_conv=rec_conv, rec_lru=rec_lru, out=out)
            for st in STEPS:
                if st.kind in does:
                    does[st.kind](st)

        @block.vector
        def _(dve):
            def init(st):
                dve.memset(ONES[:, :], 1.0).then_inc(cst, 1)
                dve.memset(NEGH[:, :], -0.5).then_inc(cst, 1)
                dve.memset(MX[:, :], 0.0).then_inc(cst, 1)
                dve.wait_ge(ld, 16 * LOADS)
                for t in range(DT):
                    dve.wait_ge(S["rows_turned"], st.at("rows_turned", t + 1))
                    dve.tensor_copy(X[:, t, :], ps[st.bank(t)][:, :]).then_inc(bank_free[st.bank(t)], 1)
                dve.wait_ge(S["dft_hi_ready"], st.at("dft_hi_ready", 1))
                dve.tensor_tensor(TDL[:, :, :], TDRAW[:, :, :], TDH[:, :, :].bitcast(F32), ALU.subtract).then_inc(S["dft_lo_ready"], 1)

            def tables1(st):
                n = 0

                def step(ins):
                    nonlocal n
                    ins.then_inc(S["table_stepped"], 1)
                    n += 1
                    dve.wait_ge(S["table_stepped"], st.at("table_stepped", n))
                step(dve.tensor_copy(POSF[:, :], POSI[:, :]))
                step(dve.tensor_copy(POSC[:, :], POSC_I[:, :]))
                step(dve.tensor_scalar(POSC[:, :], POSC[:, :], -1.0, None, ALU.mult))
                magic = 1.5 * 2.0 ** 23
                c1 = 6.28125
                c2 = float(np.float32(int((2 * np.pi - c1) * 2 ** 20)) / np.float32(2 ** 20))
                c3 = float(np.float32(2 * np.pi - c1 - c2))
                step(dve.tensor_scalar(ANG[:, :], POSF[:, :], INVF[:, 0:1], None, ALU.mult))
                step(dve.tensor_scalar(TURN[:, :], ANG[:, :], float(np.float32(1 / (2 * np.pi))), None, ALU.mult))
                step(dve.tensor_scalar(TURN[:, :], TURN[:, :], magic, None, ALU.add))
                step(dve.tensor_scalar(TURN[:, :], TURN[:, :], magic, None, ALU.subtract))
                for c in (c1, c2, c3):
                    step(dve.scalar_tensor_tensor(ANG[:, :], TURN[:, :], -c, ANG[:, :], ALU.mult, ALU.add))
                step(dve.tensor_scalar(ANG[:, :], ANG[:, :], 3.1415925, -3.1415925, ALU.min, ALU.max))
                dve.wait_ge(S["table_looked_up"], st.at("table_looked_up", ST + 2))
                step(dve.tensor_scalar(TURN[:, :], TURN[:, :], -1.0, float(np.float32(np.pi / 2)), ALU.mult, ALU.add))
                dve.wait_ge(S["table_looked_up"], st.at("table_looked_up", ST + 3))
                for t in range(ST):
                    a, b = spans("gqa", t)
                    at = (a - t + 1) * P
                    step(dve.tensor_tensor(GD[:, t, 0:(b - a) * P], GD[:, t, 0:(b - a) * P], GM[:, at:at + (b - a) * P], ALU.add))

            def operand(st):
                src, (hi, lo) = source[st.src], pair[st.dst]
                if st.y:
                    dve.wait_ge(S["factor_rows_ready"], st.at("factor_rows_ready", 0))
                    dve.wait_ge(S["operand_ready"], st.at("operand_ready", 0))
                for i in range(st.n + 1):
                    if st.y and i < st.n:
                        dve.scalar_tensor_tensor(TM[:, i % 2, :], source[st.y][:, i, :], col(st.gy, i), RBY[:, :], ALU.mult,
                                                 ALU.mult).then_inc(S["update_ready"], 1)
                        dve.wait_ge(S["update_ready"], st.at("update_ready", i + 1))
                        dve.tensor_tensor(X[:, i, :], X[:, i, :], TM[:, i % 2, :], ALU.add).then_inc(S["residual_updated"], 1)
                    if i and not on_pool(st, i - 1):
                        t = st.t + i - 1
                        if i > 1 and on_pool(st, i - 2):
                            dve.wait_ge(S["operand_ready"], st.at("operand_ready", i - 1))
                        dve.wait_ge(S["operand_hi_ready"], st.at("operand_hi_ready", i))
                        h = hi[:, t, :].bitcast(F32)
                        if st.gain:
                            dve.scalar_tensor_tensor(lo[:, t, :], src[:, t, :], col(st.gain, i - 1), h, ALU.mult, ALU.subtract)\
                               .then_inc(S["operand_ready"], 1)
                        else:
                            dve.tensor_tensor(lo[:, t, :], src[:, t, :], h, ALU.subtract).then_inc(S["operand_ready"], 1)

            def norm(st):
                dve.wait_ge(S["norm_summed"], st.at("norm_summed", 1))
                if st.at("factor_rows_ready", 0) > 0:
                    dve.wait_ge(S["factor_rows_ready"], st.at("factor_rows_ready", 0))
                dve.tensor_scalar(VAR[:, 0:ST], stat_ps[:, 0:ST], 1.0 / st.width, EPS, ALU.mult, ALU.add).then_inc(S["mean_square_ready"], 1)

            def zero(st):
                dve.memset(ACC[:, :], 0.0).then_inc(S["sum_cleared"], 1)

            def add_square(st, k, r, slot):
                dve.wait_ge(S["square_added"], st.at("square_added", k, r))
                dve.wait_ge(S["sum_cleared"], st.at("sum_cleared", 0))
                dve.tensor_tensor(ACC[:, :], ACC[:, :], SQ[:, slot, :], ALU.add).then_inc(S["square_added"], 1)

            def remainder(st, dst, src, k, r, gain=None):
                hi, lo = dst
                dve.wait_ge(S["operand_hi_ready"], st.at("operand_hi_ready", k, r))
                if gain is None:
                    dve.tensor_tensor(lo, src, hi.bitcast(F32), ALU.subtract).then_inc(S["operand_ready"], 1)
                else:
                    dve.scalar_tensor_tensor(lo, src, gain, hi.bitcast(F32), ALU.mult, ALU.subtract).then_inc(S["operand_ready"], 1)

            def fourier(st):
                for n in range(2 * FGROUPS):
                    remainder(st, (OBH[:, n, :], OBL[:, n, :]), TM[:, n % 2, :], n + 1, 0)

            def scaled(st, k, r, dst, src=None, rb=None, const=None):
                src = ps[st.bank(k)][:, :] if src is None else src
                rb = RBX[:, :] if rb is None else rb
                if const is None:
                    ins = dve.tensor_tensor(dst, src, rb, ALU.mult)
                else:
                    ins = dve.scalar_tensor_tensor(dst, src, const, rb, ALU.mult, ALU.mult)
                ins.then_inc(bank_free[st.bank(k)], 1)

            def branch(st):
                dve.wait_ge(S["factor_rows_ready"], st.at("factor_rows_ready", 0))
                def body(r):
                    for j in range(4):
                        dve.wait_ge(unit_used, st.unit(j, r) + 1)
                        if j % 2 == 0:
                            scaled(st, j, r, SG[:, j // 2, :])
                            continue
                        t = r * 2 + j // 2
                        dve.wait_ge(S["gate_ready"], st.at("gate_ready", 1 + j // 2, r))
                        if st.first:
                            scaled(st, j, r, tile_of(t, MG), rb=SG[:, j // 2, :])
                            continue
                        scaled(st, j, r, TM[:, j // 2, :], rb=SG[:, j // 2, :])
                        dve.wait_ge(bank_free[st.bank(j)], st.use(j, r) + 1)
                        dve.tensor_tensor(tile_of(t, MG), tile_of(t, MG), TM[:, j // 2, :], ALU.add).then_inc(S["product_ready"], 1)
                        if st.last:
                            remainder(st, (tile_of(t, MGH), tile_of(t, MGL)), tile_of(t, MG), 1 + j // 2, r)
                repeat(dve, st, body)

            def proj(st):
                dst = [(CQ[:, t, :], None) for t in range(4)] + [(QC[:, t, :], HD ** -0.5) for t in range(4)]
                dst += [(K2[:, 0, :], None), (VCT[:, :], None)]
                if st.at("factor_rows_ready", 0) > 0:
                    dve.wait_ge(S["factor_rows_ready"], st.at("factor_rows_ready", 0))
                for k, (d, c) in enumerate(dst):
                    dve.wait_ge(unit_used, st.unit(k) + 1)
                    scaled(st, k, 0, d, const=c)
                dve.wait_ge(unit_used, st.unit(10) + 1)
                scaled(st, 10, 0, KRAW[MLA_NOPE:MLA_QK, :], ps[st.bank(10)][0:MLA_ROPE, :], RBX[0:MLA_ROPE, :])
                dve.wait_ge(bank_free[st.bank(8)], st.use(8) + 1)
                for h in range(2):
                    dve.tensor_copy(K2[half(h), 1, :], K2[half(1 - h), 0, :]).then_inc(S["keys_copied"], 1)

            def mla_heads(st):
                for h in range(MLA_H):
                    if h % 2 == 0:
                        dve.wait_ge(S["part_multiplied"], st.at("part_multiplied", h // 2 + 1))
                    else:
                        dve.wait_ge(unit_used, st.unit(h // 2) + 1)
                    scaled(st, h, 0, QA[0:MLA_QK, h, :], ps[st.bank(h)][0:MLA_QK, :], RBQ[0:MLA_QK, :])
                for h in range(MLA_H):
                    k = MLA_H + h
                    dve.wait_ge(S["part_multiplied"], st.at("part_multiplied", 4 + h + 1))
                    scaled(st, k, 0, KA[0:MLA_NOPE, h, :], ps[st.bank(k)][0:MLA_NOPE, :], RBK[0:MLA_NOPE, :])

            def rope(st):
                at = slice(MLA_NOPE, MLA_QK)
                for n in range(MLA_H + 1):
                    dve.wait_ge(S["rope_rotated"], st.at("rope_rotated", n + 1))
                    dve.tensor_tensor(TM[at, n % 2, :], ps[st.bank(n)][at, :], SIN[at, :], ALU.mult).then_inc(bank_free[st.bank(n)], 1)
                    dve.wait_ge(bank_free[st.bank(n)], st.use(n) + 1)
                    dve.wait_ge(S["cos_applied"], st.at("cos_applied", n + 1))
                    x = KRAW[at, :] if n == 0 else QA[at, n - 1, :]
                    dve.tensor_tensor(x, x, TM[at, n % 2, :], ALU.add).then_inc(S["rope_added"], 1)

            def attention(st):
                mode = st.mode
                items = attention_items(st)
                for i in range(len(items) + DEPTH + 1):
                    if i < len(items):
                        h, c, t = items[i]
                        a, b = spans(mode, t)
                        w, s = (b - a) * P, i % 4
                        m, nm = MX[:, s:s + 1], NM[:, s:s + 1]
                        dve.wait_ge(S["scores_ready"], st.at("scores_ready", i + 1))
                        if mode == "mla":
                            dve.tensor_reduce(m, score_ps[i % 2][:, 0:w], AXX, ALU.max).then_inc(S["max_ready"], 1)
                            dve.wait_ge(S["max_ready"], st.at("max_ready", i + 1))
                            dve.tensor_scalar(nm, m, -MLA_QK ** -0.5, None, ALU.mult).then_inc(S["neg_max_ready"], 1)
                        else:
                            if mode == "gqa":
                                bias, made = BT[:, h % 2, t, 0:w], h * ST + t + 1
                            else:
                                at = (ST - 1 - t) * P
                                bias, made = BT2[:, h % 2, at:at + w], h + 1
                            dve.wait_ge(S["bias_ready"], st.at("bias_ready", made))
                            if i >= 4:
                                dve.wait_ge(S["probs_turned"], st.at("probs_turned", i - 3))
                            dve.tensor_tensor_reduce(SG[:, s, 0:w], score_ps[i % 2][:, 0:w], bias, 1.0, -3.0e38, ALU.add, ALU.max,
                                                     m).then_inc(S["scores_read"], 1)
                            dve.wait_ge(S["scores_read"], st.at("scores_read", i + 1))
                            if mode == "gqa":
                                dve.tensor_scalar(nm, m, col(f"gqa_sink{st.l}", h), -1.0, ALU.max, ALU.mult).then_inc(S["neg_max_ready"], 1)
                            else:
                                dve.tensor_scalar(nm, m, -1.0, None, ALU.mult).then_inc(S["neg_max_ready"], 1)
                    if 1 <= i <= len(items):
                        n = i - 1
                        h, c, t = items[n]
                        a, b = spans(mode, t)
                        w, s = (b - a) * P, n % 4
                        sm, rs = SM[:, s:s + 1], RS[:, s:s + 1]
                        dve.wait_ge(S["exp_ready"], st.at("exp_ready", n + 1))
                        if mode == "gqa":
                            dve.wait_ge(S["sink_exp_ready"], st.at("sink_exp_ready", n + 1))
                            dve.tensor_tensor(sm, sm, ES[:, s:s + 1], ALU.add).then_inc(S["sink_added"], 1)
                            dve.wait_ge(S["sink_added"], st.at("sink_added", n + 1))
                        dve.reciprocal(rs, sm).then_inc(S["inverse_ready"], 1)
                        if mode == "diff":
                            dve.wait_ge(S["inverse_ready"], st.at("inverse_ready", n + 1))
                            dve.tensor_tensor(rs, rs, LS[:, c:c + 1], ALU.mult).then_inc(S["lambda_applied"], 1)
                    for h in range(st.heads):
                        if i == min(((h + 1) * st.comps) * ST + DEPTH + 2, len(items) + DEPTH):
                            dve.wait_ge(S["item_multiplied"], st.at("item_multiplied", (h + 1) * st.comps * ST))
                            if mode == "diff":
                                dve.tensor_copy(UB[:, h, :], ps[st.bank(h)][:, :]).then_inc(bank_free[st.bank(h)], 1)
                                continue
                            if h % 2 == 0:
                                dve.wait_ge(S["operand_ready"], st.at("operand_ready", h // 2 - 1))
                            dve.tensor_copy(TM[half(h), (h // 2) % 2, :], ps[st.bank(h)][0:HD, :]).then_inc(bank_free[st.bank(h)], 1)
                    if mode != "diff":
                        hi, lo = pair[st.out]
                        for p in range(st.heads // 2):
                            if i == min((2 * p + 2) * ST + DEPTH + 4, len(items) + DEPTH):
                                remainder(st, (hi[:, p, :], lo[:, p, :]), TM[:, p % 2, :], p + 1, 0)

            def out_y(st):
                n = st.units // 4
                def body(r):
                    for k in range(4):
                        dve.wait_ge(bank_free[st.bank(k)], st.use(k, r) + 1)
                        add_square(st, k, r, k % 2)
                repeat(dve, st, body)

            def residual(st):
                n = st.units // 4
                def body(r):
                    for k in range(4):
                        t = r * 4 + k
                        dve.wait_ge(unit_used, st.unit(n * k + n - 1, r) + 1)
                        dve.tensor_tensor(tile_of(t, X), tile_of(t, X), ps[st.bank(k)][:, :], ALU.add).then_inc(bank_free[st.bank(k)], 1)
                        if st.gain:
                            remainder(st, (tile_of(t, HH), tile_of(t, HL)), tile_of(t, X), k + 1, r, col(st.gain, t))
                            dve.wait_ge(S["square_ready"], st.at("square_ready", k + 1, r))
                            add_square(st, k, r, k % 2)
                repeat(dve, st, body)

            def swiglu(st):
                dve.wait_ge(S["factor_rows_ready"], st.at("factor_rows_ready", 0))
                def body(r):
                    for j in range(4):
                        k = j // 2
                        dve.wait_ge(unit_used, st.unit(j, r) + 1)
                        if j % 2 == 0:
                            scaled(st, j, r, SG[:, k, :])
                            continue
                        scaled(st, j, r, TM[:, k, :])
                        dve.wait_ge(bank_free[st.bank(j)], st.use(j, r) + 1)
                        dve.wait_ge(S["gate_ready"], st.at("gate_ready", 1 + k, r))
                        dve.tensor_tensor(TM[:, k, :], TM[:, k, :], SG[:, k, :], ALU.mult).then_inc(S["product_ready"], 1)
                        remainder(st, (tile_of(r * 2 + k, F1H), tile_of(r * 2 + k, F1L)), TM[:, k, :], 1 + k, r)
                repeat(dve, st, body)

            def ple_in(st):
                for t in range(2):
                    remainder(st, (POH[:, t, :], POL[:, t, :]), TM[:, t, :], t + 1, 0)

            def ple(st):
                def body(r):
                    for k in range(2):
                        dve.wait_ge(bank_free[st.bank(2 * k)], st.use(2 * k, r) + 1)
                        dve.wait_ge(bank_free[st.bank(2 * k + 1)], st.use(2 * k + 1, r) + 1)
                        dve.tensor_tensor(tile_of(r * 2 + k, YP), SG[:, 2 * k, :], SG[:, 2 * k + 1, :], ALU.mult).then_inc(S["product_ready"], 1)
                        dve.wait_ge(S["square_ready"], st.at("square_ready", k + 1, r))
                        add_square(st, k, r, k)
                repeat(dve, st, body)

            def tables2(st):
                dve.wait_ge(S["tables_loaded"], st.at("tables_loaded", 32))
                for n in range(2):
                    dve.tensor_tensor_reduce(LAMV[:, 2 * n, :], LAMV[:, 2 * n, :], LAMV[:, 2 * n + 1, :], 1.0, 0.0, ALU.mult,
                                             ALU.add, LT[:, n:n + 1]).then_inc(S["tables_stepped"], 1)
                dve.wait_ge(S["lambda_exp_ready"], st.at("lambda_exp_ready", 1))
                dve.tensor_tensor(LS[:, 1:2], LE[:, 1:2], LE[:, 0:1], ALU.subtract).then_inc(S["tables_stepped"], 1)
                dve.wait_ge(S["tables_stepped"], st.at("tables_stepped", 3))
                dve.tensor_scalar(LS[:, 1:2], LS[:, 1:2], LAM_INIT, None, ALU.subtract).then_inc(S["tables_stepped"], 1)
                dve.memset(LS[:, 0:1], 1.0).then_inc(S["tables_stepped"], 1)
                dve.tensor_scalar(SUBG[:, :], col("b_sub_norm_20"), 1.0 - LAM_INIT, None, ALU.mult).then_inc(S["tables_stepped"], 1)
                dve.tensor_scalar(GQ[:, 0:1], col("a_q_norm_20"), HD ** -0.5, None, ALU.mult)
                dve.tensor_scalar(GQ[:, 1:2], col("b_q_norm_20"), HD ** -0.5, None, ALU.mult).then_inc(S["tables_stepped"], 1)

            def qkv(st):
                if not st.n:
                    return
                for n in range(16):
                    dve.wait_ge(S["qk_square_ready"], st.at("qk_square_ready", n + 1))
                    dve.tensor_reduce(VQ[:, n * 8:(n + 1) * 8], SQ[:, n % 2, :].rearrange("p (a c) -> p a c", c=HD), AXX, ALU.add)\
                       .then_inc(S["qk_square_summed"], 1)

            def qk_norm(st):
                dve.wait_ge(S["qk_square_summed"], st.at("qk_square_summed", 0))
                dve.tensor_scalar(VQ[:, :], VQ[:, :], 1.0 / HD, EPS, ALU.mult, ALU.add).then_inc(S["qk_factors_stepped"], 1)
                dve.wait_ge(S["qk_factors_stepped"], st.at("qk_factors_stepped", 2))
                dve.reciprocal(VQ[:, :], VQ[:, :]).then_inc(S["qk_factors_stepped"], 1)
                dve.wait_ge(S["qk_factors_stepped"], st.at("qk_factors_stepped", 3))
                for n in range(16):
                    c, s = n // 4, n % 4
                    c0 = c * SEQ
                    v = QKV[:, s, c0:c0 + SEQ].rearrange("p (a c) -> p a c", c=HD)
                    f = VQ[:, n * 8:(n + 1) * 8].rearrange("p (a o) -> p a o", o=1).to_broadcast([P, 8, HD])
                    dve.tensor_tensor(v, v, f, ALU.mult).then_inc(S["qk_normed"], 1)

            def sub_norm(st):
                dve.wait_ge(S["out_squares_summed"], st.at("out_squares_summed", 1))
                dve.tensor_scalar(VAR[:, :], stat_ps[:, 0:DIFF_H * ST], 1.0 / P, EPS, ALU.mult, ALU.add).then_inc(S["out_mean_ready"], 1)
                for h in range(DIFF_H):
                    dve.wait_ge(S["out_factors_spread"], st.at("out_factors_spread", h + 1))
                    dve.scalar_tensor_tensor(UB[:, h, :], UB[:, h, :], SUBG[:, 0:1], ps[st.bank(h)][:, :], ALU.mult, ALU.mult)\
                       .then_inc(bank_free[st.bank(h)], 1)
                    remainder(st, (O2H[:, 4 + h, :], O2L[:, 4 + h, :]), UB[:, h, :], h + 1, 0)

            def zero_u(st):
                dve.memset(U[:, :, 0:4], 0.0).then_inc(S["zeros_set"], 1)

            def conv(st, k, r, dst, w, taps):
                dve.wait_ge(S["conv_begun"], st.at("conv_begun", k + 1, r))
                n = taps - 1
                src = SG[:, k, :]
                for m in range(n):
                    d = dst if m == n - 1 else SG[:, k, :]
                    dve.scalar_tensor_tensor(d, U[:, k, n - 1 - m:n - 1 - m + SEQ], w(n - 1 - m), src, ALU.mult, ALU.add)\
                       .then_inc(S["conv_tap_added"], 1)
                    if m < n - 1:
                        dve.wait_ge(S["conv_tap_added"], st.at("conv_tap_added", n * k + m + 1, r))

            def conv_ffn(st):
                dve.wait_ge(S["factor_rows_ready"], st.at("factor_rows_ready", 0))
                dve.wait_ge(S["zeros_set"], st.at("zeros_set", 0))
                def body(r):
                    for j in range(4):
                        t = r * 2 + j // 2
                        c = t + (FT2 if j % 2 else 0)
                        dve.wait_ge(unit_used, st.unit(j, r) + 1)
                        scaled(st, j, r, U[:, j, 2:2 + SEQ])
                        conv(st, j, r, SG[:, j, :], lambda m: col(f"ffn_conv_w_2{st.l}_{m}", c), 3)
                        if j % 2:
                            dve.wait_ge(S["conv_tap_added"], st.at("conv_tap_added", 2 * j + 2, r))
                            dve.wait_ge(S["gate_ready"], st.at("gate_ready", 1 + j // 2, r))
                            dve.tensor_tensor(SG[:, j, :], SG[:, j, :], SG[:, j - 1, :], ALU.mult).then_inc(S["product_ready"], 1)
                            remainder(st, (tile_of(t, F2H), tile_of(t, F2L)), SG[:, j, :], 1 + j // 2, r)
                repeat(dve, st, body)

            def rec_conv(st):
                dve.wait_ge(S["factor_rows_ready"], st.at("factor_rows_ready", 0))
                dve.wait_ge(S["zeros_set"], st.at("zeros_set", 0))
                def body(r):
                    for j in range(4):
                        t = r * 4 + j
                        dve.wait_ge(unit_used, st.unit(j, r) + 1)
                        scaled(st, j, r, U[:, j, 3:3 + SEQ])
                        conv(st, j, r, tile_of(t, XR), lambda m: col(f"rec_conv_w_20_{m}", t), 4)
                        dve.wait_ge(S["conv_tap_added"], st.at("conv_tap_added", 3 * j + 3, r))
                        remainder(st, (tile_of(t, XRH), tile_of(t, XRL)), tile_of(t, XR), 1 + j, r)
                repeat(dve, st, body)

            def rec_lru(st):
                a = COLS[:, COL["rec_a_param_20"]:COL["rec_a_param_20"] + DT]
                n = 0

                def step(ins):
                    nonlocal n
                    ins.then_inc(S["decay_stepped"], 1)
                    n += 1
                    dve.wait_ge(S["decay_stepped"], st.at("decay_stepped", n))
                step(dve.tensor_scalar(LR[:, 1, :], a, -1.0, None, ALU.mult))
                step(dve.tensor_scalar(LR[:, 3, :], LR[:, 1, :], 0.0, None, ALU.max))
                dve.tensor_tensor(LR[:, 0, :], LR[:, 1, :], a, ALU.max).then_inc(S["decay_abs_ready"], 1)
                dve.wait_ge(S["decay_exp_ready"], st.at("decay_exp_ready", 1))
                step(dve.tensor_scalar(LR[:, 0, :], LR[:, 1, :], 2.0, None, ALU.add))
                step(dve.reciprocal(LR[:, 0, :], LR[:, 0, :]))
                step(dve.tensor_tensor(LR[:, 0, :], LR[:, 0, :], LR[:, 1, :], ALU.mult))
                step(dve.tensor_tensor(LR[:, 1, :], LR[:, 0, :], LR[:, 0, :], ALU.mult))
                terms = LOG_TERMS
                step(dve.tensor_scalar(LR[:, 2, :], LR[:, 1, :], 1.0 / (2 * terms + 1), None, ALU.mult))
                for m in range(terms - 1, 0, -1):
                    step(dve.scalar_tensor_tensor(LR[:, 2, :], LR[:, 2, :], 1.0 / (2 * m + 1), LR[:, 1, :], ALU.add, ALU.mult))
                step(dve.tensor_scalar(LR[:, 2, :], LR[:, 2, :], 1.0, 2.0, ALU.add, ALU.mult))
                step(dve.tensor_tensor(LR[:, 2, :], LR[:, 2, :], LR[:, 0, :], ALU.mult))
                step(dve.tensor_tensor(LR[:, 3, :], LR[:, 3, :], LR[:, 2, :], ALU.add))
                step(dve.tensor_scalar(LR[:, 3, :], LR[:, 3, :], -LRU_C, None, ALU.mult))
                for k in range(8, 16):
                    dve.wait_ge(bank_free[st.bank(k)], st.use(k) + 1)
                for k in range(DT):
                    dve.wait_ge(S["tanh_ready"], st.at("tanh_ready", k + 1))
                    dve.wait_ge(S["decay_squared"], st.at("decay_squared", k + 1))
                    dve.scalar_tensor_tensor(RT[:, k, :], SQ[:, k % 2, :], 1.0, RT[:, k, :], ALU.add, ALU.mult).then_inc(S["decay_rest_ready"], 1)
                    dve.tensor_tensor(IT[:, k, :], IT[:, k, :], XR[:, k, :], ALU.mult).then_inc(S["gated_input_ready"], 1)
                for k in range(DT):
                    dve.wait_ge(unit_used, st.unit(2 + k) + 1)
                    scaled(st, 16 + k, 0, GG[:, k, :])
                    dve.wait_ge(S["root_ready"], st.at("root_ready", k + 1))
                    dve.wait_ge(S["gated_input_ready"], st.at("gated_input_ready", k + 1))
                    dve.tensor_tensor(IT[:, k, :], IT[:, k, :], RT[:, k, :], ALU.mult).then_inc(S["scan_input_ready"], 1)
                    dve.wait_ge(S["scan_input_ready"], st.at("scan_input_ready", k + 1))
                    dve.tensor_tensor_scan(RT[:, k, :], DECAY[:, k, :], IT[:, k, :], 0.0, ALU.mult, ALU.add).then_inc(S["scan_done"], 1)
                    dve.wait_ge(S["scan_done"], st.at("scan_done", k + 1))
                    dve.wait_ge(S["gate_ready"], st.at("gate_ready", k + 1))
                    dve.tensor_tensor(GG[:, k, :], GG[:, k, :], RT[:, k, :], ALU.mult).then_inc(S["product_ready"], 1)
                    if k:
                        remainder(st, (ROH[:, k - 1, :], ROL[:, k - 1, :]), GG[:, k - 1, :], k, 0)
                remainder(st, (ROH[:, DT - 1, :], ROL[:, DT - 1, :]), GG[:, DT - 1, :], DT, 0)

            does = dict(init=init, tables1=tables1, operand=operand, norm=norm, zero=zero, fourier=fourier, branch=branch, proj=proj,
                        mla_heads=mla_heads, rope=rope, attention=attention, out_y=out_y, residual=residual, swiglu=swiglu,
                        ple_in=ple_in, ple=ple, tables2=tables2, qkv=qkv, qk_norm=qk_norm, sub_norm=sub_norm, zero_u=zero_u,
                        conv_ffn=conv_ffn, rec_conv=rec_conv, rec_lru=rec_lru)
            for st in STEPS:
                if st.kind in does:
                    does[st.kind](st)

        @block.gpsimd
        def _(pool):
            def remainder_of(st, j, r=0):
                n = st.unit(j) + AHEAD
                if isinstance(r, int) and n + r * st.units >= NU:
                    return
                s = n % SLOTS
                pool.wait_ge(wt_hi, n + 1 + r * st.units)
                pool.tensor_tensor(WLO[:, s, :], WRAW[:, s, :], WHI[:, s, :].bitcast(F32), ALU.subtract).then_inc(wt_lo, 1)

            def init(st):
                pool.wait_ge(cst, 3)

            def fourier(st):
                if st.u0 == 0:
                    for u in range(AHEAD):
                        pool.wait_ge(wt_hi, u + 1)
                        pool.tensor_tensor(WLO[:, u, :], WRAW[:, u, :], WHI[:, u, :].bitcast(F32), ALU.subtract).then_inc(wt_lo, 1)

            def units(st):
                def body(r):
                    for j in range(st.units):
                        remainder_of(st, j, r)
                last = st.u0 + st.reps * st.units + AHEAD >= NU
                repeat(pool, st, body, st.reps if last else 0)

            def operand(st):
                src, (hi, lo) = source[st.src], pair[st.dst]
                if st.stat:
                    pool.memset(ACC[:, :], 0.0).then_inc(S["sum_cleared"], 1)
                    pool.wait_ge(S["sum_cleared"], st.at("sum_cleared", 1))
                for i in range(st.n):
                    if on_pool(st, i):
                        t = st.t + i
                        pool.wait_ge(S["operand_hi_ready"], st.at("operand_hi_ready", i + 1))
                        if i and not on_pool(st, i - 1):
                            pool.wait_ge(S["operand_ready"], st.at("operand_ready", i))
                        h = hi[:, t, :].bitcast(F32)
                        pool.tensor_tensor(lo[:, t, :], src[:, t, :], h, ALU.subtract).then_inc(S["operand_ready"], 1)
                    if st.stat:
                        pool.wait_ge(S["square_ready"], st.at("square_ready", i + 1))
                        if i:
                            pool.wait_ge(S["square_added"], st.at("square_added", i))
                        pool.tensor_tensor(ACC[:, :], ACC[:, :], SQ[:, i % 2, :], ALU.add).then_inc(S["square_added"], 1)

            def norm(st):
                pool.wait_ge(S["mean_square_ready"], st.at("mean_square_ready", 1))
                pool.tensor_tensor(RC[st.rb][:, 0:ST], VAR[:, 0:ST], NEGH[:, 0:ST], ALU.pow).then_inc(S["factors_ready"], 1)

            def rope(st):
                at = slice(MLA_NOPE, MLA_QK)
                pool.wait_ge(wt_lo, st.u0 + AHEAD)
                for n in range(MLA_H + 1):
                    pool.wait_ge(S["rope_rotated"], st.at("rope_rotated", n + 1))
                    x = KRAW[at, :] if n == 0 else QA[at, n - 1, :]
                    pool.tensor_tensor(x, x, COS[at, :], ALU.mult).then_inc(S["cos_applied"], 1)
                pool.wait_ge(S["cos_applied"], st.at("cos_applied", MLA_H + 1))

            def attention(st):
                def bias_of(h):
                    if h >= 2 and st.mode != "mla":
                        pool.wait_ge(S["scores_read"], st.at("scores_read", (h - 1) * st.comps * ST))
                    if st.mode == "gqa":
                        slope = -float(np.float32(2.0 ** (-8.0 * (h + 1) / GQA_H)))
                        for t in range(ST):
                            w = (spans("gqa", t)[1] - spans("gqa", t)[0]) * P
                            pool.tensor_scalar(BT[:, h % 2, t, 0:w], GD[:, t, 0:w], slope, 1.0, ALU.mult, ALU.mult)\
                                .then_inc(S["bias_ready"], 1)
                    elif st.mode != "mla":
                        n = h if st.mode == "dilated" else DIL_H + h
                        slope = -float(np.float32(2.0 ** (-8.0 * (n + 1) / (DIL_H + DIFF_H))))
                        row = 0 if st.mode == "dilated" else 2
                        pool.tensor_scalar(BT2[:, h % 2, :], DIL[:, row, :], slope, 1.0, ALU.mult, ALU.mult)\
                            .then_inc(S["bias_ready" if st.mode == "diff" else "bias_scaled"], 1)
                        if st.mode == "dilated":
                            pool.wait_ge(S["bias_scaled"], st.at("bias_scaled", h + 1))
                            pool.tensor_tensor(BT2[:, h % 2, :], BT2[:, h % 2, :], DIL[:, 1, :], ALU.add).then_inc(S["bias_ready"], 1)

                per_head = st.comps * ST
                bias_of(0)
                for n, (h, c, t) in enumerate(attention_items(st)):
                    if n % per_head == 0 and h + 1 < st.heads:
                        bias_of(h + 1)
                    a, b = spans(st.mode, t)
                    done = "lambda_applied" if st.mode == "diff" else "inverse_ready"
                    pool.wait_ge(S[done], st.at(done, n + 1))
                    p = SG[:, n % 4, 0:(b - a) * P]
                    pool.tensor_scalar(p, p, RS[:, n % 4:n % 4 + 1], 1.0, ALU.mult, ALU.mult).then_inc(S["probs_ready"], 1)

            def sub_norm(st):
                pool.wait_ge(S["out_mean_ready"], st.at("out_mean_ready", 1))
                pool.tensor_tensor(RC["Y"][:, :], VAR[:, :], NEGH[:, :], ALU.pow).then_inc(S["out_factors_ready"], 1)

            does = dict(init=init, fourier=fourier, operand=operand, norm=norm, rope=rope, attention=attention, sub_norm=sub_norm)
            for st in STEPS:
                if st.kind in does:
                    does[st.kind](st)
                elif st.units:
                    units(st)


def packed_weights(inputs):
    w = np.zeros((NU, P, BLOCKS * P), np.float32)
    for n, (name, layer, r0, rows, c0, cols) in enumerate(UNITS):
        a = inputs[name][layer]
        if rows == 0:
            w[n] = a.transpose(1, 0, 2).reshape(P, BLOCKS * P)
        else:
            a = a[r0:r0 + rows, c0:c0 + cols]
            w[n, :, :rows // P * cols] = a.reshape(rows // P, P, cols).transpose(1, 0, 2).reshape(P, -1)
    return w


def packed_columns(inputs):
    cols = np.zeros((P, N_COLS), np.float32)
    for name, c in COL.items():
        tap = None
        if name.count("conv_w"):
            name, tap = name.rsplit("_", 1)
        a = inputs[name[:-1]][int(name[-1])]
        if tap is not None:
            a = a[int(tap)]
        if name.startswith("gqa_sink"):
            cols[:, c:c + GQA_H] = a[None, :]
        elif a.size < P:
            cols[:, c] = np.concatenate([a, a])
        else:
            cols[:, c:c + a.size // P] = a.reshape(-1, P).T
    return cols


def tables():
    f = np.float32
    ident = np.eye(P, dtype=f)
    rot = np.zeros((P, MLA_QK), f)
    hf = MLA_ROPE // 2
    for j in range(hf):
        rot[MLA_NOPE + hf + j, MLA_NOPE + j] = -1.0
        rot[MLA_NOPE + j, MLA_NOPE + hf + j] = 1.0
    inv = np.zeros((P, 1), f)
    inv[MLA_NOPE:MLA_QK, 0] = np.tile(f(10000.0) ** (-np.arange(hf, dtype=f) / f(hf)), 2)
    consts = np.concatenate([ident, rot, inv], 1)
    q, j = np.arange(P)[:, None], np.arange(3 * P)[None, :]
    gmask = np.where(np.abs(j - P - q) <= WINDOW, 0.0, MASKED).astype(f)
    n = np.arange(SEQ)
    ang = 2 * np.pi * ((n[:, None] * n[None, :]) % SEQ) / SEQ
    scale = 1.0 / np.sqrt(SEQ * FGROUP)
    dft = (np.stack([np.cos(ang), np.sin(ang)]) * scale).astype(f)
    m = np.arange(FGROUP)
    ang = 2 * np.pi * ((m[:, None] * m[None, :]) % FGROUP) / FGROUP
    dftc = np.concatenate([np.cos(ang), -np.sin(ang)], 1).astype(f).reshape(2, P, 2 * FGROUP)
    delta = np.arange(P)[:, None] + (ST - 1) * P - np.arange(SEQ)[None, :]
    seen = (delta >= 0) * ((delta <= P) * 1 + (delta % 4 == 0) * 1 + (delta % 16 == 0) * 1)
    dil = np.stack([np.where(seen > 0, delta, MASKED), np.log(np.maximum(seen, 1)), np.where(delta >= 0, delta, MASKED)], 1).astype(f)
    return consts, gmask, dft, dftc, dil


def kernel(**inputs):
    from concourse import bacc
    from concourse.bass_utils import run_bass_kernel_spmd

    inputs = {k: np.asarray(v) for k, v in inputs.items()}
    consts, gmask, dft, dftc, dil = tables()
    pos = inputs["positions"]
    lamv = np.concatenate([inputs[f"b_lam_{v}_2"] for v in ("q1", "k1", "q2", "k2")], 1)
    arrays = dict(wall=packed_weights(inputs), xin=inputs["x"], pin=inputs["p"], posi=pos,
                  posc=np.ascontiguousarray(pos.reshape(ST, P).T), cols=packed_columns(inputs), consts=consts, gmask=gmask,
                  dft=dft, dftc=dftc, dil=dil, lamv=lamv)
    nc = bacc.Bacc("TRN2", target_bir_lowering=False, num_devices=1, dynamic_dma_scratch_size=RING)
    aps = {k: nc.dram_tensor(k, v.shape, mybir.dt.from_np(v.dtype), kind="ExternalInput").ap() for k, v in arrays.items()}
    y = nc.dram_tensor("y", (1, SEQ, DM), F32, kind="ExternalOutput").ap()
    build(nc, out_=y, **aps)
    got = run_bass_kernel_spmd(nc, [arrays], core_ids=[0])
    return got.results[0]["y"]
```
